# Optimizing a Trainium2 kernel written in Bass

```python
import jax, jax.numpy as jnp
from jax import lax
import numpy as np

D_MODEL = 1024
BATCH = 1
SEQ = 512
DEPTH = 2

CONV_DIM = 512
CONV_WIDTH = 3
RET_HEADS = 4
RET_HEAD_DIM = 128
RET_DIM = RET_HEADS * RET_HEAD_DIM
GLA_HEADS = 4
GLA_KEY_HEAD_DIM = 64
GLA_VAL_HEAD_DIM = 128
GLA_KEY_DIM = GLA_HEADS * GLA_KEY_HEAD_DIM
GLA_VAL_DIM = GLA_HEADS * GLA_VAL_HEAD_DIM
GLA_GATE_RANK = 16
GLA_GATE_TAU = 16.0
N_BRANCHES = 3
CHUNK = 64
D_FF = (((8 * D_MODEL + 2) // 3 + 255) // 256) * 256
ROPE_BASE = 10000.0
EPS = 1e-6
IN_COLS = 3 * CONV_DIM + 4 * RET_DIM + 2 * GLA_KEY_DIM + 2 * GLA_VAL_DIM + GLA_GATE_RANK + N_BRANCHES * D_MODEL


def rms_norm(x, w):
    xf = x.astype(jnp.float32)
    y = xf * lax.rsqrt(jnp.mean(xf * xf, axis=-1, keepdims=True) + EPS)
    return (y * w.astype(jnp.float32)).astype(x.dtype)

def head_norm(y, w, center):
    b, t, h, d = y.shape
    if center:
        y = y - jnp.mean(y, axis=-1, keepdims=True)
    y = y * lax.rsqrt(jnp.mean(y * y, axis=-1, keepdims=True) + EPS)
    return y.reshape(b, t, h * d) * w.astype(jnp.float32)

def rotary(x, positions):
    half = x.shape[-1] // 2
    inv_freq = ROPE_BASE ** (-jnp.arange(half, dtype=jnp.float32) / half)
    ang = positions.astype(jnp.float32)[..., None] * inv_freq
    cos = jnp.cos(ang)[:, :, None, :]
    sin = jnp.sin(ang)[:, :, None, :]
    x1, x2 = x[..., :half], x[..., half:]
    return jnp.concatenate([x1 * cos - x2 * sin, x2 * cos + x1 * sin], axis=-1)

def to_chunks(x):
    b, t, h, d = x.shape
    return x.reshape(b, t // CHUNK, CHUNK, h, d).transpose(1, 0, 3, 2, 4)

def from_chunks(x):
    nc, b, h, c, d = x.shape
    return x.transpose(1, 0, 3, 2, 4).reshape(b, nc * c, h, d)

def short_conv(u, b_gate, c_gate, conv_w):
    z = c_gate * u
    t = z.shape[1]
    zp = jnp.pad(z, ((0, 0), (CONV_WIDTH - 1, 0), (0, 0)))
    y = sum(conv_w[i] * zp[:, i:i + t, :] for i in range(CONV_WIDTH))
    return b_gate * y

def retention(q, k, v):
    b, t, h, dk = q.shape
    dv = v.shape[-1]
    log_g = jnp.log(1.0 - 2.0 ** (-5.0 - jnp.arange(h, dtype=jnp.float32)))
    idx = jnp.arange(CHUNK, dtype=jnp.float32)
    diff = idx[:, None] - idx[None, :]
    causal = diff >= 0
    decay_mask = jnp.where(causal, jnp.exp(log_g[:, None, None] * jnp.maximum(diff, 0.0)), 0.0)
    q_decay = jnp.exp(log_g[:, None] * (idx + 1.0))[None, :, :, None]
    k_decay = jnp.exp(log_g[:, None] * (CHUNK - 1.0 - idx))[None, :, :, None]
    chunk_decay = jnp.exp(log_g * CHUNK)[None, :, None, None]
    q = q * (dk ** -0.5)

    def step(state, inp):
        qi, ki, vi = inp
        s = jnp.einsum('bhid,bhjd->bhij', qi, ki) * decay_mask
        intra = jnp.einsum('bhij,bhjv->bhiv', s, vi)
        inter = jnp.einsum('bhid,bhdv->bhiv', qi * q_decay, state)
        new_state = state * chunk_decay + jnp.einsum('bhjd,bhjv->bhdv', ki * k_decay, vi)
        return new_state, intra + inter

    state0 = jnp.zeros((b, h, dk, dv), jnp.float32)
    _, out = lax.scan(step, state0, (to_chunks(q), to_chunks(k), to_chunks(v)))
    return from_chunks(out)

def gated_linear_attention(q, k, v, log_a):
    b, t, h, dk = q.shape
    dv = v.shape[-1]
    q = q * (dk ** -0.5)
    tril = jnp.tril(jnp.ones((CHUNK, CHUNK), dtype=bool))[None, None, :, :, None]

    def step(state, inp):
        qi, ki, vi, gi = inp
        cum = jnp.cumsum(gi, axis=2)
        rel = cum[:, :, :, None, :] - cum[:, :, None, :, :]
        pair_decay = jnp.where(tril, jnp.exp(jnp.where(tril, rel, 0.0)), 0.0)
        s = jnp.einsum('bhid,bhjd,bhijd->bhij', qi, ki, pair_decay)
        intra = jnp.einsum('bhij,bhjv->bhiv', s, vi)
        inter = jnp.einsum('bhid,bhdv->bhiv', qi * jnp.exp(cum), state)
        last = cum[:, :, -1:, :]
        new_state = state * jnp.exp(last)[:, :, 0, :, None] + jnp.einsum(
            'bhjd,bhjv->bhdv', ki * jnp.exp(last - cum), vi)
        return new_state, intra + inter

    state0 = jnp.zeros((b, h, dk, dv), jnp.float32)
    _, out = lax.scan(step, state0, (to_chunks(q), to_chunks(k), to_chunks(v), to_chunks(log_a)))
    return from_chunks(out)

def split_columns(proj):
    sizes = ([CONV_DIM] * 3 + [RET_DIM] * 4
             + [GLA_KEY_DIM, GLA_KEY_DIM, GLA_VAL_DIM, GLA_VAL_DIM, GLA_GATE_RANK]
             + [D_MODEL] * N_BRANCHES)
    offsets = [int(o) for o in np.cumsum(sizes)[:-1]]
    return jnp.split(proj, offsets, axis=-1)

def mixer_block(h, positions, w_in, conv_w, ret_gn_w, gla_w_a2, gla_b_a, gla_gn_w,
                w_branch_a, w_branch_b, w_branch_c, w_out):
    bsz, t, _ = h.shape
    proj = (h @ w_in).astype(jnp.float32)
    (cu, cb, cc, rq, rk, rv, rg, gq, gk, gv, gr, ga_down,
     gate_a, gate_b, gate_c) = split_columns(proj)

    y_a = short_conv(cu, cb, cc, conv_w.astype(jnp.float32))

    rq = rotary(rq.reshape(bsz, t, RET_HEADS, RET_HEAD_DIM), positions)
    rk = rotary(rk.reshape(bsz, t, RET_HEADS, RET_HEAD_DIM), positions)
    rv = rv.reshape(bsz, t, RET_HEADS, RET_HEAD_DIM)
    y_b = head_norm(retention(rq, rk, rv), ret_gn_w, center=True) * jax.nn.silu(rg)

    gate_logits = ga_down @ gla_w_a2.astype(jnp.float32) + gla_b_a.astype(jnp.float32)
    log_a = (jax.nn.log_sigmoid(gate_logits) / GLA_GATE_TAU).reshape(bsz, t, GLA_HEADS, GLA_KEY_HEAD_DIM)
    gq = gq.reshape(bsz, t, GLA_HEADS, GLA_KEY_HEAD_DIM)
    gk = gk.reshape(bsz, t, GLA_HEADS, GLA_KEY_HEAD_DIM)
    gv = gv.reshape(bsz, t, GLA_HEADS, GLA_VAL_HEAD_DIM)
    y_c = head_norm(gated_linear_attention(gq, gk, gv, log_a), gla_gn_w, center=False) * jax.nn.silu(gr)

    merged = (jax.nn.sigmoid(gate_a) * (y_a @ w_branch_a.astype(jnp.float32))
              + jax.nn.sigmoid(gate_b) * (y_b @ w_branch_b.astype(jnp.float32))
              + jax.nn.sigmoid(gate_c) * (y_c @ w_branch_c.astype(jnp.float32)))
    return (merged @ w_out.astype(jnp.float32)).astype(h.dtype)

def swiglu(h, w_gate, w_up, w_down):
    return (jax.nn.silu(h @ w_gate) * (h @ w_up)) @ w_down

def first_inputs(seed: int = 0) -> dict:
    key = jax.random.key(seed)
    ks = jax.random.split(key, 20)
    f32 = jnp.float32

    def normal(k, shape, scale):
        return jax.random.normal(k, shape, f32) * scale

    def gain(k, shape):
        return 1.0 + 0.1 * jax.random.normal(k, shape, f32)

    return {
        "x": normal(ks[0], (BATCH, SEQ, D_MODEL), 1.0),
        "positions": jnp.broadcast_to(jnp.arange(SEQ, dtype=jnp.int32), (BATCH, SEQ)),
        "norm_mix_pre": gain(ks[1], (DEPTH, D_MODEL)),
        "w_in": normal(ks[2], (DEPTH, D_MODEL, IN_COLS), D_MODEL ** -0.5),
        "conv_w": normal(ks[3], (DEPTH, CONV_WIDTH, CONV_DIM), CONV_WIDTH ** -0.5),
        "ret_gn_w": gain(ks[4], (DEPTH, RET_DIM)),
        "gla_w_a2": normal(ks[5], (DEPTH, GLA_GATE_RANK, GLA_KEY_DIM), GLA_GATE_RANK ** -0.5),
        "gla_b_a": normal(ks[6], (DEPTH, GLA_KEY_DIM), 0.1),
        "gla_gn_w": gain(ks[7], (DEPTH, GLA_VAL_DIM)),
        "w_branch_a": normal(ks[8], (DEPTH, CONV_DIM, D_MODEL), CONV_DIM ** -0.5),
        "w_branch_b": normal(ks[9], (DEPTH, RET_DIM, D_MODEL), RET_DIM ** -0.5),
        "w_branch_c": normal(ks[10], (DEPTH, GLA_VAL_DIM, D_MODEL), GLA_VAL_DIM ** -0.5),
        "w_out": normal(ks[11], (DEPTH, D_MODEL, D_MODEL), D_MODEL ** -0.5),
        "norm_mix_post": gain(ks[12], (DEPTH, D_MODEL)),
        "norm_ffn_pre": gain(ks[13], (DEPTH, D_MODEL)),
        "w_ffn_gate": normal(ks[14], (DEPTH, D_MODEL, D_FF), D_MODEL ** -0.5),
        "w_ffn_up": normal(ks[15], (DEPTH, D_MODEL, D_FF), D_MODEL ** -0.5),
        "w_ffn_down": normal(ks[16], (DEPTH, D_FF, D_MODEL), D_FF ** -0.5),
        "norm_ffn_post": gain(ks[17], (DEPTH, D_MODEL)),
    }

def first_block(x, positions, norm_mix_pre, w_in, conv_w, ret_gn_w, gla_w_a2, gla_b_a, gla_gn_w,
              w_branch_a, w_branch_b, w_branch_c, w_out, norm_mix_post, norm_ffn_pre,
              w_ffn_gate, w_ffn_up, w_ffn_down, norm_ffn_post):
    for layer in range(DEPTH):
        h = rms_norm(x, norm_mix_pre[layer])
        m = mixer_block(h, positions, w_in[layer], conv_w[layer], ret_gn_w[layer], gla_w_a2[layer],
                        gla_b_a[layer], gla_gn_w[layer], w_branch_a[layer], w_branch_b[layer],
                        w_branch_c[layer], w_out[layer])
        x = x + rms_norm(m, norm_mix_post[layer]).astype(x.dtype)
        h = rms_norm(x, norm_ffn_pre[layer])
        f = swiglu(h, w_ffn_gate[layer], w_ffn_up[layer], w_ffn_down[layer])
        x = x + rms_norm(f, norm_ffn_post[layer]).astype(x.dtype)
    return x


DEPTH_2 = 1

HEAD_DIM = 64
D_MIX = D_MODEL
N_HEADS_A = (D_MIX // 2) // HEAD_DIM
N_KV_A = 2
N_HEADS_B = (D_MIX // 2) // HEAD_DIM
DILATED_CONFIGS = ((128, 1), (512, 4), (2048, 16))
Q_BLOCK = 128
GRID_W = 64
ROPE_THETA = 10000.0
D_FF_2 = 2816
NEG_INF = -1e30

A_Q = N_HEADS_A * HEAD_DIM
A_KV = N_KV_A * HEAD_DIM
B_QKV = N_HEADS_B * HEAD_DIM
QKV_COLS = A_Q + 2 * A_KV + 3 * B_QKV
QKV_SPLITS = (A_Q, A_Q + A_KV, A_Q + 2 * A_KV, A_Q + 2 * A_KV + B_QKV, A_Q + 2 * A_KV + 2 * B_QKV)


def _rmsnorm(x, g):
    xf = x.astype(jnp.float32)
    r = lax.rsqrt(jnp.mean(xf * xf, axis=-1, keepdims=True) + EPS)
    return (xf * r * g.astype(jnp.float32)).astype(x.dtype)

def _rope_angles(pos, dim):
    freqs = ROPE_THETA ** (-jnp.arange(0, dim, 2, dtype=jnp.float32) / dim)
    return pos.astype(jnp.float32)[:, None] * freqs[None, :]

def _apply_rope(x, ang):
    xf = x.astype(jnp.float32)
    x1, x2 = jnp.split(xf, 2, axis=-1)
    cos = jnp.cos(ang)[None, :, None, :]
    sin = jnp.sin(ang)[None, :, None, :]
    return jnp.concatenate([x1 * cos - x2 * sin, x2 * cos + x1 * sin], axis=-1).astype(x.dtype)

def _apply_axial_rope(x, ang_row, ang_col):
    xr, xc = jnp.split(x, 2, axis=-1)
    return jnp.concatenate([_apply_rope(xr, ang_row), _apply_rope(xc, ang_col)], axis=-1)

def _swiglu(x, w_gate, w_up, w_down):
    return (jax.nn.silu(x @ w_gate) * (x @ w_up)) @ w_down

def _gqa_dense_blocked(q, k, v):
    B, S, Hq, D = q.shape
    Hkv = k.shape[2]
    G = Hq // Hkv
    nq = S // Q_BLOCK
    scale = D ** -0.5
    qb = q.reshape(B, nq, Q_BLOCK, Hkv, G, D).transpose(1, 0, 2, 3, 4, 5)

    def block(qi):
        s = jnp.einsum('bqkgd,bskd->bkgqs', qi, k, preferred_element_type=jnp.float32) * scale
        p = jax.nn.softmax(s, axis=-1)
        o = jnp.einsum('bkgqs,bskd->bqkgd', p.astype(v.dtype), v, preferred_element_type=jnp.float32)
        return o.astype(v.dtype)

    o = lax.map(block, qb)
    return o.transpose(1, 0, 2, 3, 4, 5).reshape(B, S, Hq, D)

def _dilated_window_partial(q, k, v, window, dilation):
    B, S, H, D = q.shape
    span = (window // 2) // dilation
    L = S // dilation
    blk = span
    nb = -(-L // blk)
    Lp = nb * blk
    scale = D ** -0.5

    def strided(x):
        return x.reshape(B, L, dilation, H, D).transpose(0, 2, 1, 3, 4)

    qs = jnp.pad(strided(q), ((0, 0), (0, 0), (0, Lp - L), (0, 0), (0, 0)))
    kv_pad = ((0, 0), (0, 0), (blk, Lp - L + blk), (0, 0), (0, 0))
    ks = jnp.pad(strided(k), kv_pad).reshape(B, dilation, nb + 2, blk, H, D)
    vs = jnp.pad(strided(v), kv_pad).reshape(B, dilation, nb + 2, blk, H, D)
    qb = qs.reshape(B, dilation, nb, blk, H, D)
    kw = jnp.concatenate([ks[:, :, :-2], ks[:, :, 1:-1], ks[:, :, 2:]], axis=3)
    vw = jnp.concatenate([vs[:, :, :-2], vs[:, :, 1:-1], vs[:, :, 2:]], axis=3)

    qpos = jnp.arange(nb)[:, None] * blk + jnp.arange(blk)[None, :]
    kpos = jnp.arange(nb)[:, None] * blk + jnp.arange(3 * blk)[None, :] - blk
    diff = kpos[:, None, :] - qpos[:, :, None]
    valid = (jnp.abs(diff) <= span) & (kpos[:, None, :] >= 0) & (kpos[:, None, :] < L)

    s = jnp.einsum('brcihe,brcjhe->brchij', qb, kw, preferred_element_type=jnp.float32) * scale
    s = jnp.where(valid[None, None, :, None], s, NEG_INF)
    m = jnp.max(s, axis=-1)
    p = jnp.exp(s - m[..., None])
    l = jnp.sum(p, axis=-1)
    o = jnp.einsum('brchij,brcjhe->brcihe', p.astype(vw.dtype), vw, preferred_element_type=jnp.float32)

    o = o.reshape(B, dilation, Lp, H, D)[:, :, :L].transpose(0, 2, 1, 3, 4).reshape(B, S, H, D)

    def unstride_stat(a):
        a = a.transpose(0, 1, 2, 4, 3).reshape(B, dilation, Lp, H)[:, :, :L]
        return a.transpose(0, 2, 1, 3).reshape(B, S, H)

    return o, unstride_stat(m), unstride_stat(l)

def _dilated_mixture(q, k, v):
    parts = [_dilated_window_partial(q, k, v, w, d) for (w, d) in DILATED_CONFIGS]
    m_all = jnp.max(jnp.stack([p[1] for p in parts], axis=0), axis=0)
    num = jnp.zeros(q.shape, jnp.float32)
    den = jnp.zeros(q.shape[:3], jnp.float32)
    for o_i, m_i, l_i in parts:
        w_i = jnp.exp(m_i - m_all)
        num = num + w_i[..., None] * o_i
        den = den + w_i * l_i
    return (num / den[..., None]).astype(q.dtype)

def second_inputs(seed: int = 0) -> dict:
    key = jax.random.key(seed)
    ks = jax.random.split(key, 18)
    f32 = jnp.float32

    def w(k, shape, fan_in):
        return jax.random.normal(k, shape, f32) * (fan_in ** -0.5)

    def gain(k, dim):
        return 1.0 + 0.02 * jax.random.normal(k, (DEPTH_2, dim), f32)

    return {
        "x": jax.random.normal(ks[0], (BATCH, SEQ, D_MODEL), f32),
        "ffn1_pre_g": gain(ks[1], D_MODEL),
        "ffn1_post_g": gain(ks[2], D_MODEL),
        "ffn1_w_gate": w(ks[3], (DEPTH_2, D_MODEL, D_FF_2), D_MODEL),
        "ffn1_w_up": w(ks[4], (DEPTH_2, D_MODEL, D_FF_2), D_MODEL),
        "ffn1_w_down": w(ks[5], (DEPTH_2, D_FF_2, D_MODEL), D_FF_2),
        "mix_pre_g": gain(ks[6], D_MODEL),
        "mix_post_g": gain(ks[7], D_MODEL),
        "w_qkv": w(ks[8], (DEPTH_2, D_MODEL, QKV_COLS), D_MODEL),
        "q_norm_g": gain(ks[9], HEAD_DIM),
        "k_norm_g": gain(ks[10], HEAD_DIM),
        "w_out": w(ks[11], (DEPTH_2, D_MIX, D_MODEL), D_MIX),
        "ffn2_pre_g": gain(ks[12], D_MODEL),
        "ffn2_post_g": gain(ks[13], D_MODEL),
        "ffn2_w_gate": w(ks[14], (DEPTH_2, D_MODEL, D_FF_2), D_MODEL),
        "ffn2_w_up": w(ks[15], (DEPTH_2, D_MODEL, D_FF_2), D_MODEL),
        "ffn2_w_down": w(ks[16], (DEPTH_2, D_FF_2, D_MODEL), D_FF_2),
    }

def second_block(x, ffn1_pre_g, ffn1_post_g, ffn1_w_gate, ffn1_w_up, ffn1_w_down,
              mix_pre_g, mix_post_g, w_qkv, q_norm_g, k_norm_g, w_out,
              ffn2_pre_g, ffn2_post_g, ffn2_w_gate, ffn2_w_up, ffn2_w_down):
    B, S, _ = x.shape
    ROWS = S // GRID_W
    pos = jnp.arange(S, dtype=jnp.int32)
    row = jnp.repeat(jnp.arange(ROWS, dtype=jnp.int32), GRID_W)
    col = jnp.tile(jnp.arange(GRID_W, dtype=jnp.int32), ROWS)
    ang_row = _rope_angles(row, HEAD_DIM // 2)
    ang_col = _rope_angles(col, HEAD_DIM // 2)
    ang_1d = _rope_angles(pos, HEAD_DIM)

    for l in range(DEPTH_2):
        f = _swiglu(_rmsnorm(x, ffn1_pre_g[l]), ffn1_w_gate[l], ffn1_w_up[l], ffn1_w_down[l])
        x = x + 0.5 * _rmsnorm(f, ffn1_post_g[l])

        h = _rmsnorm(x, mix_pre_g[l])
        qkv = h @ w_qkv[l]
        qa, ka, va, qb, kb, vb = jnp.split(qkv, QKV_SPLITS, axis=-1)

        qa = _rmsnorm(qa.reshape(B, S, N_HEADS_A, HEAD_DIM), q_norm_g[l])
        ka = _rmsnorm(ka.reshape(B, S, N_KV_A, HEAD_DIM), k_norm_g[l])
        va = va.reshape(B, S, N_KV_A, HEAD_DIM)
        qa = _apply_axial_rope(qa, ang_row, ang_col)
        ka = _apply_axial_rope(ka, ang_row, ang_col)
        out_a = _gqa_dense_blocked(qa, ka, va)

        qb = _apply_rope(qb.reshape(B, S, N_HEADS_B, HEAD_DIM), ang_1d)
        kb = _apply_rope(kb.reshape(B, S, N_HEADS_B, HEAD_DIM), ang_1d)
        vb = vb.reshape(B, S, N_HEADS_B, HEAD_DIM)
        out_b = _dilated_mixture(qb, kb, vb)

        heads = jnp.concatenate([out_a.reshape(B, S, A_Q), out_b.reshape(B, S, B_QKV)], axis=-1)
        x = x + _rmsnorm(heads @ w_out[l], mix_post_g[l])

        f = _swiglu(_rmsnorm(x, ffn2_pre_g[l]), ffn2_w_gate[l], ffn2_w_up[l], ffn2_w_down[l])
        x = x + 0.5 * _rmsnorm(f, ffn2_post_g[l])
    return x


def setup_inputs(seed=0):
    out = dict(first_inputs(seed))
    for name, value in second_inputs(seed + 1).items():
        if name != "x":
            out[name + "_2"] = value
    return out


def reference(
    x, positions, norm_mix_pre, w_in, conv_w, ret_gn_w, gla_w_a2, gla_b_a, gla_gn_w, w_branch_a,
    w_branch_b, w_branch_c, w_out, norm_mix_post, norm_ffn_pre, w_ffn_gate, w_ffn_up,
    w_ffn_down, norm_ffn_post, ffn1_pre_g_2, ffn1_post_g_2, ffn1_w_gate_2, ffn1_w_up_2,
    ffn1_w_down_2, mix_pre_g_2, mix_post_g_2, w_qkv_2, q_norm_g_2, k_norm_g_2, w_out_2,
    ffn2_pre_g_2, ffn2_post_g_2, ffn2_w_gate_2, ffn2_w_up_2, ffn2_w_down_2,
):
    x = first_block(
        x, positions, norm_mix_pre, w_in, conv_w, ret_gn_w, gla_w_a2, gla_b_a, gla_gn_w,
        w_branch_a, w_branch_b, w_branch_c, w_out, norm_mix_post, norm_ffn_pre, w_ffn_gate,
        w_ffn_up, w_ffn_down, norm_ffn_post,
    )
    return second_block(
        x, ffn1_pre_g_2, ffn1_post_g_2, ffn1_w_gate_2, ffn1_w_up_2, ffn1_w_down_2, mix_pre_g_2,
        mix_post_g_2, w_qkv_2, q_norm_g_2, k_norm_g_2, w_out_2, ffn2_pre_g_2, ffn2_post_g_2,
        ffn2_w_gate_2, ffn2_w_up_2, ffn2_w_down_2,
    )


_drawn_inputs = setup_inputs


def setup_inputs(seed=0):
    import zlib

    import numpy as np

    out = dict(_drawn_inputs(seed))
    spreads = {}
    factors = {'ffn1_pre_g_2': 7.795,
     'ffn1_post_g_2': 8.0,
     'mix_pre_g_2': 4.294,
     'mix_post_g_2': 21.3,
     'q_norm_g_2': 8.0,
     'k_norm_g_2': 8.0,
     'ffn2_pre_g_2': 36.863,
     'ffn2_post_g_2': 51.389}
    for name, (base, spread) in spreads.items():
        noise = np.random.default_rng([zlib.crc32(name.encode()), seed]).standard_normal(out[name].shape)
        drawn = base * np.exp(spread * noise) if base else spread * noise
        out[name] = __import__('jax').numpy.asarray(drawn.astype(out[name].dtype))
    for name, factor in factors.items():
        out[name] = (out[name] * factor).astype(out[name].dtype)
    return out
```

```python
import math
from contextlib import ExitStack

import numpy as np

import concourse.bass as bass
from concourse import mybir

F32 = mybir.dt.float32
F32R = mybir.dt.float32r
I32 = mybir.dt.int32
U32 = mybir.dt.uint32
ACT = mybir.ActivationFunctionType
ALU = mybir.AluOpType
AX = mybir.AxisListType
CONSTS = 16 * 7
EXP_LN = "natural_log_exp_and_others"

P = 128
T = 512
TT = T // P
D = 1024
KD = D // P
LAYERS = 2
EPS = 1e-6
CONV, RET, GKEY, GVAL, RANK = 512, 512, 256, 512, 16
HEADS = 4
DFF = 2816
FT = DFF // P
HD = 64
NEG = -1e30
LEVELS = (1, 128, 64, 32, 16, 8, 4, 2, 256, 512)
MASKED = LEVELS[:8]
UNITS = [(lev, t) for lev in LEVELS for t in range(2)]

BLK = 1024
RING = 4
RAW = 2
AHEAD = RING - 1
N_HEAD = 40
N_GATE = 12
GATE_TURNS = KD // 2
N_UP = 4
UP_TURNS = FT // 2
N_DOWN = 12
DOWN_TURNS = 2
DOWN_K = (8, 8, 6)
N_FFN = N_UP * UP_TURNS + N_DOWN * DOWN_TURNS
N_LAYER = N_HEAD + N_GATE * GATE_TURNS + KD + N_FFN
N_QKV = 18
COLS_GATE = 2 * 3 * (BLK + BLK // 2)
COLS_DOWN = 4 * FT * P
COLS_FFN = UP_TURNS * N_UP * BLK + DOWN_TURNS * COLS_DOWN
COLS_LAYER = N_HEAD * BLK + GATE_TURNS * COLS_GATE + KD * BLK + COLS_FFN
COLS = LAYERS * COLS_LAYER + 2 * COLS_FFN + (N_QKV + KD) * BLK
OUT_FFN = N_UP * UP_TURNS + 4 * DOWN_TURNS
OUT_LAYER = N_HEAD + N_GATE * GATE_TURNS + KD + OUT_FFN

G_MIX_PRE, G_MIX_POST, G_FFN_PRE, G_FFN_POST = 0, 8, 16, 24
P_CONV, P_RETGN, P_GLAGN, P_BA, P_WGA = 32, 44, 48, 52, 54
N_PAR = P_WGA + KD * RANK
H_F1PRE, H_F1POST, H_MPRE, H_MPOST, H_F2PRE, H_F2POST, H_QN, H_KN = 0, 8, 16, 24, 32, 40, 48, 49
N_PAR2 = 50
C_ONES, C_IDENT, C_BD64, C_ROT64, C_ROT32, C_ROT16 = range(6)
N_SQ = 6


class Blocks:

    def __init__(self, quads, s=0):
        self.quads, self.s = quads, s

    def n(self, p):
        return self.quads * 4 + (self.s + p)

    def slot(self, p):
        return (self.s + p) % RING

    def raw(self, p):
        return (self.s + p) % RAW

    def raw_uses(self, p):
        return self.quads * 2 + (self.s + p) // RAW

    def on(self, p):
        return Blocks(self.quads, self.s + p)


class Outs:

    def __init__(self, quads, s=0):
        self.quads, self.s = quads, s

    def bank(self, e):
        return (self.s + e) % 4

    def uses(self, e):
        return self.quads + (self.s + e) // 4

    def on(self, e):
        return Outs(self.quads, self.s + e)


class Event:

    def __init__(self, sem, per, credit=0):
        self.sem, self.per, self.credit = sem, per, credit

    def upto(self, inst, n):
        return inst * self.per + (self.credit + n)


class Use:

    def __init__(self, mem, drained, filled, n):
        self.mem, self.drained, self.filled, self.n = mem, drained, filled, n


def side_banks():
    layer = [("pre0", 7), ("tm0", 6), ("ga", 4), ("z0", 5), ("z1", 6)]
    layer += [(f"gla{u}{h}", 4 + 2 * (u % 2) + h) for u in range(len(UNITS)) for h in range(2)]
    layer += [(f"rot{i}", 4 + i % 2) for i in range(8)]
    layer += [("out0", 7), ("out1", 7), ("out2", 7), ("var0", 6), ("out3", 7), ("var1", 6), ("var2", 6), ("var3", 6)]
    for h in range(HEADS):
        layer += [(f"s{h}0", 4), (f"s{h}1", 5), (f"s{h}2", 6)]
        if h >= 1:
            layer += [(f"out{3 + h}", 7)]
        if h >= 2:
            layer += [(f"var{2 + h}", 6)]
    layer += [("out7", 7), ("var6", 6), ("var7", 6), ("post0", 7), ("pre1", 7), ("post1", 7)]
    second = [("pre2", 7), ("post2", 7), ("pre3", 7), ("tm3", 6)]
    second += [(f"qvar{i}", 6) for i in range(5)] + [(f"rope{i}", 4 + i % 2) for i in range(13)]
    second += [(f"pt{u}", 4 + u % 2) for u in range(64)] + [(f"o{u}", 6 + u % 2) for u in range(64)]
    second += [("post3", 7), ("pre4", 7), ("post4", 7)]
    table, used = {}, [0] * 8
    for key, b in layer:
        table[key] = (b, used[b])
        used[b] += 1
    per = list(used)
    used = [LAYERS * n for n in per]
    for key, b in second:
        table[key] = (b, used[b])
        used[b] += 1
    return table, per


def build(nc, dram):
    ctx = ExitStack()
    with ctx:
        top = [(nc.sbuf_base + 127) // 128 * 128]

        def place(name, shape, dt=F32, offset=None):
            size = 4 * math.prod(shape[1:])
            if offset is None:
                offset = top[0]
                top[0] += (size + 31) // 32 * 32
                assert top[0] <= nc.sbuf_usable_end, name
            return nc.alloc_sbuf_tensor_at(name, shape, dt, offset=offset)

        x = place("x", [P, KD, T])
        u_hi_at = top[0]
        u_hi = place("u_hi", [P, KD, T], F32R)
        u_lo = place("u_lo", [P, KD, T], F32R)
        raw = place("raw", [P, RAW, BLK])
        w_hi = place("w_hi", [P, RING, BLK], F32R)
        w_lo = place("w_lo", [P, RING, BLK], F32R)
        sq_consts = place("sq_consts", [P, N_SQ, P])
        gla_masks = place("gla_masks", [P, len(MASKED), P])
        ret_cos = place("ret_cos", [P, T])
        ret_sin = place("ret_sin", [P, T])
        r = place("r", [P, T])
        r_tm = place("r_tm", [P, TT])
        acc = place("acc", [P, T])
        par_all = place("par_all", [P, LAYERS, N_PAR])
        par = place("par", [P, N_PAR])
        par2 = place("par2", [P, N_PAR2])
        inv_freq = place("inv_freq", [P, 1])
        wa2_all = place("wa2_all", [RANK, LAYERS, GKEY])
        wa2 = place("wa2", [RANK, GKEY])
        v_sum = place("v_sum", [P, TT, HEADS])
        row_max = place("row_max", [P, 4])
        row_sum = place("row_sum", [P, 4])
        row_inv = place("row_inv", [P, 4])
        wait_cell = place("wait_cell", [P, 2 * len(UNITS)])
        scratch_at = top[0]
        S = [place(f"scratch{i}", [P, T]) for i in range(5)]
        arena = top[0]
        KB = 1024
        place("arena", [P, 88 * KB // 4])

        def region(name, shape, kb, dt=F32):
            assert kb * KB + 4 * math.prod(shape[1:]) <= 88 * KB, name
            return place(name, shape, dt, arena + int(kb * KB))

        sq_x = region("sq_x", [P, KD, T], 0)
        mix_out = region("mix_out", [P, KD, T], 0)
        ffn_out = place("ffn_out", [P, KD, T], F32, u_hi_at)
        ya_hi = region("ya_hi", [P, 4, T], 0, F32R)
        ya_lo = region("ya_lo", [P, 4, T], 8, F32R)
        ga_hi = region("ga_hi", [P, KD, P], 16, F32R)
        ga_lo = region("ga_lo", [P, KD, P], 20, F32R)
        s_diag = region("s_diag", [P, HEADS, T], 16)
        s_off = region("s_off", [P, HEADS, 768], 24)
        g_v = region("g_v", [P, TT, GVAL], 36)
        ga_t = region("ga_t", [RANK, T], 44)
        hn_r = region("hn_r", [P, 2, T], 44)
        g_cum = region("g_cum", [P, 2, T], 48)
        g_q = region("g_q", [P, 2, T], 52)
        g_k = region("g_k", [P, 2, T], 56)
        lev_e = region("lev_e", [P, 2, T], 60)
        lev_q = region("lev_q", [P, 2, T], 64)
        lev_k = region("lev_k", [P, 2, T], 68)
        c_t = region("c_t", [P, T], 72)
        c_z = region("c_z", [P, T + 2], 74)
        c_a = region("c_a", [P, T], 77)
        c_b = region("c_b", [P, T], 79)
        z_b = region("z_b", [P, 2, T], 81)
        rot_in = region("rot_in", [P, 2, T], 48)
        rot_s = region("rot_s", [P, 2, T], 52)
        y_b = region("y_b", [P, HEADS, T], 48)
        y_c = region("y_c", [P, HEADS, T], 56)
        r_q = region("r_q", [P, HEADS, T], 64)
        r_k = region("r_k", [P, HEADS, T], 72)
        r_v = region("r_v", [P, TT, RET], 80)
        ret_mask = region("ret_mask", [P, HEADS, T], 36)
        s_ret = region("s_ret", [P, 2, 1280], 16)
        yc_hi = region("yc_hi", [P, 4, T], 16, F32R)
        yc_lo = region("yc_lo", [P, 4, T], 24, F32R)
        yb_hi = region("yb_hi", [P, 4, T], 32, F32R)
        yb_lo = region("yb_lo", [P, 4, T], 40, F32R)
        mg_hi = region("mg_hi", [P, KD, T], 48, F32R)
        mg_lo = region("mg_lo", [P, KD, T], 64, F32R)
        hid_hi = region("hid_hi", [P, FT, T], 0, F32R)
        hid_lo = region("hid_lo", [P, FT, T], 44, F32R)
        a_q = region("a_q", [P, 4, T], 0)
        a_k = region("a_k", [P, 1, T], 8)
        a_v = region("a_v", [P, TT, P], 10)
        d_q = region("d_q", [P, 4, T], 12)
        d_k = region("d_k", [P, 4, T], 20)
        d_v = region("d_v", [P, TT, T], 28)
        bias = region("bias", [P, TT, T], 36)
        rope_tab = region("rope_tab", [P, 4, T], 44)
        heads = region("heads", [P, TT, D], 52)
        prob = region("prob", [P, 3, T], 68)
        prob_t = region("prob_t", [P, 2, T], 74)
        q_in = region("q_in", [P, 3, T], 78)
        q_s = region("q_s", [P, 2, T], 84)
        q_r = S[4]
        ang = [region(f"ang{i}", [P, T], 48 + 2 * i) for i in range(5)]
        pos_i = region("pos_i", [P, T], 58, I32)

        ones_c = sq_consts[:, C_ONES, :]
        ident_c = sq_consts[:, C_IDENT, :]
        tgate, sq_h = S[0:2], S[2:4]
        z_a = S[0:2]
        gt, mac, br = S[0:2], S[2:4], S[4]
        f_s, f_a = S[0:2], S[2:4]
        sq_m = S[0:2]

        ps = [ctx.enter_context(nc.psum_tensor(f"bank{b}", [P, T], F32)) for b in range(8)]

        def sem(name):
            return ctx.enter_context(nc.semaphore(name))

        consts_in = sem("consts_in")
        x_in = sem("x_in")
        stored = sem("stored")
        masks_in = sem("masks_in")
        tables_in = sem("tables_in")
        raw_in = [sem(f"raw_in{i}") for i in range(RAW)]
        hi_split = sem("hi_split")
        lo_split = sem("lo_split")
        block_done = sem("block_done")
        drained = [sem(f"drained{b}") for b in range(8)]
        filled = [sem(f"filled{b}") for b in range(8)]

        def ev(name, per, credit=0):
            return Event(sem(name), per, credit)

        x_ready = ev("x_ready", KD)
        u_hi_ev = ev("u_hi_done", KD)
        u_lo_ev = ev("u_lo_done", KD)
        sq_done = ev("sq_done", KD)
        acc_done = ev("acc_done", 14)
        r_done = ev("r_done", 2)
        out_in = ev("out_in", KD)
        t_done = ev("t_done", KD)
        r_tm_done = ev("r_tm_done", 1)
        par_done = ev("par_done", 2)
        zeroed = ev("zeroed", 5)
        ga_split = ev("ga_split", 2)
        z_abs = ev("z_abs", 2)
        z_exp = ev("z_exp", 2)
        z_ln = ev("z_ln", 2)
        z_log = ev("z_log", 2)
        cum_done = ev("cum_done", 2)
        n_lev = len(UNITS) - 2
        lev_d = ev("lev_d", n_lev)
        lev_x = ev("lev_x", n_lev)
        lev_qk = ev("lev_qk", n_lev)
        conv_t = ev("conv_t", 4)
        conv_a = ev("conv_a", 12)
        conv_y = ev("conv_y", 4)
        y_hi = ev("y_hi", 12)
        y_lo = ev("y_lo", 12)
        rot_c = ev("rot_c", 8)
        rot_y = ev("rot_y", 8)
        rv_sum = ev("rv_sum", 4)
        rv_cent = ev("rv_cent", 4)
        hn_sq = ev("hn_sq", 8)
        hn_rr = ev("hn_rr", 8)
        hn_y = ev("hn_y", 8)
        silu_g = ev("silu_g", 8)
        y_gated = ev("y_gated", 8)
        sig = ev("sig", 24)
        mac_add = ev("mac_add", 16)
        mg_hi_ev = ev("mg_hi_done", KD)
        mg_lo_ev = ev("mg_lo_done", KD)
        silu_f = ev("silu_f", FT)
        act_f = ev("act_f", FT)
        hid_hi_ev = ev("hid_hi_done", FT)
        hid_lo_ev = ev("hid_lo_done", FT)
        q_sq, q_rr, q_n = ev("q_sq", 5), ev("q_rr", 5), ev("q_n", 5)
        rope_c, rope_y = ev("rope_c", 13), ev("rope_y", 13)
        biased, maxed = ev("biased", 32), ev("maxed", 64)
        scored, inv_done = ev("scored", 64), ev("inv_done", 64)
        turned, hd_hi = ev("turned", KD), ev("hd_hi", KD)
        ang_step = sem("ang_step")
        trig_done = sem("trig_done")
        trig_tab = sem("trig_tab")

        side_table, side_per = side_banks()

        def side(key, li=None):
            b, n = side_table[key]
            return Use(ps[b], drained[b], filled[b], n if li is None else li * side_per[b] + n)

        def result(ou, e):
            b = ou.bank(e)
            return Use(ps[b], drained[b], None, ou.uses(e))

        def one(i):
            return slice(i, i + 1) if isinstance(i, int) else bass.ds(i, 1)

        def flat(t):
            return t[:, :].rearrange("p (o n) -> p o n", o=1)

        def three(out, st_hi, st_lo, mv_hi, mv_lo, first, last):
            nc.tensor.matmul(out, st_hi, mv_hi, start=first, stop=False)
            nc.tensor.matmul(out, st_hi, mv_lo, start=False, stop=False)
            return nc.tensor.matmul(out, st_lo, mv_hi, start=False, stop=last)

        def pe_block(pe, bl, p, ou, e, in_hi, in_lo, k0=0, kn=KD, first=True, last=True, each_k=None):
            b, s = ou.bank(e), bl.slot(p)
            pe.wait_ge(lo_split, bl.n(p) + (RAW + 1))
            if first:
                pe.wait_ge(drained[b], ou.uses(e) + 1)
            for k in range(kn):
                if each_k is not None:
                    each_k(k)
                w = slice(k * P, (k + 1) * P)
                mm = three(ps[b][:, :], w_hi[:, s, w], w_lo[:, s, w], in_hi[:, k0 + k, :], in_lo[:, k0 + k, :],
                           first and k == 0, last and k == kn - 1)
            mm.then_inc(block_done, 1)

        def pe_values(pe, bl, p, ou, e):
            for q in range(4):
                s = bl.slot(p + q)
                pe.wait_ge(lo_split, bl.n(p + q) + (RAW + 1))
                for k2 in range(2):
                    k = 2 * q + k2
                    w = slice(k2 * T, (k2 + 1) * T)
                    for t in range(TT):
                        if k == 0:
                            pe.wait_ge(drained[ou.bank(e + t)], ou.uses(e + t) + 1)
                        tok = slice(t * P, (t + 1) * P)
                        mm = three(ps[ou.bank(e + t)][:, :], u_hi[:, k, tok], u_lo[:, k, tok],
                                   w_hi[:, s, w], w_lo[:, s, w], k == 0, k == KD - 1)
                mm.then_inc(block_done, 1)

        def pe_sums(pe, key, s, n, li=None):
            use = side(key, li)
            pe.wait_ge(use.drained, use.n + 1)
            pe.wait_ge(acc_done.sem, acc_done.upto(s, n))
            nc.tensor.matmul(use.mem[:, :], ones_c, acc[:, :], start=True, stop=True).then_inc(use.filled, 1)

        def pe_sums_tm(pe, key, li=None):
            use = side(key, li)
            pe.wait_ge(use.drained, use.n + 1)
            for t in range(TT):
                mm = nc.tensor.matmul(use.mem[:, 2 * t:2 * t + 2], acc[:, t * P:(t + 1) * P], ones_c[:, 0:2],
                                      start=True, stop=True)
            mm.then_inc(use.filled, 1)

        def act_split(act, bl, p):
            act.wait_ge(raw_in[bl.raw(p)], bl.raw_uses(p) * 16 + 16)
            act.wait_ge(block_done, bl.n(p) + 1)
            nc.scalar.activation(w_hi[:, bl.slot(p), :], raw[:, bl.raw(p), :], ACT.Copy).then_inc(hi_split, 1)

        def dve_split(dve, bl, p):
            dve.wait_ge(hi_split, bl.n(p) + 1)
            nc.vector.tensor_tensor(w_lo[:, bl.slot(p), :], raw[:, bl.raw(p), :],
                                    w_hi[:, bl.slot(p), :].bitcast(F32), ALU.subtract).then_inc(lo_split, 1)

        def act_pre(act, s, gains):
            for k in range(KD):
                act.wait_ge(x_ready.sem, x_ready.upto(s, k + 1))
                nc.scalar.activation(u_hi[:, k, :], x[:, k, :], ACT.Copy, scale=gains[:, k:k + 1]).then_inc(u_hi_ev.sem, 1)
                nc.scalar.activation(sq_x[:, k, :], x[:, k, :], ACT.Square).then_inc(sq_done.sem, 1)

        def act_rsqrt(act, key, li=None, half=False):
            four = 4.0 if half else 1.0
            use = side(key, li)
            act.wait_ge(use.filled, use.n + 1)
            nc.scalar.activation(r[:, :], use.mem[:, :], ACT.Ln, scale=four / D, bias=four * EPS).then_inc(use.drained, 1)
            src = side(key, li)
            act.wait_ge(src.drained, src.n + 2)
            nc.scalar.activation(r[:, :], r[:, :], ACT.Exp, scale=-0.5).then_inc(r_done.sem, 1)

        def act_rsqrt_tm(act, key, li=None):
            use = side(key, li)
            act.wait_ge(use.filled, use.n + 1)
            nc.scalar.activation(r_tm[:, :], use.mem[:, 0:2 * TT:2], ACT.Ln, scale=1.0 / D, bias=EPS).then_inc(use.drained, 1)
            src = side(key, li)
            act.wait_ge(src.drained, src.n + 2)
            nc.scalar.activation(r_tm[:, :], r_tm[:, :], ACT.Exp, scale=-0.5).then_inc(r_tm_done.sem, 1)

        def dve_pre(dve, s, gains):
            for k in range(KD):
                dve.wait_ge(u_hi_ev.sem, u_hi_ev.upto(s, k + 1))
                nc.vector.scalar_tensor_tensor(u_lo[:, k, :], x[:, k, :], gains[:, k:k + 1],
                                               u_hi[:, k, :].bitcast(F32), ALU.mult, ALU.subtract).then_inc(u_lo_ev.sem, 1)
            for k in range(1, KD):
                dve.wait_ge(sq_done.sem, sq_done.upto(s, k + 1))
                if k > 1:
                    dve.wait_ge(acc_done.sem, acc_done.upto(s, k - 1))
                nc.vector.tensor_tensor(acc[:, :], sq_x[:, 0, :] if k == 1 else acc[:, :], sq_x[:, k, :],
                                        ALU.add).then_inc(acc_done.sem, 1)

        def dve_out(dve, bl, p, ou, e, out):
            use = result(ou, e)
            dve.wait_ge(block_done, bl.n(p) + (RING + 1))
            nc.vector.tensor_scalar(out, use.mem[:, :], 1.0, None, ALU.mult).then_inc(out_in.sem, 1)

        def dve_out_acc(dve, s, m, ou, e):
            dve.wait_ge(drained[ou.bank(e)], ou.uses(e) + 2)
            if m > 1:
                dve.wait_ge(acc_done.sem, acc_done.upto(s, 7 + m - 1))
            nc.vector.tensor_tensor(acc[:, :], sq_m[0][:, :] if m == 1 else acc[:, :], sq_m[m % 2][:, :],
                                    ALU.add).then_inc(acc_done.sem, 1)

        def act_out(act, s, m, ou, e):
            act.wait_ge(out_in.sem, out_in.upto(s, m + 1))
            if m >= 2:
                act.wait_ge(acc_done.sem, acc_done.upto(s, 7 + max(m - 2, 1)))
            b = ou.bank(e)
            nc.scalar.activation(sq_m[m % 2][:, :], ps[b][:, :], ACT.Square).then_inc(drained[b], 1)

        def dve_post(dve, s, gains, out):
            dve.wait_ge(r_done.sem, r_done.upto(s, 2))
            for k in range(KD):
                nc.vector.scalar_tensor_tensor(out[:, k, :], out[:, k, :], gains[:, k:k + 1], r[:, :],
                                               ALU.mult, ALU.mult).then_inc(t_done.sem, 1)

        def pool_post(pool, s, out):
            for k in range(KD):
                pool.wait_ge(t_done.sem, t_done.upto(s, k + 1))
                nc.gpsimd.tensor_tensor(x[:, k, :], x[:, k, :], out[:, k, :], ALU.add).then_inc(x_ready.sem, 1)

        def turn(bl, ou, j, blocks, outs):
            return Blocks(bl.quads + j * (blocks // 4), bl.s), Outs(ou.quads + j * (outs // 4), ou.s)

        def pe_ffn(pe, s, f, bl, ou, pre, post, li=None):
            def first_k(k):
                pe.wait_ge(u_lo_ev.sem, u_lo_ev.upto(s, k + 1))
            for i in range(N_UP):
                pe_block(pe, bl, i, ou, i, u_hi, u_lo, each_k=first_k if i == 0 else None)
                if i == 0:
                    pe_sums(pe, pre, s, 7, li)
            with pe.Fori(1, UP_TURNS) as j:
                b, o = turn(bl, ou, j, N_UP, N_UP)
                for i in range(N_UP):
                    pe_block(pe, b, i, o, i, u_hi, u_lo)
            b1, o1 = bl.on(N_UP * UP_TURNS), ou.on(N_UP * UP_TURNS)
            for m in range(KD):
                k0 = 0
                for q, kn in enumerate(DOWN_K):
                    def hidden_k(k, k0=k0):
                        if k0 + k == 0:
                            pe.wait_ge(hid_lo_ev.sem, hid_lo_ev.upto(f, FT - 4))
                        if k0 + k >= FT - 4:
                            pe.wait_ge(hid_lo_ev.sem, hid_lo_ev.upto(f, k0 + k + 1))
                    pe_block(pe, b1, 3 * m + q, o1, m, hid_hi, hid_lo, k0, kn, q == 0, q == 2, hidden_k if m == 0 else None)
                    k0 += kn
            pe_sums(pe, post, s, 14, li)

        def act_ffn(act, s, f, bl, ou, gains, pre, post, li=None, half=False, last=False):
            act_pre(act, s, gains)

            def up(j):
                b, o = turn(bl, ou, j, N_UP, N_UP)
                for i in range(2):
                    act_split(act, b, 2 * i + AHEAD)
                    if isinstance(j, int) and i == 0:
                        act_rsqrt(act, pre, li)
                    act.wait_ge(drained[o.bank(2 * i)], o.uses(2 * i) + 2)
                    nc.scalar.activation(f_s[i][:, :], f_s[i][:, :], ACT.Silu).then_inc(silu_f.sem, 1)
                    act_split(act, b, 2 * i + 1 + AHEAD)
                    act.wait_ge(act_f.sem, act_f.upto(f, j * 2 + (i + 1)))
                    act.wait_ge(consts_in, CONSTS)
                    nc.scalar.activation(hid_hi[:, one(j * 2 + i), :], flat(f_a[i]), ACT.Copy).then_inc(hid_hi_ev.sem, 1)
            up(0)
            with act.Fori(1, UP_TURNS) as j:
                up(j)
            b1, o1 = bl.on(N_UP * UP_TURNS), ou.on(N_UP * UP_TURNS)
            nc.scalar.preload_act_table_set(EXP_LN)
            for m in range(KD):
                for q in range(3):
                    if not last or 3 * m + q + AHEAD < 3 * KD:
                        act_split(act, b1, 3 * m + q + AHEAD)
                act_out(act, s, m, o1, m)
            act_rsqrt(act, post, li, half)

        def dve_ffn(dve, s, f, bl, ou, pre_gains, post_gains, last=False):
            dve_pre(dve, s, pre_gains)

            def up(j):
                b, o = turn(bl, ou, j, N_UP, N_UP)
                for i in range(2):
                    dve_split(dve, b, 2 * i + AHEAD)
                    if isinstance(j, int) and i == 0:
                        dve.wait_ge(r_done.sem, r_done.upto(s, 1))
                    use = result(o, 2 * i)
                    dve.wait_ge(block_done, b.n(2 * i) + (RING + 1))
                    nc.vector.tensor_tensor(f_s[i][:, :], use.mem[:, :], r[:, :], ALU.mult).then_inc(use.drained, 1)
                    dve_split(dve, b, 2 * i + 1 + AHEAD)
                    use = result(o, 2 * i + 1)
                    dve.wait_ge(block_done, b.n(2 * i + 1) + (RING + 1))
                    dve.wait_ge(silu_f.sem, silu_f.upto(f, j * 2 + (i + 1)))
                    nc.vector.tensor_tensor(f_a[i][:, :], use.mem[:, :], f_s[i][:, :], ALU.mult).then_inc(use.drained, 1)
                    dve.wait_ge(drained[o.bank(2 * i + 1)], o.uses(2 * i + 1) + 2)
                    nc.vector.tensor_tensor(f_a[i][:, :], f_a[i][:, :], r[:, :], ALU.mult).then_inc(act_f.sem, 1)
                    dve.wait_ge(hid_hi_ev.sem, hid_hi_ev.upto(f, j * 2 + (i + 1)))
                    nc.vector.tensor_tensor(hid_lo[:, one(j * 2 + i), :], flat(f_a[i]),
                                            hid_hi[:, one(j * 2 + i), :].bitcast(F32), ALU.subtract).then_inc(hid_lo_ev.sem, 1)
            up(0)
            with dve.Fori(1, UP_TURNS) as j:
                up(j)
            b1, o1 = bl.on(N_UP * UP_TURNS), ou.on(N_UP * UP_TURNS)
            for m in range(KD):
                for q in range(3):
                    if not last or 3 * m + q + AHEAD < 3 * KD:
                        dve_split(dve, b1, 3 * m + q + AHEAD)
                dve_out(dve, b1, 3 * m + 2, o1, m, ffn_out[:, m, :])
                if m >= 2:
                    dve_out_acc(dve, s, m - 1, o1, m - 1)
            dve_out_acc(dve, s, KD - 1, o1, KD - 1)
            dve_post(dve, s, post_gains, ffn_out)

        GQ, GK, GV, CV, RQ, RK, RV, GR, RG = 0, 2, 4, 8, 20, 24, 28, 32, 36
        unit_no = {u: i for i, u in enumerate(UNITS)}

        def conv_units(i):
            return [2 + 2 * (i - 3), 3 + 2 * (i - 3)] if 3 <= i <= 11 else []

        def halves(ap, lev):
            v = ap.rearrange("p (n b) -> p n b", b=lev)
            h = lev // 2
            return v[:, :, 0:h], v[:, :, h:lev], v[:, :, h - 1:h].to_broadcast([P, T // lev, h])

        def head_rows(h):
            return slice(HD * (h % 2), HD * (h % 2) + HD)

        def tok(i, n=1):
            return slice(i * P, (i + n) * P)

        def rope_tile(i):
            if i < 5:
                return (a_q[:, i, :] if i < 4 else a_k[:, 0, :]), i, 0, C_ROT16
            return (d_q if i < 9 else d_k)[:, (i - 5) % 4, :], i + 1, 2, C_ROT32

        def attention_unit(u):
            dense, t, h, it = u < 32, u % 32 // 8, u // 4 % 2, u % 4
            return dense, t, h, it, HD * (t + 4 * h if dense else 8 + 2 * t + h)

        block = ctx.enter_context(nc.Block())

        @block.sync
        def _(sp):
            for to, name in ((inv_freq[:, :], "inv_freq"), (pos_i[:, :], "positions"), (sq_consts[:, :, :], "sq_consts"),
                             (par_all[:, :, :], "par_all"), (wa2_all[:, :, :], "wa2"), (par2[:, :], "par2"),
                             (gla_masks[:, :, :], "gla_masks")):
                src = dram[name].to_broadcast([P, T]) if name == "positions" else dram[name]
                sp.dma_start(to, src).then_inc(consts_in, 16)
            sp.dma_start(x[:, :, :], dram["x"]).then_inc(x_in, 16)

            def load(bl, p, col, size):
                if isinstance(col, int):
                    src = dram["weights"][:, col:col + size]
                else:
                    src = dram["weights"][:, bass.ds(sp.snap(col), size)]
                sp.wait_ge(lo_split, bl.n(p) + 1)
                sp.dma_start(raw[:, bl.raw(p), 0:size], src).then_inc(raw_in[bl.raw(p)], 16)

            def ffn(bl, col):
                with sp.Fori(0, UP_TURNS) as j:
                    for i in range(N_UP):
                        load(Blocks(bl.quads + j, bl.s), i, j * (N_UP * BLK) + (col + i * BLK), BLK)
                b, c = bl.on(N_UP * UP_TURNS), col + UP_TURNS * N_UP * BLK
                with sp.Fori(0, DOWN_TURNS) as j:
                    at = 0
                    for m in range(4):
                        for q, kn in enumerate(DOWN_K):
                            load(Blocks(b.quads + j * (N_DOWN // 4), b.s), 3 * m + q, j * COLS_DOWN + (c + at), kn * P)
                            at += kn * P

            with sp.Fori(0, LAYERS) as li:
                bl, col = Blocks(li * (N_LAYER // 4)), li * COLS_LAYER
                for i in range(N_HEAD):
                    load(bl, i, col + i * BLK, BLK)
                    if i == RV + 3:
                        src = side("out3", li)
                        sp.wait_ge(src.drained, src.n + 2)
                        sp.dma_start(ret_mask[:, :, :], dram["ret_mask"]).then_inc(masks_in, 16)
                with sp.Fori(0, GATE_TURNS) as j:
                    at = N_HEAD * BLK
                    for i in range(N_GATE):
                        size = BLK if i % 2 == 0 else BLK // 2
                        load(Blocks(bl.quads + j * (N_GATE // 4), N_HEAD), i, li * COLS_LAYER + j * COLS_GATE + at, size)
                        at += size
                b = bl.on(N_HEAD + N_GATE * GATE_TURNS)
                c = N_HEAD * BLK + GATE_TURNS * COLS_GATE
                for i in range(KD):
                    load(b, i, col + (c + i * BLK), BLK)
                ffn(b.on(KD), col + (c + KD * BLK))
            bl, col = Blocks(LAYERS * (N_LAYER // 4)), LAYERS * COLS_LAYER
            ffn(bl, col)
            bl, col = bl.on(N_FFN), col + COLS_FFN
            for i in range(N_QKV + KD):
                load(bl, i, col + i * BLK, BLK)
                if i == RING:
                    sp.wait_ge(r_done.sem, r_done.upto(4, 2))
                    sp.dma_start(bias[:, :, :], dram["bias"]).then_inc(tables_in, 16)
                    sp.dma_start(rope_tab[:, :, :], dram["rope_tab"]).then_inc(tables_in, 16)
            ffn(bl.on(N_QKV + KD), col + (N_QKV + KD) * BLK)
            for k in range(KD):
                sp.wait_ge(x_ready.sem, x_ready.upto(7, k + 1))
                sp.dma_start(dram["out"][:, k, :], x[:, k, :]).then_inc(stored, 16)
            sp.wait_ge(stored, 16 * KD)

        @block.gpsimd
        def _(pool):
            credits = [(lo_split, RAW), (block_done, RING)] + [(d, 1) for d in drained] + [(x_ready.sem, KD)]
            for i, (free, n) in enumerate(credits):
                if free is x_ready.sem:
                    pool.wait_ge(x_in, 16)
                nc.gpsimd.memset(wait_cell[:, i:i + 1], 0.0).then_inc(free, n)
            with pool.Fori(0, LAYERS) as li:
                nc.gpsimd.memset(ga_hi[:, :, :].bitcast(F32), 0.0).then_inc(zeroed.sem, 1)
                nc.gpsimd.memset(ga_lo[:, :, :].bitcast(F32), 0.0).then_inc(zeroed.sem, 1)
                nc.gpsimd.memset(lev_q[:, :, :], 0.0).then_inc(zeroed.sem, 1)
                nc.gpsimd.memset(lev_k[:, :, :], 0.0).then_inc(zeroed.sem, 1)
                nc.gpsimd.memset(c_z[:, 0:2], 0.0).then_inc(zeroed.sem, 1)
                ou = Outs(li * (OUT_LAYER // 4))
                for i in range(8):
                    to = (r_q if i < 4 else r_k)[:, i % 4, :]
                    if i == 0:
                        old = side(f"gla{len(UNITS) - 1}1", li)
                        pool.wait_ge(old.filled, old.n + 1)
                    pool.wait_ge(drained[ou.bank(RQ + i)], ou.uses(RQ + i) + 2)
                    nc.gpsimd.tensor_tensor(to, rot_in[:, i % 2, :], ret_cos[:, :], ALU.mult).then_inc(rot_c.sem, 1)
                    src = side(f"rot{i}", li)
                    pool.wait_ge(src.drained, src.n + 2)
                    pool.wait_ge(rot_c.sem, rot_c.upto(li, i + 1))
                    nc.gpsimd.tensor_tensor(to, to, rot_s[:, i % 2, :], ALU.add).then_inc(rot_y.sem, 1)
                pool_post(pool, li * 2, mix_out)
                pool_post(pool, li * 2 + 1, ffn_out)
            pool_post(pool, 4, ffn_out)
            ou = Outs(LAYERS * (OUT_LAYER // 4), OUT_FFN)
            pool.wait_ge(tables_in, 32)
            for i in range(13):
                to, e, tab, _ = rope_tile(i)
                if i < 5:
                    pool.wait_ge(q_n.sem, q_n.upto(0, i + 1))
                else:
                    pool.wait_ge(drained[ou.bank(e)], ou.uses(e) + 2)
                nc.gpsimd.tensor_tensor(to, q_in[:, i % 3, :], rope_tab[:, tab, :], ALU.mult).then_inc(rope_c.sem, 1)
                src = side(f"rope{i}")
                pool.wait_ge(src.drained, src.n + 2)
                pool.wait_ge(rope_c.sem, rope_c.upto(0, i + 1))
                nc.gpsimd.tensor_tensor(to, to, q_s[:, i % 2, :], ALU.add).then_inc(rope_y.sem, 1)
            pool_post(pool, 5, mix_out)
            pool_post(pool, 6, ffn_out)

        @block.tensor
        def _(pe):
            def unit(u, li):
                lev, t = UNITS[u]
                if lev == 1:
                    for e in range(4):
                        pe.wait_ge(drained[Outs(li * (OUT_LAYER // 4)).bank(GQ + e)], Outs(li * (OUT_LAYER // 4)).uses(GQ + e) + 2)
                    q, k = g_q[:, t, :], g_k[:, t, :]
                else:
                    pe.wait_ge(lev_qk.sem, lev_qk.upto(li, u - 1))
                    q, k = lev_q[:, u % 2, :], lev_k[:, u % 2, :]
                if lev == 512:
                    parts = [(0, 2, 2, 0), (1, 2, 2, 256)]
                elif lev == 256:
                    parts = [(0, 1, 1, 0), (2, 3, 1, 128)]
                else:
                    parts = [(i, i, 1, i * P) for i in range(TT)]
                for h in range(2):
                    use = side(f"gla{u}{h}", li)
                    pe.wait_ge(use.drained, use.n + 1)
                    for kt, qt, n, c in parts:
                        mm = nc.tensor.matmul(use.mem[:, c:c + n * P], k[head_rows(h), tok(kt)], q[head_rows(h), tok(qt, n)],
                                              start=True, stop=True)
                    mm.then_inc(use.filled, 1)

            def gla_out(h, li):
                if h % 2 == 0:
                    for t in range(TT):
                        pe.wait_ge(drained[Outs(li * (OUT_LAYER // 4)).bank(GV + t)], Outs(li * (OUT_LAYER // 4)).uses(GV + t) + 2)
                    for hh in range(2):
                        src = side(f"gla{unit_no[(512, h // 2)]}{hh}", li)
                        pe.wait_ge(src.drained, src.n + 2)
                use = side(f"out{h}", li)
                pe.wait_ge(use.drained, use.n + 1)

                def add(kt, qt, n, s, first=False, last=False):
                    return nc.tensor.matmul(use.mem[:, tok(qt, n)], g_v[:, kt, tok(h)], s, start=first, stop=last)
                for i in range(TT):
                    add(i, i, 1, s_diag[:, h, tok(i)], i == 0)
                add(0, 1, 1, s_off[:, h, 0:128])
                add(2, 3, 1, s_off[:, h, 128:256])
                add(0, 2, 2, s_off[:, h, 256:512])
                add(1, 2, 2, s_off[:, h, 512:768], last=True).then_inc(use.filled, 1)

            def ret_scores(h, li):
                pe.wait_ge(rot_y.sem, rot_y.upto(li, 4 + h + 1))
                use = side(f"s{h}0", li)
                pe.wait_ge(use.drained, use.n + 1)
                nc.tensor.matmul(use.mem[:, :], r_k[:, h, tok(0)], r_q[:, h, :], start=True, stop=True).then_inc(use.filled, 1)
                use = side(f"s{h}1", li)
                pe.wait_ge(use.drained, use.n + 1)
                nc.tensor.matmul(use.mem[:, 0:384], r_k[:, h, tok(1)], r_q[:, h, tok(1, 3)], start=True, stop=True)
                nc.tensor.matmul(use.mem[:, 384:512], r_k[:, h, tok(3)], r_q[:, h, tok(3)], start=True, stop=True).then_inc(use.filled, 1)
                use = side(f"s{h}2", li)
                pe.wait_ge(use.drained, use.n + 1)
                nc.tensor.matmul(use.mem[:, 0:256], r_k[:, h, tok(2)], r_q[:, h, tok(2, 2)], start=True, stop=True).then_inc(use.filled, 1)

            def ret_out(h, li):
                for i in range(3):
                    src = side(f"s{h}{i}", li)
                    pe.wait_ge(src.drained, src.n + 2)
                if h == 0:
                    pe.wait_ge(rv_cent.sem, rv_cent.upto(li, 4))
                use = side(f"out{4 + h}", li)
                pe.wait_ge(use.drained, use.n + 1)
                s = s_ret[:, h % 2, :]
                for kt, a, b in ((0, 0, 512), (1, 512, 896), (2, 896, 1152), (3, 1152, 1280)):
                    mm = nc.tensor.matmul(use.mem[:, tok(kt, TT - kt)], r_v[:, kt, tok(h)], s[:, a:b], start=kt == 0, stop=kt == 3)
                mm.then_inc(use.filled, 1)

            def head_var(n, li):
                pe.wait_ge(hn_sq.sem, hn_sq.upto(li, n + 1))
                use = side(f"var{n}", li)
                pe.wait_ge(use.drained, use.n + 1)
                nc.tensor.matmul(use.mem[:, :], ones_c, sq_h[n % 2][:, :], start=True, stop=True).then_inc(use.filled, 1)

            def rotate(i, li):
                pe.wait_ge(drained[Outs(li * (OUT_LAYER // 4)).bank(RQ + i)], Outs(li * (OUT_LAYER // 4)).uses(RQ + i) + 2)
                use = side(f"rot{i}", li)
                pe.wait_ge(use.drained, use.n + 1)
                nc.tensor.matmul(use.mem[:, :], sq_consts[:, C_ROT64, :], rot_in[:, i % 2, :], start=True, stop=True).then_inc(use.filled, 1)

            def layer(li):
                bl, ou, s = Blocks(li * (N_LAYER // 4)), Outs(li * (OUT_LAYER // 4)), li * 2

                def project(i):
                    pe_block(pe, bl, i, ou, i, u_hi, u_lo)

                def first_k(k):
                    pe.wait_ge(u_lo_ev.sem, u_lo_ev.upto(s, k + 1))
                pe_block(pe, bl, 0, ou, 0, u_hi, u_lo, each_k=first_k)
                pe_sums(pe, "pre0", s, 7, li)
                pe_sums_tm(pe, "tm0", li)
                for i in range(1, 4):
                    project(i)
                pe.wait_ge(ga_split.sem, ga_split.upto(li, 2))
                use = side("ga", li)
                pe.wait_ge(use.drained, use.n + 1)
                for k in range(KD):
                    mm = three(use.mem[:, :], ga_hi[:, k, :], ga_lo[:, k, :], u_hi[:, k, :], u_lo[:, k, :], k == 0, k == KD - 1)
                mm.then_inc(use.filled, 1)
                pe_values(pe, bl, GV, ou, GV)
                src = side("ga", li)
                pe.wait_ge(src.drained, src.n + 2)
                pe.wait_ge(par_done.sem, par_done.upto(li, 2))
                for t in range(2):
                    use = side(f"z{t}", li)
                    pe.wait_ge(use.drained, use.n + 1)
                    nc.tensor.matmul(use.mem[:, :], wa2[:, tok(t)], ga_t[:, :], start=True, stop=True).then_inc(use.filled, 1)
                unit(0, li)
                unit(1, li)
                for i in range(12):
                    project(CV + i)
                    for u in conv_units(i - 1):
                        unit(u, li)
                project(RQ)
                for u in conv_units(11):
                    unit(u, li)
                for i in range(1, 8):
                    project(RQ + i)
                    rotate(i - 1, li)
                    if i <= 4:
                        gla_out(i - 1, li)
                    if 2 <= i <= 5:
                        head_var(i - 2, li)
                pe_values(pe, bl, RV, ou, RV)
                rotate(7, li)
                for h in range(HEADS):
                    project(GR + h)
                    ret_scores(h, li)
                    if h >= 1:
                        ret_out(h - 1, li)
                    if h >= 2:
                        head_var(2 + h, li)
                project(RG)
                ret_out(3, li)
                head_var(6, li)
                project(RG + 1)
                head_var(7, li)
                project(RG + 2)
                project(RG + 3)
                with pe.Fori(0, GATE_TURNS) as j:
                    b, o = turn(bl.on(N_HEAD), ou.on(N_HEAD), j, N_GATE, N_GATE)
                    for i in range(N_GATE // 2):
                        pe_block(pe, b, 2 * i, o, 2 * i, u_hi, u_lo)
                        pe.wait_ge(y_lo.sem, y_lo.upto(li, 12 if i % 3 == 2 else 8))
                        y = ((ya_hi, ya_lo), (yc_hi, yc_lo), (yb_hi, yb_lo))[i % 3]
                        pe_block(pe, b, 2 * i + 1, o, 2 * i + 1, y[0], y[1], kn=4)
                b, o = bl.on(N_HEAD + N_GATE * GATE_TURNS), ou.on(N_HEAD + N_GATE * GATE_TURNS)

                def merged_k(k):
                    pe.wait_ge(mg_lo_ev.sem, mg_lo_ev.upto(li, k + 1))
                for i in range(KD):
                    pe_block(pe, b, i, o, i, mg_hi, mg_lo, each_k=merged_k if i == 0 else None)
                pe_sums(pe, "post0", s, 14, li)
                pe_ffn(pe, s + 1, li, b.on(KD), o.on(KD), "pre1", "post1", li)

            pe.wait_ge(consts_in, CONSTS)
            with pe.Fori(0, LAYERS) as li:
                layer(li)

            bl, ou = Blocks(LAYERS * (N_LAYER // 4)), Outs(LAYERS * (OUT_LAYER // 4))
            pe_ffn(pe, 4, 2, bl, ou, "pre2", "post2")
            bl, ou = bl.on(N_FFN), ou.on(OUT_FFN)

            def first_k(k):
                pe.wait_ge(u_lo_ev.sem, u_lo_ev.upto(5, k + 1))

            def q_var(i):
                pe.wait_ge(q_sq.sem, q_sq.upto(0, i + 1))
                use = side(f"qvar{i}")
                pe.wait_ge(use.drained, use.n + 1)
                nc.tensor.matmul(use.mem[:, :], sq_consts[:, C_BD64, :], sq_h[i % 2][:, :], start=True, stop=True).then_inc(use.filled, 1)

            def rope(i):
                _, e, _, rot = rope_tile(i)
                if i < 5:
                    pe.wait_ge(q_n.sem, q_n.upto(0, i + 1))
                else:
                    pe.wait_ge(drained[ou.bank(e)], ou.uses(e) + 2)
                use = side(f"rope{i}")
                pe.wait_ge(use.drained, use.n + 1)
                nc.tensor.matmul(use.mem[:, :], sq_consts[:, rot, :], q_in[:, i % 3, :], start=True, stop=True).then_inc(use.filled, 1)

            for i in range(14):
                if i == 5:
                    b, s = ou.bank(5), bl.slot(5)
                    pe.wait_ge(lo_split, bl.n(5) + (RAW + 1))
                    pe.wait_ge(drained[b], ou.uses(5) + 1)
                    for t in range(TT):
                        for k in range(KD):
                            mm = three(ps[b][:, tok(t)], u_hi[:, k, tok(t)], u_lo[:, k, tok(t)],
                                       w_hi[:, s, tok(k)], w_lo[:, s, tok(k)], k == 0, k == KD - 1)
                    mm.then_inc(block_done, 1)
                else:
                    pe_block(pe, bl, i, ou, i, u_hi, u_lo, each_k=first_k if i == 0 else None)
                if i == 0:
                    pe_sums(pe, "pre3", 5, 7)
                    pe_sums_tm(pe, "tm3")
                if 1 <= i <= 5:
                    q_var(i - 1)
                if i >= 2:
                    rope(i - 2)
            pe_values(pe, bl, 14, ou, 14)
            rope(12)

            def score(u):
                dense, t, h, it, _ = attention_unit(u)
                if u == 0:
                    pe.wait_ge(rope_y.sem, rope_y.upto(0, 5))
                if u == 32:
                    pe.wait_ge(rope_y.sem, rope_y.upto(0, 13))
                e = N_QKV + u
                pe.wait_ge(drained[ou.bank(e)], ou.uses(e) + 1)
                q, k = (a_q, a_k[:, 0, :]) if dense else (d_q, d_k[:, t, :])
                nc.tensor.matmul(ps[ou.bank(e)][:, :], q[head_rows(h), t, tok(it)], k[head_rows(h), :],
                                 start=True, stop=True).then_inc(scored.sem, 1)

            def turn_probs(u):
                pe.wait_ge(drained[ou.bank(N_QKV + u)], ou.uses(N_QKV + u) + 2)
                use = side(f"pt{u}")
                pe.wait_ge(use.drained, use.n + 1)
                for j in range(TT):
                    mm = nc.tensor.transpose(use.mem[:, tok(j)], prob[:, u % 3, tok(j)], ident_c)
                mm.then_inc(use.filled, 1)

            def weigh(u):
                dense, t, h, it, _ = attention_unit(u)
                if u == 0:
                    pe.wait_ge(drained[ou.bank(5)], ou.uses(5) + 2)
                if u == 32:
                    for i in range(TT):
                        pe.wait_ge(drained[ou.bank(14 + i)], ou.uses(14 + i) + 2)
                src = side(f"pt{u}")
                pe.wait_ge(src.drained, src.n + 2)
                use = side(f"o{u}")
                pe.wait_ge(use.drained, use.n + 1)
                v, c = (a_v, HD * h) if dense else (d_v, HD * (2 * t + h))
                for j in range(TT):
                    mm = nc.tensor.matmul(use.mem[:, 0:HD], prob_t[:, u % 2, tok(j)], v[:, j, c:c + HD], start=j == 0, stop=j == TT - 1)
                mm.then_inc(use.filled, 1)

            for u in range(-3, 64):
                if u + 3 < 64:
                    score(u + 3)
                if u >= 0:
                    turn_probs(u)
                if u >= 1:
                    weigh(u - 1)
            weigh(63)
            for k in range(KD):
                e = N_QKV + 64 + k
                if k == 0:
                    src = side("o62")
                    pe.wait_ge(src.drained, src.n + 2)
                    src = side("o63")
                    pe.wait_ge(src.drained, src.n + 2)
                pe.wait_ge(drained[ou.bank(e)], ou.uses(e) + 1)
                for t in range(TT):
                    mm = nc.tensor.transpose(ps[ou.bank(e)][:, tok(t)], heads[:, t, tok(k)], ident_c)
                mm.then_inc(turned.sem, 1)

            def heads_k(k):
                pe.wait_ge(drained[ou.bank(N_QKV + 64 + k)], ou.uses(N_QKV + 64 + k) + 2)
            for i in range(KD):
                pe_block(pe, bl, N_QKV + i, ou, N_QKV + 64 + KD + i, u_hi, u_lo, each_k=heads_k if i == 0 else None)
            pe_sums(pe, "post3", 5, 14)
            pe_ffn(pe, 6, 3, bl.on(N_QKV + KD), ou.on(N_QKV + 64 + 2 * KD), "pre4", "post4")

        @block.scalar
        def _(act):
            def head_copy(n, li):
                y = (y_c if n < 4 else y_b)[:, n % 4, :]
                if n == 4:
                    act.wait_ge(rot_y.sem, rot_y.upto(li, 8))
                use = side(f"out{n}", li)
                act.wait_ge(use.filled, use.n + 1)
                nc.scalar.activation(y, use.mem[:, :], ACT.Copy).then_inc(use.drained, 1)
                src = side(f"out{n}", li)
                act.wait_ge(src.drained, src.n + 2)
                nc.scalar.activation(sq_h[n % 2][:, :], y, ACT.Square).then_inc(hn_sq.sem, 1)

            def head_rsqrt(n, li):
                use = side(f"var{n}", li)
                act.wait_ge(use.filled, use.n + 1)
                if n >= 2:
                    act.wait_ge(hn_y.sem, hn_y.upto(li, n - 1))
                nc.scalar.activation(hn_r[:, n % 2, :], use.mem[:, :], ACT.Ln, scale=1.0 / P, bias=EPS).then_inc(use.drained, 1)
                src = side(f"var{n}", li)
                act.wait_ge(src.drained, src.n + 2)
                nc.scalar.activation(hn_r[:, n % 2, :], hn_r[:, n % 2, :], ACT.Exp, scale=-0.5).then_inc(hn_rr.sem, 1)

            def level_exp(u, li):
                act.wait_ge(lev_d.sem, lev_d.upto(li, u - 1))
                nc.scalar.activation(lev_e[:, u % 2, :], lev_e[:, u % 2, :], ACT.Exp, scale=1.0 / 16).then_inc(lev_x.sem, 1)

            def take_off(u, li):
                lev, t = UNITS[u]
                for h in range(2):
                    use = side(f"gla{u}{h}", li)
                    act.wait_ge(use.filled, use.n + 1)
                    a, n = (0, 256) if lev == 256 else (256, 512)
                    nc.scalar.activation(s_off[:, 2 * t + h, a:a + n], use.mem[:, 0:n], ACT.Copy).then_inc(use.drained, 1)

            def values(bl, p, ou, e, to):
                for t in range(TT):
                    use = result(ou, e + t)
                    act.wait_ge(block_done, bl.n(p + 3) + (RING + 1))
                    nc.scalar.activation(to[:, t, :], use.mem[:, :], ACT.Copy, scale=r_tm[:, t:t + 1]).then_inc(use.drained, 1)

            def gate_silu(g, ou, li):
                act.wait_ge(drained[ou.bank(GR + g)], ou.uses(GR + g) + 2)
                nc.scalar.activation(tgate[g % 2][:, :], tgate[g % 2][:, :], ACT.Silu).then_inc(silu_g.sem, 1)

            def y_high(n, li):
                if n < 4:
                    act.wait_ge(conv_y.sem, conv_y.upto(li, n + 1))
                    to, of = ya_hi, c_a[:, :]
                else:
                    act.wait_ge(y_gated.sem, y_gated.upto(li, n - 3))
                    to, of = (yc_hi, y_c[:, n % 4, :]) if n < 8 else (yb_hi, y_b[:, n % 4, :])
                nc.scalar.activation(to[:, n % 4, :], of, ACT.Copy).then_inc(y_hi.sem, 1)

            def layer(li):
                bl, ou, s = Blocks(li * (N_LAYER // 4)), Outs(li * (OUT_LAYER // 4)), li * 2

                def split(i):
                    act_split(act, bl, i + AHEAD)
                nc.scalar.preload_act_table_set(EXP_LN)
                act.wait_ge(par_done.sem, par_done.upto(li, 2))
                act_pre(act, s, par[:, G_MIX_PRE:G_MIX_PRE + KD])
                act.wait_ge(zeroed.sem, zeroed.upto(li, 5))
                nc.scalar.activation(ga_hi[:, :, 0:RANK], par[:, P_WGA:].rearrange("p (k n) -> p k n", k=KD),
                                     ACT.Copy).then_inc(ga_split.sem, 1)
                split(0)
                act_rsqrt(act, "pre0", li)
                act_rsqrt_tm(act, "tm0", li)
                for i in range(1, 8):
                    split(i)
                act.wait_ge(r_tm_done.sem, r_tm_done.upto(li, 1))
                values(bl, GV, ou, GV, g_v)
                for t in range(2):
                    act.wait_ge(z_abs.sem, z_abs.upto(li, t + 1))
                    nc.scalar.activation(z_a[t][:, :], z_a[t][:, :], ACT.Exp).then_inc(z_exp.sem, 1)
                for t in range(2):
                    act.wait_ge(z_exp.sem, z_exp.upto(li, t + 1))
                    nc.scalar.activation(z_a[t][:, :], z_a[t][:, :], ACT.Ln, bias=1.0).then_inc(z_ln.sem, 1)
                for i in range(12):
                    split(CV + i)
                    for u in conv_units(i):
                        level_exp(u, li)
                    if i == 11:
                        take_off(16, li)
                        take_off(17, li)
                    if i % 3 == 2:
                        y_high(i // 3, li)
                split(RQ)
                take_off(18, li)
                take_off(19, li)
                for i in range(1, 8):
                    split(RQ + i)
                    if i <= 4:
                        head_copy(i - 1, li)
                    if 2 <= i <= 5:
                        head_rsqrt(i - 2, li)
                for i in range(4):
                    split(RV + i)
                values(bl, RV, ou, RV, r_v)
                for h in range(HEADS):
                    split(GR + h)
                    gate_silu(h, ou, li)
                    if h >= 1:
                        head_copy(3 + h, li)
                    if h >= 2:
                        head_rsqrt(2 + h, li)
                split(RG)
                gate_silu(4, ou, li)
                head_copy(7, li)
                head_rsqrt(6, li)
                split(RG + 1)
                gate_silu(5, ou, li)
                head_rsqrt(7, li)
                for n in range(4, 9):
                    y_high(n, li)
                split(RG + 2)
                gate_silu(6, ou, li)
                y_high(9, li)
                split(RG + 3)
                gate_silu(7, ou, li)
                y_high(10, li)
                y_high(11, li)
                with act.Fori(0, GATE_TURNS) as j:
                    b, o = turn(bl.on(N_HEAD), ou.on(N_HEAD), j, N_GATE, N_GATE)
                    for i in range(N_GATE // 2):
                        act_split(act, b, 2 * i + AHEAD)
                        act.wait_ge(drained[o.bank(2 * i)], o.uses(2 * i) + 2)
                        nc.scalar.activation(gt[i % 2][:, :], gt[i % 2][:, :], ACT.Sigmoid).then_inc(sig.sem, 1)
                        act_split(act, b, 2 * i + 1 + AHEAD)
                        if i % 3 == 2:
                            m = i // 3
                            act.wait_ge(mac_add.sem, mac_add.upto(li, j * 4 + (2 * m + 2)))
                            act.wait_ge(consts_in, CONSTS)
                            nc.scalar.activation(mg_hi[:, one(j * 2 + m), :], flat(mac[m]), ACT.Copy).then_inc(mg_hi_ev.sem, 1)
                b, o = bl.on(N_HEAD + N_GATE * GATE_TURNS), ou.on(N_HEAD + N_GATE * GATE_TURNS)
                nc.scalar.preload_act_table_set(EXP_LN)
                for m in range(KD):
                    act_split(act, b, m + AHEAD)
                    act_out(act, s, m, o, m)
                act_rsqrt(act, "post0", li)
                act_ffn(act, s + 1, li, b.on(KD), o.on(KD), par[:, G_FFN_PRE:G_FFN_PRE + KD], "pre1", "post1", li)

            for i, to in ((0, ret_sin), (1, ret_cos)):
                act.wait_ge(trig_done, i + 1)
                nc.scalar.activation(to[:, :], ang[2 + i][:, :], ACT.Sin).then_inc(trig_tab, 1)
            for i in range(AHEAD):
                act_split(act, Blocks(0), i)
            with act.Fori(0, LAYERS) as li:
                layer(li)

            bl, ou = Blocks(LAYERS * (N_LAYER // 4)), Outs(LAYERS * (OUT_LAYER // 4))
            act_ffn(act, 4, 2, bl, ou, par2[:, H_F1PRE:H_F1PRE + KD], "pre2", "post2", half=True)
            bl, ou = bl.on(N_FFN), ou.on(OUT_FFN)
            act_pre(act, 5, par2[:, H_MPRE:H_MPRE + KD])

            def q_square(i):
                act.wait_ge(drained[ou.bank(i)], ou.uses(i) + 2)
                nc.scalar.activation(sq_h[i % 2][:, :], q_in[:, i % 3, :], ACT.Square).then_inc(q_sq.sem, 1)

            def q_rsqrt(i):
                use = side(f"qvar{i}")
                act.wait_ge(use.filled, use.n + 1)
                if i >= 1:
                    act.wait_ge(q_n.sem, q_n.upto(0, i))
                n = HD if i < 4 else 1
                nc.scalar.activation(q_r[:, :], use.mem[:, :], ACT.Ln, scale=n / HD, bias=n * EPS).then_inc(use.drained, 1)
                src = side(f"qvar{i}")
                act.wait_ge(src.drained, src.n + 2)
                nc.scalar.activation(q_r[:, :], q_r[:, :], ACT.Exp, scale=-0.5).then_inc(q_rr.sem, 1)

            for i in range(18):
                act_split(act, bl, i + AHEAD)
                if i == 0:
                    act_rsqrt(act, "pre3")
                    act_rsqrt_tm(act, "tm3")
                if i <= 4:
                    q_square(i)
                if i == 5:
                    act.wait_ge(r_tm_done.sem, r_tm_done.upto(LAYERS, 1))
                    use = result(ou, 5)
                    act.wait_ge(block_done, bl.n(5) + (RING + 1))
                    for t in range(TT):
                        last = nc.scalar.activation(a_v[:, t, :], use.mem[:, tok(t)], ACT.Copy, scale=r_tm[:, t:t + 1])
                    last.then_inc(use.drained, 1)
                if 1 <= i <= 5:
                    q_rsqrt(i - 1)
            values(bl, 14, ou, 14, d_v)
            for u in range(65):
                if u < 64:
                    e = N_QKV + u
                    act.wait_ge(maxed.sem, maxed.upto(0, u + 1))
                    if u >= 3:
                        old = side(f"pt{u - 3}")
                        act.wait_ge(old.filled, old.n + 1)
                    if u >= 4:
                        act.wait_ge(inv_done.sem, inv_done.upto(0, u - 3))
                    b = ou.bank(e)
                    nc.scalar.activation(prob[:, u % 3, :], ps[b][:, :], ACT.Exp, bias=row_max[:, u % 4:u % 4 + 1],
                                         accum_out=row_sum[:, u % 4:u % 4 + 1]).then_inc(drained[b], 1)
                if u >= 33:
                    v = u - 1
                    use = side(f"pt{v}")
                    act.wait_ge(use.filled, use.n + 1)
                    old = side(f"o{v - 2}")
                    act.wait_ge(old.filled, old.n + 1)
                    nc.scalar.activation(prob_t[:, v % 2, :], use.mem[:, :], ACT.Copy).then_inc(use.drained, 1)
            for k in range(KD):
                act.wait_ge(turned.sem, turned.upto(0, k + 1))
                nc.scalar.activation(u_hi[:, k, :], ps[ou.bank(N_QKV + 64 + k)][:, :], ACT.Copy).then_inc(hd_hi.sem, 1)
            for m in range(KD):
                act_split(act, bl, N_QKV + m + AHEAD)
                act_out(act, 5, m, ou, N_QKV + 64 + KD + m)
            act_rsqrt(act, "post3")
            act_ffn(act, 6, 3, bl.on(N_QKV + KD), ou.on(N_QKV + 64 + 2 * KD), par2[:, H_F2PRE:H_F2PRE + KD],
                    "pre4", "post4", half=True, last=True)

        @block.vector
        def _(dve):
            def exponents(u, li):
                lev, t = UNITS[u]
                cl, cr, mid = halves(g_cum[:, t, :], lev)
                el, er, _ = halves(lev_e[:, u % 2, :], lev)
                if t == 0:
                    dve.wait_ge(cum_done.sem, cum_done.upto(li, 2))
                if u >= 4:
                    dve.wait_ge(lev_qk.sem, lev_qk.upto(li, u - 3))
                nc.vector.tensor_tensor(er, cr, mid, ALU.subtract)
                nc.vector.tensor_tensor(el, mid, cl, ALU.subtract).then_inc(lev_d.sem, 1)

            def decayed(u, li):
                lev, t = UNITS[u]
                el, er, _ = halves(lev_e[:, u % 2, :], lev)
                dve.wait_ge(lev_x.sem, lev_x.upto(li, u - 1))
                if u >= 4:
                    for h in range(2):
                        old = side(f"gla{u - 2}{h}", li)
                        dve.wait_ge(old.filled, old.n + 1)
                nc.vector.tensor_tensor(halves(lev_q[:, u % 2, :], lev)[1], halves(g_q[:, t, :], lev)[1], er, ALU.mult)
                nc.vector.tensor_tensor(halves(lev_k[:, u % 2, :], lev)[0], halves(g_k[:, t, :], lev)[0], el, ALU.mult).then_inc(lev_qk.sem, 1)

            def select(u, li):
                lev, t = UNITS[u]
                if lev not in MASKED:
                    return
                mask = gla_masks[:, MASKED.index(lev), :].rearrange("p (o n) -> p o n", o=1).to_broadcast([P, TT, P])
                for h in range(2):
                    use = side(f"gla{u}{h}", li)
                    dve.wait_ge(use.filled, use.n + 1)
                    to = s_diag[:, 2 * t + h, :].rearrange("p (a n) -> p a n", a=TT)
                    of = use.mem[:, :].rearrange("p (a n) -> p a n", a=TT)
                    if lev == 1:
                        nc.vector.tensor_tensor(to, of, mask, ALU.mult).then_inc(use.drained, 1)
                    else:
                        nc.vector.memset(wait_cell[:, 2 * u + h:2 * u + h + 1], 0.0)
                        nc.vector.copy_predicated(to, mask.bitcast(U32), of).then_inc(use.drained, 1)

            def y_low(n, li):
                dve.wait_ge(y_hi.sem, y_hi.upto(li, n + 1))
                hi, lo, of = ((ya_hi, ya_lo, c_a[:, :]), (yc_hi, yc_lo, y_c[:, n % 4, :]), (yb_hi, yb_lo, y_b[:, n % 4, :]))[n // 4]
                nc.vector.tensor_tensor(lo[:, n % 4, :], of, hi[:, n % 4, :].bitcast(F32), ALU.subtract).then_inc(y_lo.sem, 1)

            def conv(i, bl, ou, li):
                c, part = i // 3, i % 3
                use = result(ou, CV + i)
                dve.wait_ge(block_done, bl.n(CV + i) + (RING + 1))
                if part == 0:
                    nc.vector.tensor_tensor(c_t[:, :], use.mem[:, :], r[:, :], ALU.mult).then_inc(use.drained, 1)
                    dve.wait_ge(drained[ou.bank(CV + i)], ou.uses(CV + i) + 2)
                    nc.vector.tensor_tensor(c_t[:, :], c_t[:, :], r[:, :], ALU.mult).then_inc(conv_t.sem, 1)
                elif part == 1:
                    dve.wait_ge(conv_t.sem, conv_t.upto(li, c + 1))
                    nc.vector.tensor_tensor(c_z[:, 2:], use.mem[:, :], c_t[:, :], ALU.mult).then_inc(use.drained, 1)
                    dve.wait_ge(drained[ou.bank(CV + i)], ou.uses(CV + i) + 2)
                    if c == 0:
                        dve.wait_ge(zeroed.sem, zeroed.upto(li, 5))
                    for w in range(3):
                        gain = par[:, P_CONV + 4 * w + c:P_CONV + 4 * w + c + 1]
                        if w == 0:
                            nc.vector.tensor_scalar(c_a[:, :], c_z[:, 0:T], gain, None, ALU.mult).then_inc(conv_a.sem, 1)
                        else:
                            dve.wait_ge(conv_a.sem, conv_a.upto(li, 3 * c + w))
                            nc.vector.scalar_tensor_tensor(c_a[:, :], c_z[:, w:w + T], gain, c_a[:, :], ALU.mult, ALU.add).then_inc(conv_a.sem, 1)
                else:
                    nc.vector.tensor_tensor(c_b[:, :], use.mem[:, :], r[:, :], ALU.mult).then_inc(use.drained, 1)
                    dve.wait_ge(drained[ou.bank(CV + i)], ou.uses(CV + i) + 2)
                    dve.wait_ge(conv_a.sem, conv_a.upto(li, 3 * c + 3))
                    nc.vector.tensor_tensor(c_a[:, :], c_a[:, :], c_b[:, :], ALU.mult).then_inc(conv_y.sem, 1)

            def rotated(i, li):
                use = side(f"rot{i}", li)
                dve.wait_ge(use.filled, use.n + 1)
                if i >= 2:
                    dve.wait_ge(rot_y.sem, rot_y.upto(li, i - 1))
                nc.vector.tensor_tensor(rot_s[:, i % 2, :], use.mem[:, :], ret_sin[:, :], ALU.mult).then_inc(use.drained, 1)

            def head_norm(n, li):
                y = (y_c if n < 4 else y_b)[:, n % 4, :]
                gain = (P_GLAGN if n < 4 else P_RETGN) + n % 4
                dve.wait_ge(hn_rr.sem, hn_rr.upto(li, n + 1))
                nc.vector.scalar_tensor_tensor(y, y, par[:, gain:gain + 1], hn_r[:, n % 2, :], ALU.mult, ALU.mult).then_inc(hn_y.sem, 1)

            def gate_in(g, bl, ou, li):
                use = result(ou, GR + g)
                dve.wait_ge(block_done, bl.n(GR + g) + (RING + 1))
                if g >= 2:
                    dve.wait_ge(y_gated.sem, y_gated.upto(li, g - 1))
                nc.vector.tensor_tensor(tgate[g % 2][:, :], use.mem[:, :], r[:, :], ALU.mult).then_inc(use.drained, 1)

            def gated(g, li):
                y = (y_c if g < 4 else y_b)[:, g % 4, :]
                dve.wait_ge(hn_y.sem, hn_y.upto(li, g + 1))
                dve.wait_ge(silu_g.sem, silu_g.upto(li, g + 1))
                nc.vector.tensor_tensor(y, y, tgate[g % 2][:, :], ALU.mult).then_inc(y_gated.sem, 1)

            def ret_decay(h, li):
                s, mask = s_ret[:, h % 2, :], ret_mask[:, h, :]
                if h == 0:
                    dve.wait_ge(masks_in, li * 16 + 16)
                if h >= 2:
                    old = side(f"out{2 + h}", li)
                    dve.wait_ge(old.filled, old.n + 1)
                use = side(f"s{h}0", li)
                dve.wait_ge(use.filled, use.n + 1)
                nc.vector.tensor_tensor(s[:, 0:512], use.mem[:, :], mask, ALU.mult).then_inc(use.drained, 1)
                use = side(f"s{h}1", li)
                dve.wait_ge(use.filled, use.n + 1)
                nc.vector.tensor_tensor(s[:, 512:896], use.mem[:, 0:384], mask[:, 0:384], ALU.mult)
                nc.vector.tensor_tensor(s[:, 1152:1280], use.mem[:, 384:512], mask[:, 0:128], ALU.mult).then_inc(use.drained, 1)
                use = side(f"s{h}2", li)
                dve.wait_ge(use.filled, use.n + 1)
                nc.vector.tensor_tensor(s[:, 896:1152], use.mem[:, 0:256], mask[:, 0:256], ALU.mult).then_inc(use.drained, 1)

            def layer(li):
                bl, ou, s = Blocks(li * (N_LAYER // 4)), Outs(li * (OUT_LAYER // 4)), li * 2

                def split(i):
                    dve_split(dve, bl, i + AHEAD)
                nc.vector.tensor_copy(flat(par), par_all[:, one(li), :]).then_inc(par_done.sem, 1)
                nc.vector.tensor_copy(flat(wa2), wa2_all[:, one(li), :]).then_inc(par_done.sem, 1)
                dve.wait_ge(par_done.sem, par_done.upto(li, 2))
                dve_pre(dve, s, par[:, G_MIX_PRE:G_MIX_PRE + KD])
                dve.wait_ge(ga_split.sem, ga_split.upto(li, 1))
                nc.vector.tensor_tensor(ga_lo[:, :, 0:RANK], par[:, P_WGA:].rearrange("p (k n) -> p k n", k=KD),
                                        ga_hi[:, :, 0:RANK].bitcast(F32), ALU.subtract).then_inc(ga_split.sem, 1)
                for i in range(4):
                    split(i)
                    if i == 0:
                        dve.wait_ge(r_done.sem, r_done.upto(s, 1))
                    use = result(ou, i)
                    dve.wait_ge(block_done, bl.n(i) + (RING + 1))
                    if i < 2:
                        nc.vector.scalar_tensor_tensor(g_q[:, i, :], use.mem[:, :], HD ** -0.5, r[:, :], ALU.mult, ALU.mult).then_inc(use.drained, 1)
                    else:
                        nc.vector.tensor_tensor(g_k[:, i - 2, :], use.mem[:, :], r[:, :], ALU.mult).then_inc(use.drained, 1)
                split(4)
                use = side("ga", li)
                dve.wait_ge(use.filled, use.n + 1)
                nc.vector.tensor_tensor(ga_t[:, :], use.mem[0:RANK, :], r[0:RANK, :], ALU.mult).then_inc(use.drained, 1)
                for i in range(5, 8):
                    split(i)
                for t in range(2):
                    use = side(f"z{t}", li)
                    dve.wait_ge(use.filled, use.n + 1)
                    nc.vector.tensor_scalar(z_b[:, t, :], use.mem[:, :], par[:, P_BA + t:P_BA + t + 1], None, ALU.add).then_inc(use.drained, 1)
                for t in range(2):
                    src = side(f"z{t}", li)
                    dve.wait_ge(src.drained, src.n + 2)
                    nc.vector.scalar_tensor_tensor(z_a[t][:, :], z_b[:, t, :], -1.0, z_b[:, t, :], ALU.mult, ALU.min).then_inc(z_abs.sem, 1)
                select(0, li)
                select(1, li)
                for t in range(2):
                    dve.wait_ge(z_ln.sem, z_ln.upto(li, t + 1))
                    nc.vector.scalar_tensor_tensor(z_b[:, t, :], z_b[:, t, :], 0.0, z_a[t][:, :], ALU.min, ALU.subtract).then_inc(z_log.sem, 1)
                for t in range(2):
                    dve.wait_ge(z_log.sem, z_log.upto(li, t + 1))
                    nc.vector.tensor_tensor_scan(g_cum[:, t, :], ones_c[:, 0:1].to_broadcast([P, T]), z_b[:, t, :], 0.0,
                                                 ALU.mult, ALU.add).then_inc(cum_done.sem, 1)
                dve.wait_ge(zeroed.sem, zeroed.upto(li, 5))
                for i in range(12):
                    for u in conv_units(i):
                        exponents(u, li)
                    split(CV + i)
                    if i % 3 == 0 and i > 0:
                        y_low(i // 3 - 1, li)
                    conv(i, bl, ou, li)
                    for u in conv_units(i - 1):
                        select(u, li)
                    for u in conv_units(i):
                        decayed(u, li)
                for i in range(8):
                    split(RQ + i)
                    if i == 0:
                        y_low(3, li)
                    if i >= 2:
                        dve.wait_ge(rot_c.sem, rot_c.upto(li, i - 1))
                    use = result(ou, RQ + i)
                    dve.wait_ge(block_done, bl.n(RQ + i) + (RING + 1))
                    if i < 4:
                        nc.vector.scalar_tensor_tensor(rot_in[:, i % 2, :], use.mem[:, :], P ** -0.5, r[:, :], ALU.mult, ALU.mult).then_inc(use.drained, 1)
                    else:
                        nc.vector.tensor_tensor(rot_in[:, i % 2, :], use.mem[:, :], r[:, :], ALU.mult).then_inc(use.drained, 1)
                    if i >= 1:
                        rotated(i - 1, li)
                    if 3 <= i <= 6:
                        head_norm(i - 3, li)
                for i in range(4):
                    split(RV + i)
                    if i == 0:
                        pass
                rotated(7, li)
                for t in range(TT):
                    dve.wait_ge(drained[ou.bank(RV + t)], ou.uses(RV + t) + 2)
                    nc.vector.tensor_reduce(v_sum[:, t, :], r_v[:, t, :].rearrange("p (h n) -> p h n", h=HEADS),
                                            AX.X, ALU.add).then_inc(rv_sum.sem, 1)
                for t in range(TT):
                    dve.wait_ge(rv_sum.sem, rv_sum.upto(li, t + 1))
                    v = r_v[:, t, :].rearrange("p (h n) -> p h n", h=HEADS)
                    mean = v_sum[:, t, :].rearrange("p (h o) -> p h o", o=1).to_broadcast([P, HEADS, P])
                    nc.vector.scalar_tensor_tensor(v, mean, -1.0 / P, v, ALU.mult, ALU.add).then_inc(rv_cent.sem, 1)
                for h in range(HEADS):
                    split(GR + h)
                    gate_in(h, bl, ou, li)
                    ret_decay(h, li)
                    gated(h, li)
                    if h == 3:
                        head_norm(4, li)
                split(RG)
                gate_in(4, bl, ou, li)
                head_norm(5, li)
                gated(4, li)
                split(RG + 1)
                gate_in(5, bl, ou, li)
                head_norm(6, li)
                gated(5, li)
                for n in range(4, 9):
                    y_low(n, li)
                split(RG + 2)
                gate_in(6, bl, ou, li)
                head_norm(7, li)
                gated(6, li)
                y_low(9, li)
                split(RG + 3)
                gate_in(7, bl, ou, li)
                gated(7, li)
                y_low(10, li)
                y_low(11, li)
                with dve.Fori(0, GATE_TURNS) as j:
                    b, o = turn(bl.on(N_HEAD), ou.on(N_HEAD), j, N_GATE, N_GATE)
                    for i in range(N_GATE // 2):
                        m, branch = i // 3, i % 3
                        dve_split(dve, b, 2 * i + AHEAD)
                        use = result(o, 2 * i)
                        dve.wait_ge(block_done, b.n(2 * i) + (RING + 1))
                        nc.vector.tensor_tensor(gt[i % 2][:, :], use.mem[:, :], r[:, :], ALU.mult).then_inc(use.drained, 1)
                        dve_split(dve, b, 2 * i + 1 + AHEAD)
                        use = result(o, 2 * i + 1)
                        dve.wait_ge(block_done, b.n(2 * i + 1) + (RING + 1))
                        dve.wait_ge(sig.sem, sig.upto(li, j * 6 + (i + 1)))
                        to = mac[m] if branch == 0 else br
                        nc.vector.tensor_tensor(to[:, :], use.mem[:, :], gt[i % 2][:, :], ALU.mult).then_inc(use.drained, 1)
                        if branch > 0:
                            dve.wait_ge(drained[o.bank(2 * i + 1)], o.uses(2 * i + 1) + 2)
                            if branch == 2:
                                dve.wait_ge(mac_add.sem, mac_add.upto(li, j * 4 + (2 * m + 1)))
                            nc.vector.tensor_tensor(mac[m][:, :], mac[m][:, :], br[:, :], ALU.add).then_inc(mac_add.sem, 1)
                        if branch == 2:
                            dve.wait_ge(mg_hi_ev.sem, mg_hi_ev.upto(li, j * 2 + (m + 1)))
                            nc.vector.tensor_tensor(mg_lo[:, one(j * 2 + m), :], flat(mac[m]),
                                                    mg_hi[:, one(j * 2 + m), :].bitcast(F32), ALU.subtract).then_inc(mg_lo_ev.sem, 1)
                b, o = bl.on(N_HEAD + N_GATE * GATE_TURNS), ou.on(N_HEAD + N_GATE * GATE_TURNS)
                for m in range(KD):
                    dve_split(dve, b, m + AHEAD)
                    dve_out(dve, b, m, o, m, mix_out[:, m, :])
                    if m >= 2:
                        dve_out_acc(dve, s, m - 1, o, m - 1)
                dve_out_acc(dve, s, KD - 1, o, KD - 1)
                dve_post(dve, s, par[:, G_MIX_POST:G_MIX_POST + KD], mix_out)
                dve_ffn(dve, s + 1, li, b.on(KD), o.on(KD), par[:, G_FFN_PRE:G_FFN_PRE + KD], par[:, G_FFN_POST:G_FFN_POST + KD])
                dve.wait_ge(t_done.sem, t_done.upto(s + 1, KD))
                nc.vector.memset(wait_cell[:, 0:1], 0.0)

            dve.wait_ge(consts_in, CONSTS)
            steps = [0]

            def step(ins):
                ins.then_inc(ang_step, 1)
                steps[0] += 1
                dve.wait_ge(ang_step, steps[0])
            magic = 1.5 * 2 ** 23
            two_pi = [201 / 32]
            two_pi.append(float(np.float32(round((2 * math.pi - two_pi[0]) * 2 ** 20) / 2 ** 20)))
            two_pi.append(2 * math.pi - two_pi[0] - two_pi[1])
            step(nc.vector.tensor_copy(ang[0][:, :], pos_i[:, :]))
            step(nc.vector.tensor_scalar(ang[0][:, :], ang[0][:, :], inv_freq[:, 0:1], None, ALU.mult))
            for i, shift in ((0, 0.0), (1, 0.25)):
                to = ang[2 + i]
                step(nc.vector.tensor_scalar(ang[1][:, :], ang[0][:, :], 1 / (2 * math.pi), shift, ALU.mult, ALU.add))
                step(nc.vector.tensor_scalar(ang[1][:, :], ang[1][:, :], magic, None, ALU.add))
                step(nc.vector.tensor_scalar(ang[1][:, :], ang[1][:, :], magic, None, ALU.subtract))
                for n, part in enumerate(two_pi):
                    of = ang[0] if n == 0 else to
                    step(nc.vector.scalar_tensor_tensor(to[:, :], ang[1][:, :], -part, of[:, :], ALU.mult, ALU.add))
                step(nc.vector.tensor_scalar(to[:, :], to[:, :], shift * 2 * math.pi, 3.1415925, ALU.add, ALU.min))
                nc.vector.tensor_scalar(to[:, :], to[:, :], -3.1415925, None, ALU.max).then_inc(trig_done, 1)
            for i in range(AHEAD):
                dve_split(dve, Blocks(0), i)
            dve.wait_ge(trig_tab, 2)
            with dve.Fori(0, LAYERS) as li:
                layer(li)

            bl, ou = Blocks(LAYERS * (N_LAYER // 4)), Outs(LAYERS * (OUT_LAYER // 4))
            dve_ffn(dve, 4, 2, bl, ou, par2[:, H_F1PRE:H_F1PRE + KD], par2[:, H_F1POST:H_F1POST + KD])
            bl, ou = bl.on(N_FFN), ou.on(OUT_FFN)
            dve_pre(dve, 5, par2[:, H_MPRE:H_MPRE + KD])

            def q_norm(i):
                gain = H_QN if i < 4 else H_KN
                dve.wait_ge(q_rr.sem, q_rr.upto(0, i + 1))
                nc.vector.scalar_tensor_tensor(q_in[:, i % 3, :], q_in[:, i % 3, :], par2[:, gain:gain + 1], q_r[:, :],
                                               ALU.mult, ALU.mult).then_inc(q_n.sem, 1)

            def roped(i):
                _, _, tab, _ = rope_tile(i)
                use = side(f"rope{i}")
                dve.wait_ge(use.filled, use.n + 1)
                if i >= 2:
                    dve.wait_ge(rope_y.sem, rope_y.upto(0, i - 1))
                if i == 0:
                    dve.wait_ge(tables_in, 32)
                nc.vector.tensor_tensor(q_s[:, i % 2, :], use.mem[:, :], rope_tab[:, tab + 1, :], ALU.mult).then_inc(use.drained, 1)

            dve.wait_ge(r_done.sem, r_done.upto(5, 1))
            for i in range(18):
                dve_split(dve, bl, i + AHEAD)
                tile = i if i < 5 else i - 1
                if i != 5 and i < 14:
                    use = result(ou, i)
                    dve.wait_ge(block_done, bl.n(i) + (RING + 1))
                    if tile >= 3:
                        dve.wait_ge(rope_c.sem, rope_c.upto(0, tile - 2))
                    to = q_in[:, tile % 3, :]
                    if 6 <= i < 10:
                        nc.vector.scalar_tensor_tensor(to, use.mem[:, :], HD ** -0.5, r[:, :], ALU.mult, ALU.mult).then_inc(use.drained, 1)
                    else:
                        nc.vector.tensor_tensor(to, use.mem[:, :], r[:, :], ALU.mult).then_inc(use.drained, 1)
                if 1 <= i <= 5:
                    q_norm(i - 1)
                if 2 <= i < 14:
                    roped(i - 2)
            roped(12)

            def row_maximum(u):
                dense, t, h, it, _ = attention_unit(u)
                scores = ps[ou.bank(N_QKV + u)]
                dve.wait_ge(scored.sem, scored.upto(0, u + 1))
                if not dense:
                    nc.vector.tensor_tensor(scores[:, :], scores[:, :], bias[:, it, :], ALU.add).then_inc(biased.sem, 1)
                    dve.wait_ge(biased.sem, biased.upto(0, u - 31))
                nc.vector.tensor_reduce(row_max[:, u % 4:u % 4 + 1], scores[:, :], AX.X, ALU.max, negate=True).then_inc(maxed.sem, 1)

            for u in range(67):
                if u < 64:
                    row_maximum(u)
                v = u - 2
                if 0 <= v < 64:
                    dve.wait_ge(drained[ou.bank(N_QKV + v)], ou.uses(N_QKV + v) + 2)
                    nc.vector.reciprocal(row_inv[:, v % 4:v % 4 + 1], row_sum[:, v % 4:v % 4 + 1]).then_inc(inv_done.sem, 1)
                if 0 <= v < 32:
                    use = side(f"pt{v}")
                    dve.wait_ge(use.filled, use.n + 1)
                    if v >= 2:
                        old = side(f"o{v - 2}")
                        dve.wait_ge(old.filled, old.n + 1)
                    nc.vector.tensor_copy(prob_t[:, v % 2, :], use.mem[:, :]).then_inc(use.drained, 1)
                v = u - 3
                if v >= 0:
                    _, _, _, it, col = attention_unit(v)
                    use = side(f"o{v}")
                    dve.wait_ge(use.filled, use.n + 1)
                    dve.wait_ge(inv_done.sem, inv_done.upto(0, v + 1))
                    nc.vector.tensor_scalar(heads[:, it, col:col + HD], use.mem[:, 0:HD], row_inv[:, v % 4:v % 4 + 1], None,
                                            ALU.mult).then_inc(use.drained, 1)
            for k in range(KD):
                b = ou.bank(N_QKV + 64 + k)
                dve.wait_ge(hd_hi.sem, hd_hi.upto(0, k + 1))
                nc.vector.tensor_tensor(u_lo[:, k, :], ps[b][:, :], u_hi[:, k, :].bitcast(F32), ALU.subtract).then_inc(drained[b], 1)
            for m in range(KD):
                e = N_QKV + 64 + KD + m
                dve_split(dve, bl, N_QKV + m + AHEAD)
                dve_out(dve, bl, N_QKV + m, ou, e, mix_out[:, m, :])
                if m >= 2:
                    dve_out_acc(dve, 5, m - 1, ou, e - 1)
            dve_out_acc(dve, 5, KD - 1, ou, N_QKV + 64 + 2 * KD - 1)
            dve_post(dve, 5, par2[:, H_MPOST:H_MPOST + KD], mix_out)
            dve_ffn(dve, 6, 3, bl.on(N_QKV + KD), ou.on(N_QKV + 64 + 2 * KD), par2[:, H_F2PRE:H_F2PRE + KD],
                    par2[:, H_F2POST:H_F2POST + KD], last=True)


def tile_columns(w, c):
    k = w.shape[0] // P
    return w[:, c:c + P].reshape(k, P, P).transpose(1, 0, 2).reshape(P, k * P)


def value_columns(w, c):
    return w[:, c:c + T].reshape(KD, P, T).transpose(1, 0, 2).reshape(P, KD * T)


def ffn_blocks(gate, up, down):
    out = []
    for f in range(FT):
        out += [tile_columns(gate, f * P), tile_columns(up, f * P)]
    return out + [tile_columns(down, m * P) for m in range(KD)]


def weight_stream(a):
    out = []
    for li in range(LAYERS):
        w = a["w_in"][li]
        out += [tile_columns(w, 3584 + i * P) for i in range(4)]
        out += [value_columns(w, 4096)]
        for c in range(4):
            out += [tile_columns(w, at + c * P) for at in (0, 1024, 512)]
        out += [tile_columns(w, 1536 + i * P) for i in range(8)]
        out += [value_columns(w, 2560)]
        out += [tile_columns(w, 4608 + i * P) for i in range(4)]
        out += [tile_columns(w, 3072 + i * P) for i in range(4)]
        for m in range(KD):
            for at, name in ((5136, "w_branch_a"), (7184, "w_branch_c"), (6160, "w_branch_b")):
                out += [tile_columns(w, at + m * P), tile_columns(a[name][li], m * P)]
        out += [tile_columns(a["w_out"][li], m * P) for m in range(KD)]
        out += ffn_blocks(a["w_ffn_gate"][li], a["w_ffn_up"][li], a["w_ffn_down"][li])
    out += ffn_blocks(a["ffn1_w_gate_2"][0], a["ffn1_w_up_2"][0], a["ffn1_w_down_2"][0])
    w = a["w_qkv_2"][0]
    for t in range(4):
        out += [tile_columns(np.concatenate([w[:, t * HD:(t + 1) * HD], w[:, (t + 4) * HD:(t + 5) * HD]], axis=1), 0)]
    out += [tile_columns(w, 512 + i * P) for i in range(10)]
    out += [value_columns(w, 1792)]
    out += [tile_columns(a["w_out_2"][0], m * P) for m in range(KD)]
    out += ffn_blocks(a["ffn2_w_gate_2"][0], a["ffn2_w_up_2"][0], a["ffn2_w_down_2"][0])
    return np.concatenate(out, axis=1)


def per_partition(v):
    return v.reshape(-1, P).T


def layer_parameters(a):
    out = []
    for li in range(LAYERS):
        cols = [per_partition(a[n][li]) for n in ("norm_mix_pre", "norm_mix_post", "norm_ffn_pre", "norm_ffn_post")]
        cols += [per_partition(a["conv_w"][li][w]) for w in range(3)]
        cols += [per_partition(a[n][li]) for n in ("ret_gn_w", "gla_gn_w", "gla_b_a")]
        cols += [a["w_in"][li][:, 5120:5120 + RANK].reshape(KD, P, RANK).transpose(1, 0, 2).reshape(P, KD * RANK)]
        out.append(np.concatenate(cols, axis=1))
    return np.stack(out, axis=1)


def second_gains(a):
    cols = [per_partition(a[n + "_2"][0]) for n in ("ffn1_pre_g", "ffn1_post_g", "mix_pre_g", "mix_post_g", "ffn2_pre_g", "ffn2_post_g")]
    cols += [np.concatenate([a[n + "_2"][0]] * 2).reshape(P, 1) for n in ("q_norm_g", "k_norm_g")]
    return np.concatenate(cols, axis=1)


def rotation(width):
    m = np.zeros((P, P), np.float32)
    h = width // 2
    for d in range(P):
        if d % width < h:
            m[d + h, d] = -1
        else:
            m[d - h, d] = 1
    return m


def constants():
    f = np.float32
    i, j = np.arange(P)[None, :], np.arange(P)[:, None]
    squares = [np.ones((P, P), f), np.eye(P, dtype=f), (i // HD == j // HD).astype(f), rotation(128), rotation(64), rotation(32)]
    masks = []
    for lev in MASKED:
        if lev == 1:
            masks.append((i == j).astype(f))
        else:
            masks.append(((i // lev == j // lev) & (j % lev < lev // 2) & (i % lev >= lev // 2)).astype(f))
    c = np.arange(T)[None, :] - np.arange(P)[:, None]
    log_g = np.log(1.0 - 2.0 ** (-5.0 - np.arange(HEADS)))
    decay = [np.where(c >= 0, np.exp(lg * np.maximum(c, 0)), 0.0).astype(f) for lg in log_g]
    inv = np.power(f(10000.0), -np.arange(HD, dtype=f) / f(HD)).astype(f)
    t = np.arange(T)

    def angles(pos, dim):
        freqs = np.power(f(10000.0), -np.arange(0, dim, 2, dtype=f) / f(dim)).astype(f)
        return pos.astype(f)[:, None] * freqs[None, :]
    row, col, seq = angles(t // 64, HD // 2), angles(t % 64, HD // 2), angles(t, HD)
    axial = np.concatenate([row, row, col, col] * 2, axis=1).T
    along = np.concatenate([seq, seq] * 2, axis=1).T
    tables = [g(x).astype(f) for x in (axial, along) for g in (np.cos, np.sin)]
    d = t[None, :] - t[:, None]
    times = sum(((d % dil == 0) & (np.abs(d // dil) <= win // 2 // dil)).astype(int) for win, dil in ((128, 1), (512, 4), (2048, 16)))
    bias = np.where(times > 0, np.log(np.maximum(times, 1)), NEG).astype(f)
    return {
        "sq_consts": np.stack(squares, axis=1), "gla_masks": np.stack(masks, axis=1), "ret_mask": np.stack(decay, axis=1),
        "inv_freq": np.concatenate([inv, inv]).reshape(P, 1), "rope_tab": np.stack(tables, axis=1),
        "bias": bias.reshape(TT, P, T).transpose(1, 0, 2),
    }


def kernel(**inputs):
    import concourse.bacc as bacc
    from concourse.bass_utils import run_bass_kernel_spmd

    a = {k: np.asarray(v) for k, v in inputs.items()}
    arrays = {
        "x": a["x"][0].T.reshape(KD, P, T).transpose(1, 0, 2),
        "positions": a["positions"].reshape(1, T),
        "weights": weight_stream(a),
        "par_all": layer_parameters(a),
        "par2": second_gains(a),
        "wa2": a["gla_w_a2"].transpose(1, 0, 2),
    }
    arrays.update(constants())
    arrays = {k: np.ascontiguousarray(v) for k, v in arrays.items()}
    nc = bacc.Bacc("TRN2", target_bir_lowering=False, num_devices=1)
    dram = {k: nc.dram_tensor(f"in_{k}", v.shape, mybir.dt.from_np(v.dtype), kind="ExternalInput").ap() for k, v in arrays.items()}
    dram["out"] = nc.dram_tensor("out", (P, KD, T), F32, kind="ExternalOutput").ap()
    build(nc, dram)
    result = run_bass_kernel_spmd(nc, [{f"in_{k}": v for k, v in arrays.items()}], core_ids=[0])
    y = result.results[0]["out"]
    return y.transpose(2, 1, 0).reshape(1, T, D)
```

```python
import math
from contextlib import ExitStack

import numpy as np

import concourse.bass as bass
from concourse import mybir

F32 = mybir.dt.float32
F32R = mybir.dt.float32r
I32 = mybir.dt.int32
U32 = mybir.dt.uint32
ACT = mybir.ActivationFunctionType
ALU = mybir.AluOpType
AX = mybir.AxisListType
CONSTS = 16 * 4
EXP_LN = "natural_log_exp_and_others"

P = 128
T = 512
TT = T // P
D = 1024
KD = D // P
LAYERS = 2
EPS = 1e-6
CONV, RET, GKEY, GVAL, RANK = 512, 512, 256, 512, 16
HEADS = 4
DFF = 2816
FT = DFF // P
HD = 64
NEG = -1e30
LEVELS = (1, 128, 64, 32, 16, 8, 4, 2, 256, 512)
MASKED = LEVELS[1:8]
HALF = P // 2
LAST_DVE = (2, 4, 7)
Q_IN = 6
Q_S = 4
WARM = 5
X_PARTS = 4
UNITS = [(lev, t) for lev in LEVELS for t in range(2)]

BLK = 1024
RING = 4
RAW = 2
AHEAD = RING - 1
N_HEAD = 40
N_GATE = 12
GATE_TURNS = KD // 2
N_UP = 4
UP_TURNS = FT // 2
N_DOWN = 12
DOWN_TURNS = 2
DOWN_K = (8, 8, 6)
N_FFN = N_UP * UP_TURNS + N_DOWN * DOWN_TURNS
N_LAYER = N_HEAD + N_GATE * GATE_TURNS + KD + N_FFN
N_QKV = 18
COLS_GATE = 2 * 3 * (BLK + BLK // 2)
COLS_DOWN = 4 * FT * P
COLS_FFN = UP_TURNS * N_UP * BLK + DOWN_TURNS * COLS_DOWN
COLS_LAYER = N_HEAD * BLK + GATE_TURNS * COLS_GATE + KD * BLK + COLS_FFN
COLS = LAYERS * COLS_LAYER + 2 * COLS_FFN + (N_QKV + KD) * BLK
OUT_FFN = N_UP * UP_TURNS + 4 * DOWN_TURNS
OUT_LAYER = N_HEAD + N_GATE * GATE_TURNS + KD + OUT_FFN

G_NEXT, G_MIX_POST, G_FFN_PRE, G_FFN_POST = 0, 8, 16, 24
P_CONV, P_RETGN, P_GLAGN, P_BA, P_WGA = 32, 44, 48, 52, 54
N_PAR = P_WGA + KD * RANK
H_FIRST, H_F1POST, H_MPRE, H_MPOST, H_F2PRE, H_F2POST, H_QN, H_KN = 0, 8, 16, 24, 32, 40, 48, 49
N_PAR2 = 50
C_ONES, C_IDENT, C_BD64 = range(3)
N_SQ = 3


def level_keys(u):
    return [f"gla{u}{i}" for i in range(2 if UNITS[u][0] in (1, 512) else 1)]


class Blocks:

    def __init__(self, quads, s=0):
        self.quads, self.s = quads, s

    def n(self, p):
        return self.quads * 4 + (self.s + p)

    def slot(self, p):
        return (self.s + p) % RING

    def raw(self, p):
        return (self.s + p) % RAW

    def raw_uses(self, p):
        return self.quads * 2 + (self.s + p) // RAW

    def on(self, p):
        return Blocks(self.quads, self.s + p)


class Outs:

    def __init__(self, quads, s=0):
        self.quads, self.s = quads, s

    def bank(self, e):
        return (self.s + e) % 4

    def uses(self, e):
        return self.quads + (self.s + e) // 4

    def on(self, e):
        return Outs(self.quads, self.s + e)


class Event:

    def __init__(self, sem, per, credit=0):
        self.sem, self.per, self.credit = sem, per, credit

    def upto(self, inst, n):
        return inst * self.per + (self.credit + n)


class Use:

    def __init__(self, mem, drained, filled, n):
        self.mem, self.drained, self.filled, self.n = mem, drained, filled, n


def side_banks():
    layer = [("pre0", 7), ("tm0", 6), ("ga", 4), ("z0", 5), ("z1", 6)]
    layer += [(key, 4 + i % 4) for i, key in enumerate(k for u in range(len(UNITS)) for k in level_keys(u))]
    layer += [("out0", 7), ("out1", 7), ("out2", 7), ("var0", 6), ("out3", 7), ("var1", 6), ("var2", 6), ("var3", 6)]
    for h in range(HEADS):
        layer += [(f"s{h}0", 4), (f"s{h}1", 5), (f"s{h}2", 6)]
        if h >= 1:
            layer += [(f"out{3 + h}", 7)]
        if h >= 2:
            layer += [(f"var{2 + h}", 6)]
    layer += [("out7", 7), ("var6", 6), ("var7", 6), ("post0", 7), ("pre1", 7), ("post1", 7)]
    second = [("pre2", 7), ("post2", 7), ("pre3", 7), ("tm3", 6)]
    second += [(f"qvar{i}", 6) for i in range(5)]
    second += [(f"pt{u}", 4 + u % 2) for u in range(64)] + [(f"o{u}", 6 + u % 2) for u in range(64)]
    second += [("post3", 7), ("pre4", 7), ("post4", 7)]
    table, used = {}, [0] * 8
    for key, b in layer:
        table[key] = (b, used[b])
        used[b] += 1
    per = list(used)
    used = [LAYERS * n for n in per]
    for key, b in second:
        table[key] = (b, used[b])
        used[b] += 1
    return table, per


def build(nc, dram):
    ctx = ExitStack()
    with ctx:
        top = [(nc.sbuf_base + 127) // 128 * 128]

        def place(name, shape, dt=F32, offset=None):
            size = 4 * math.prod(shape[1:])
            if offset is None:
                offset = top[0]
                top[0] += (size + 31) // 32 * 32
                assert top[0] <= nc.sbuf_usable_end, name
            return nc.alloc_sbuf_tensor_at(name, shape, dt, offset=offset)

        x = place("x", [P, KD, T])
        u_hi_at = top[0]
        u_hi = place("u_hi", [P, KD, T], F32R)
        u_lo = place("u_lo", [P, KD, T], F32R)
        raw = place("raw", [P, RAW, BLK])
        w_hi = place("w_hi", [P, RING, BLK], F32R)
        w_lo = place("w_lo", [P, RING, BLK], F32R)
        sq_consts = place("sq_consts", [P, N_SQ, P])
        gla_masks = place("gla_masks", [P, len(MASKED), HALF])
        ret_cos = place("ret_cos", [P, T])
        ret_sin = place("ret_sin", [P, T])
        r = place("r", [P, T])
        r_tm = place("r_tm", [P, TT])
        acc = place("acc", [P, T])
        par_all = place("par_all", [P, LAYERS, N_PAR])
        par = place("par", [P, N_PAR])
        par2 = place("par2", [P, N_PAR2])
        inv_freq = place("inv_freq", [P, 1])
        wa2_all = place("wa2_all", [2 * RANK, LAYERS, GKEY])
        wa2 = place("wa2", [2 * RANK, GKEY])
        v_sum = place("v_sum", [P, TT, HEADS])
        row_max = place("row_max", [P, 4])
        row_sum = place("row_sum", [P, 4])
        row_inv = place("row_inv", [P, 4])
        wait_cell = place("wait_cell", [P, 2 * len(UNITS)])
        scratch_at = top[0]
        S = [place(f"scratch{i}", [P, T]) for i in range(5)]
        arena = top[0]
        KB = 1024
        place("arena", [P, 88 * KB // 4])

        def region(name, shape, kb, dt=F32):
            assert kb * KB + 4 * math.prod(shape[1:]) <= 88 * KB, name
            return place(name, shape, dt, arena + int(kb * KB))

        sq_x = region("sq_x", [P, KD, T], 0)
        mix_out = region("mix_out", [P, KD, T], 0)
        ffn_out = place("ffn_out", [P, KD, T], F32, u_hi_at)
        ya_hi = region("ya_hi", [P, 4, T], 0, F32R)
        ya_lo = region("ya_lo", [P, 4, T], 8, F32R)
        ga_w = region("ga_w", [P, KD, P], 16, F32R)
        s_diag = region("s_diag", [P, HEADS, T], 16)
        s_off = region("s_off", [P, HEADS, 768], 24)
        g_v = region("g_v", [P, TT, GVAL], 36)
        ga_t = region("ga_t", [2 * RANK, T], 44)
        hn_r = region("hn_r", [P, 2, T], 44)
        g_cum = region("g_cum", [P, 2, T], 48)
        g_q = region("g_q", [P, 2, T], 52)
        g_k = region("g_k", [P, 2, T], 56)
        lev_e = region("lev_e", [P, 2, T], 60)
        lev_q = region("lev_q", [P, 2, T], 64)
        lev_k = region("lev_k", [P, 2, T], 68)
        c_t = region("c_t", [P, T], 72)
        c_z = region("c_z", [P, T + 2], 74)
        c_a = region("c_a", [P, T], 77)
        c_b = region("c_b", [P, T], 79)
        z_b = region("z_b", [P, 2, T], 81)
        rot_in = region("rot_in", [P, 2, T], 48)
        rot_s = region("rot_s", [P, 2, T], 52)
        y_b = region("y_b", [P, HEADS, T], 48)
        y_c = region("y_c", [P, HEADS, T], 56)
        r_q = region("r_q", [P, HEADS, T], 64)
        r_k = region("r_k", [P, HEADS, T], 72)
        r_v = region("r_v", [P, TT, RET], 80)
        ret_mask = region("ret_mask", [P, HEADS, T], 36)
        s_ret = region("s_ret", [P, 2, 1280], 16)
        yc_hi = region("yc_hi", [P, 4, T], 16, F32R)
        yc_lo = region("yc_lo", [P, 4, T], 24, F32R)
        yb_hi = region("yb_hi", [P, 4, T], 32, F32R)
        yb_lo = region("yb_lo", [P, 4, T], 40, F32R)
        mg_hi = region("mg_hi", [P, KD, T], 48, F32R)
        mg_lo = region("mg_lo", [P, KD, T], 64, F32R)
        hid_hi = region("hid_hi", [P, FT, T], 0, F32R)
        hid_lo = region("hid_lo", [P, FT, T], 44, F32R)
        a_q = region("a_q", [P, 4, T], 0)
        a_k = region("a_k", [P, 1, T], 8)
        a_v = region("a_v", [P, TT, P], 10)
        a_q_lo, a_k_lo = region("a_q_lo", [P, 4, T], 0, F32R), region("a_k_lo", [P, 1, T], 8, F32R)
        d_q_lo, d_k_lo = region("d_q_lo", [P, 4, T], 12, F32R), region("d_k_lo", [P, 4, T], 20, F32R)
        a_q_st = [region("a_q_st0", [P, 4, T], 36, F32R), region("a_q_st1", [P, TT, D], 52, F32R)[:, :, T:]]
        a_k_st = [place(f"a_k_st{h}", [P, 1, T], F32R, scratch_at + h * 4 * T) for h in range(2)]
        d_q_st = [u_hi[:, 4 * h:4 * h + 4, :] for h in range(2)]
        d_k_st = [u_lo[:, 4 * h:4 * h + 4, :] for h in range(2)]
        d_q = region("d_q", [P, 4, T], 12)
        d_k = region("d_k", [P, 4, T], 20)
        d_v = region("d_v", [P, TT, T], 28)
        bias = region("bias", [P, TT, T], 44)
        rope_tab = region("rope_tab", [P, 4, T], 44)
        heads = region("heads", [P, TT, D], 52)
        prob = region("prob", [P, 3, T], 68)
        prob_t = region("prob_t", [P, 2, T], 74)
        q_in = region("q_in", [P, Q_IN, T], 68)
        q_s = region("q_s", [P, Q_S, T], 80)
        q_r = S[4]
        ang = [region(f"ang{i}", [P, T], 48 + 2 * i) for i in range(5)]
        pos_i = region("pos_i", [P, T], 58, I32)

        ones_c = sq_consts[:, C_ONES, :]
        ident_c = sq_consts[:, C_IDENT, :]
        tgate, sq_h = S[0:2], S[2:4]
        z_a = S[0:2]
        gt, mac, br = S[0:2], S[2:4], S[4]
        f_s, f_a = S[0:2], S[2:4]
        sq_m = S[0:2]

        ps = [ctx.enter_context(nc.psum_tensor(f"bank{b}", [P, T], F32)) for b in range(8)]

        def sem(name):
            return ctx.enter_context(nc.semaphore(name))

        consts_in = sem("consts_in")
        gains_in = sem("gains_in")
        positions_in = sem("positions_in")
        x_in = [sem(f"x_in{i}") for i in range(X_PARTS)]
        stored = sem("stored")
        x_last = sem("x_last")
        masks_in = sem("masks_in")
        tables_in = sem("tables_in")
        bias_in = sem("bias_in")
        dense_stacked = sem("dense_stacked")
        dilated_stacked = sem("dilated_stacked")
        raw_in = [sem(f"raw_in{i}") for i in range(RAW)]
        hi_split = sem("hi_split")
        lo_split = sem("lo_split")
        block_done = sem("block_done")
        drained = [sem(f"drained{b}") for b in range(8)]
        filled = [sem(f"filled{b}") for b in range(8)]

        def ev(name, per, credit=0):
            return Event(sem(name), per, credit)

        x_ready = ev("x_ready", KD)
        u_hi_ev = ev("u_hi_done", KD)
        u_lo_ev = ev("u_lo_done", KD)
        sq_done = ev("sq_done", KD)
        acc_done = ev("acc_done", 13)
        r_done = ev("r_done", 2)
        out_sq = ev("out_sq", KD)
        t_done = ev("t_done", KD)
        r_tm_done = ev("r_tm_done", 1)
        par_done = ev("par_done", 2)
        zeroed = ev("zeroed", 4)
        ga_split = ev("ga_split", 2)
        z_abs = ev("z_abs", 2)
        z_exp = ev("z_exp", 2)
        z_ln = ev("z_ln", 2)
        z_log = ev("z_log", 2)
        cum_done = ev("cum_done", 2)
        n_lev = len(UNITS) - 2
        lev_d = ev("lev_d", n_lev)
        lev_x = ev("lev_x", n_lev)
        lev_qk = ev("lev_qk", n_lev)
        conv_t = ev("conv_t", 4)
        conv_a = ev("conv_a", 12)
        conv_y = ev("conv_y", 4)
        y_hi = ev("y_hi", 12)
        y_lo = ev("y_lo", 12)
        rot_c = ev("rot_c", 8)
        rot_y = ev("rot_y", 8)
        rot_z = ev("rot_z", 8)
        rot_moved = [sem(f"rot_moved{i}") for i in range(2)]
        rv_sum = ev("rv_sum", 4)
        rv_cent = ev("rv_cent", 4)
        hn_sq = ev("hn_sq", 8)
        hn_rr = ev("hn_rr", 8)
        hn_y = ev("hn_y", 8)
        silu_g = ev("silu_g", 8)
        y_gated = ev("y_gated", 8)
        sig = ev("sig", 24)
        mac_add = ev("mac_add", 16)
        mg_hi_ev = ev("mg_hi_done", KD)
        mg_lo_ev = ev("mg_lo_done", KD)
        silu_f = ev("silu_f", FT)
        act_f = ev("act_f", FT)
        hid_hi_ev = ev("hid_hi_done", FT)
        hid_lo_ev = ev("hid_lo_done", FT)
        q_sq, q_rr, q_n = ev("q_sq", 5), ev("q_rr", 5), ev("q_n", 5)
        rope_c, rope_z, rope_y = ev("rope_c", 13), ev("rope_z", 13), ev("rope_y", 13)
        rope_moved = [sem(f"rope_moved{i}") for i in range(Q_S)]
        qk_hi = ev("qk_hi", 18)
        dense_lo, dilated_lo = ev("dense_lo", 10), ev("dilated_lo", 8)
        biased, maxed = ev("biased", 32), ev("maxed", 64)
        scored, inv_done = ev("scored", 64), ev("inv_done", 64)
        turned, hd_hi = ev("turned", KD), ev("hd_hi", KD)
        ang_step = sem("ang_step")
        trig_done = sem("trig_done")
        trig_tab = sem("trig_tab")

        side_table, side_per = side_banks()

        def side(key, li=None):
            b, n = side_table[key]
            return Use(ps[b], drained[b], filled[b], n if li is None else li * side_per[b] + n)

        def layer_outs(li):
            return Outs(li * (OUT_LAYER // 4))

        def result(ou, e):
            b = ou.bank(e)
            return Use(ps[b], drained[b], None, ou.uses(e))

        def one(i):
            return slice(i, i + 1) if isinstance(i, int) else bass.ds(i, 1)

        def flat(t):
            return t[:, :].rearrange("p (o n) -> p o n", o=1)

        def three(out, st_hi, st_lo, mv_hi, mv_lo, first, last):
            nc.tensor.matmul(out, st_hi, mv_hi, start=first, stop=False)
            nc.tensor.matmul(out, st_hi, mv_lo, start=False, stop=False)
            return nc.tensor.matmul(out, st_lo, mv_hi, start=False, stop=last)

        def pe_block(pe, bl, p, ou, e, in_hi, in_lo, k0=0, kn=KD, first=True, last=True, each_k=None):
            b, s = ou.bank(e), bl.slot(p)
            pe.wait_ge(lo_split, bl.n(p) + (RAW + 1))
            if first:
                pe.wait_ge(drained[b], ou.uses(e) + 1)
            for k in range(kn):
                if each_k is not None:
                    each_k(k)
                w = slice(k * P, (k + 1) * P)
                mm = three(ps[b][:, :], w_hi[:, s, w], w_lo[:, s, w], in_hi[:, k0 + k, :], in_lo[:, k0 + k, :],
                           first and k == 0, last and k == kn - 1)
            mm.then_inc(block_done, 1)

        def pe_pair(pe, bl, p, ou, e, in_hi, in_lo, in_ready, inst):
            for i in range(2):
                pe.wait_ge(lo_split, bl.n(p + i) + (RAW + 1))
                pe.wait_ge(drained[ou.bank(e + i)], ou.uses(e + i) + 1)
            for k in range(KD):
                pe.wait_ge(in_ready.sem, in_ready.upto(inst, k + 1))
                w = slice(k * P, (k + 1) * P)
                for i in range(2):
                    s = bl.slot(p + i)
                    mm = three(ps[ou.bank(e + i)][:, :], w_hi[:, s, w], w_lo[:, s, w], in_hi[:, k, :], in_lo[:, k, :],
                               k == 0, k == KD - 1)
                    if k == KD - 1:
                        mm.then_inc(block_done, 1)

        def pe_values(pe, bl, p, ou, e):
            for q in range(4):
                s = bl.slot(p + q)
                pe.wait_ge(lo_split, bl.n(p + q) + (RAW + 1))
                for k2 in range(2):
                    k = 2 * q + k2
                    w = slice(k2 * T, (k2 + 1) * T)
                    for t in range(TT):
                        if k == 0:
                            pe.wait_ge(drained[ou.bank(e + t)], ou.uses(e + t) + 1)
                        tok = slice(t * P, (t + 1) * P)
                        mm = three(ps[ou.bank(e + t)][:, :], u_hi[:, k, tok], u_lo[:, k, tok],
                                   w_hi[:, s, w], w_lo[:, s, w], k == 0, k == KD - 1)
                mm.then_inc(block_done, 1)

        def pe_sums_pre(pe, key, s, li=None):
            use = side(key, li)
            pe.wait_ge(use.drained, use.n + 1)
            pe.wait_ge(acc_done.sem, acc_done.upto(s, 7))
            nc.tensor.matmul(use.mem[:, :], ones_c, acc[:, :], start=True, stop=True).then_inc(use.filled, 1)

        def pe_sums_post(pe, key, s, li=None):
            use = side(key, li)
            pe.wait_ge(use.drained, use.n + 1)
            pe.wait_ge(acc_done.sem, acc_done.upto(s, 13))
            nc.tensor.matmul(use.mem[:, :], ones_c, acc[:, :], start=True, stop=False)
            pe.wait_ge(out_sq.sem, out_sq.upto(s, KD))
            nc.tensor.matmul(use.mem[:, :], ones_c, sq_m[(KD - 1) % 2][:, :], start=False, stop=True).then_inc(use.filled, 1)
            if key != "post4":
                pe.wait_ge(use.drained, use.n + 2)
                for _ in range(WARM):
                    nc.tensor.matmul(use.mem[:, :], ident_c, ret_cos[:, :], start=True, stop=True)

        def pe_sums_tm(pe, key, li=None):
            use = side(key, li)
            pe.wait_ge(use.drained, use.n + 1)
            for t in range(TT):
                mm = nc.tensor.matmul(use.mem[:, 2 * t:2 * t + 2], acc[:, t * P:(t + 1) * P], ones_c[:, 0:2],
                                      start=True, stop=True)
            mm.then_inc(use.filled, 1)

        def act_split(act, bl, p):
            act.wait_ge(raw_in[bl.raw(p)], bl.raw_uses(p) * 16 + 16)
            act.wait_ge(block_done, bl.n(p) + 1)
            nc.scalar.activation(w_hi[:, bl.slot(p), :], raw[:, bl.raw(p), :], ACT.Copy).then_inc(hi_split, 1)

        def dve_split(dve, bl, p):
            dve.wait_ge(hi_split, bl.n(p) + 1)
            nc.vector.tensor_tensor(w_lo[:, bl.slot(p), :], raw[:, bl.raw(p), :],
                                    w_hi[:, bl.slot(p), :].bitcast(F32), ALU.subtract).then_inc(lo_split, 1)

        def act_pre(act, s, gains, tiles=range(KD)):
            for k in tiles:
                act.wait_ge(x_ready.sem, x_ready.upto(s, k + 1))
                nc.scalar.activation(u_hi[:, k, :], x[:, k, :], ACT.Copy, scale=gains[:, k:k + 1]).then_inc(u_hi_ev.sem, 1)
                nc.scalar.activation(sq_x[:, k, :], x[:, k, :], ACT.Square).then_inc(sq_done.sem, 1)

        def act_rsqrt(act, key, li=None, half=False):
            four = 4.0 if half else 1.0
            use = side(key, li)
            act.wait_ge(use.filled, use.n + 1)
            nc.scalar.activation(r[:, :], use.mem[:, :], ACT.Ln, scale=four / D, bias=four * EPS).then_inc(use.drained, 1)
            src = side(key, li)
            act.wait_ge(src.drained, src.n + 2)
            nc.scalar.activation(r[:, :], r[:, :], ACT.Exp, scale=-0.5).then_inc(r_done.sem, 1)

        def act_rsqrt_tm(act, key, li=None):
            use = side(key, li)
            act.wait_ge(use.filled, use.n + 1)
            nc.scalar.activation(r_tm[:, :], use.mem[:, 0:2 * TT:2], ACT.Ln, scale=1.0 / D, bias=EPS).then_inc(use.drained, 1)
            src = side(key, li)
            act.wait_ge(src.drained, src.n + 2)
            nc.scalar.activation(r_tm[:, :], r_tm[:, :], ACT.Exp, scale=-0.5).then_inc(r_tm_done.sem, 1)

        def dve_low(dve, s, gains, k):
            dve.wait_ge(u_hi_ev.sem, u_hi_ev.upto(s, k + 1))
            nc.vector.scalar_tensor_tensor(u_lo[:, k, :], x[:, k, :], gains[:, k:k + 1],
                                           u_hi[:, k, :].bitcast(F32), ALU.mult, ALU.subtract).then_inc(u_lo_ev.sem, 1)

        def dve_squares(dve, s):
            for k in range(1, KD):
                dve.wait_ge(sq_done.sem, sq_done.upto(s, k + 1))
                if k > 1:
                    dve.wait_ge(acc_done.sem, acc_done.upto(s, k - 1))
                nc.vector.tensor_tensor(acc[:, :], sq_x[:, 0, :] if k == 1 else acc[:, :], sq_x[:, k, :],
                                        ALU.add).then_inc(acc_done.sem, 1)

        def act_out(act, s, m, bl, p, ou, e):
            act.wait_ge(block_done, bl.n(p) + (RING + 1))
            if m >= 2:
                act.wait_ge(acc_done.sem, acc_done.upto(s, 7 + max(m - 2, 1)))
            nc.scalar.activation(sq_m[m % 2][:, :], ps[ou.bank(e)][:, :], ACT.Square).then_inc(out_sq.sem, 1)

        def dve_out(dve, s, m, ou, e, gains, out):
            if m >= 2:
                dve.wait_ge(out_sq.sem, out_sq.upto(s, m))
                if m > 2:
                    dve.wait_ge(acc_done.sem, acc_done.upto(s, 7 + m - 2))
                nc.vector.tensor_tensor(acc[:, :], sq_m[0][:, :] if m == 2 else acc[:, :], sq_m[(m - 1) % 2][:, :],
                                        ALU.add).then_inc(acc_done.sem, 1)
            use = result(ou, e)
            dve.wait_ge(out_sq.sem, out_sq.upto(s, m + 1))
            nc.vector.tensor_scalar(out[:, m, :], use.mem[:, :], gains[:, m:m + 1], None, ALU.mult).then_inc(use.drained, 1)

        def dve_between(dve, s, ou, e, out, next_gains=None):
            LAG = 4
            use = result(ou, e)
            dve.wait_ge(use.drained, use.n + 2)
            dve.wait_ge(r_done.sem, r_done.upto(s, 2))
            for k in range(KD + LAG):
                if k < KD:
                    nc.vector.tensor_tensor(out[:, k, :], out[:, k, :], r[:, :], ALU.mult).then_inc(t_done.sem, 1)
                if k >= LAG and next_gains is not None:
                    dve_low(dve, s + 1, next_gains, k - LAG)
                if k in LAST_DVE and next_gains is None:
                    dve.wait_ge(t_done.sem, t_done.upto(s, k + 1))
                    nc.vector.tensor_tensor(x[:, k, :], x[:, k, :], out[:, k, :], ALU.add).then_inc(x_last, 1)
            if next_gains is not None:
                dve_squares(dve, s + 1)

        def pool_post(pool, s, out, tiles=range(KD)):
            for k in tiles:
                pool.wait_ge(t_done.sem, t_done.upto(s, k + 1))
                nc.gpsimd.tensor_tensor(x[:, k, :], x[:, k, :], out[:, k, :], ALU.add).then_inc(x_ready.sem, 1)

        def turn(bl, ou, j, blocks, outs):
            return Blocks(bl.quads + j * (blocks // 4), bl.s), Outs(ou.quads + j * (outs // 4), ou.s)

        def pe_ffn(pe, s, f, bl, ou, pre, post, li=None):
            pe_pair(pe, bl, 0, ou, 0, u_hi, u_lo, u_lo_ev, s)
            pe_block(pe, bl, 2, ou, 2, u_hi, u_lo)
            pe_sums_pre(pe, pre, s, li)
            pe_block(pe, bl, 3, ou, 3, u_hi, u_lo)
            with pe.Fori(1, UP_TURNS) as j:
                b, o = turn(bl, ou, j, N_UP, N_UP)
                for i in range(N_UP):
                    pe_block(pe, b, i, o, i, u_hi, u_lo)
            b1, o1 = bl.on(N_UP * UP_TURNS), ou.on(N_UP * UP_TURNS)
            for m in range(KD):
                k0 = 0
                for q, kn in enumerate(DOWN_K):
                    def hidden_k(k, k0=k0):
                        if k0 + k == 0:
                            pe.wait_ge(hid_lo_ev.sem, hid_lo_ev.upto(f, FT - 4))
                        if k0 + k >= FT - 4:
                            pe.wait_ge(hid_lo_ev.sem, hid_lo_ev.upto(f, k0 + k + 1))
                    pe_block(pe, b1, 3 * m + q, o1, m, hid_hi, hid_lo, k0, kn, q == 0, q == 2, hidden_k if m == 0 else None)
                    k0 += kn
            pe_sums_post(pe, post, s, li)

        def act_ffn(act, s, f, bl, ou, pre, post, li=None, half=False, next_gains=None):
            def up(j):
                b, o = turn(bl, ou, j, N_UP, N_UP)
                for i in range(2):
                    act_split(act, b, 2 * i + AHEAD)
                    if isinstance(j, int) and i == 0:
                        act_split(act, b, 1 + AHEAD)
                        act_rsqrt(act, pre, li)
                    act.wait_ge(drained[o.bank(2 * i)], o.uses(2 * i) + 2)
                    nc.scalar.activation(f_s[i][:, :], f_s[i][:, :], ACT.Silu).then_inc(silu_f.sem, 1)
                    if not isinstance(j, int) or i > 0:
                        act_split(act, b, 2 * i + 1 + AHEAD)
                    act.wait_ge(act_f.sem, act_f.upto(f, j * 2 + (i + 1)))
                    act.wait_ge(consts_in, CONSTS)
                    nc.scalar.activation(hid_hi[:, one(j * 2 + i), :], flat(f_a[i]), ACT.Copy).then_inc(hid_hi_ev.sem, 1)
            up(0)
            with act.Fori(1, UP_TURNS) as j:
                up(j)
            b1, o1 = bl.on(N_UP * UP_TURNS), ou.on(N_UP * UP_TURNS)
            nc.scalar.preload_act_table_set(EXP_LN)
            for m in range(KD):
                for q in range(3):
                    if next_gains is not None or 3 * m + q + AHEAD < 3 * KD:
                        act_split(act, b1, 3 * m + q + AHEAD)
                act_out(act, s, m, b1, 3 * m + 2, o1, m)
            act_rsqrt(act, post, li, half)
            if next_gains is not None:
                act_pre(act, s + 1, next_gains)

        def dve_ffn(dve, s, f, bl, ou, post_gains, next_gains=None):
            def up(j):
                b, o = turn(bl, ou, j, N_UP, N_UP)
                for i in range(2):
                    dve_split(dve, b, 2 * i + AHEAD)
                    if isinstance(j, int) and i == 0:
                        dve_split(dve, b, 1 + AHEAD)
                        dve.wait_ge(r_done.sem, r_done.upto(s, 1))
                    use = result(o, 2 * i)
                    dve.wait_ge(block_done, b.n(2 * i) + (RING + 1))
                    nc.vector.tensor_tensor(f_s[i][:, :], use.mem[:, :], r[:, :], ALU.mult).then_inc(use.drained, 1)
                    if not isinstance(j, int) or i > 0:
                        dve_split(dve, b, 2 * i + 1 + AHEAD)
                    use = result(o, 2 * i + 1)
                    dve.wait_ge(block_done, b.n(2 * i + 1) + (RING + 1))
                    dve.wait_ge(silu_f.sem, silu_f.upto(f, j * 2 + (i + 1)))
                    nc.vector.tensor_tensor(f_a[i][:, :], use.mem[:, :], f_s[i][:, :], ALU.mult).then_inc(use.drained, 1)
                    dve.wait_ge(drained[o.bank(2 * i + 1)], o.uses(2 * i + 1) + 2)
                    nc.vector.tensor_tensor(f_a[i][:, :], f_a[i][:, :], r[:, :], ALU.mult).then_inc(act_f.sem, 1)
                    dve.wait_ge(hid_hi_ev.sem, hid_hi_ev.upto(f, j * 2 + (i + 1)))
                    nc.vector.tensor_tensor(hid_lo[:, one(j * 2 + i), :], flat(f_a[i]),
                                            hid_hi[:, one(j * 2 + i), :].bitcast(F32), ALU.subtract).then_inc(hid_lo_ev.sem, 1)
            up(0)
            with dve.Fori(1, UP_TURNS) as j:
                up(j)
            b1, o1 = bl.on(N_UP * UP_TURNS), ou.on(N_UP * UP_TURNS)
            for m in range(KD):
                for q in range(3):
                    if next_gains is not None or 3 * m + q + AHEAD < 3 * KD:
                        dve_split(dve, b1, 3 * m + q + AHEAD)
                dve_out(dve, s, m, o1, m, post_gains, ffn_out)
            dve_between(dve, s, o1, KD - 1, ffn_out, next_gains)

        GQ, GK, GV, CV, RQ, RK, RV, GR, RG = 0, 2, 4, 8, 20, 24, 28, 32, 36
        unit_no = {u: i for i, u in enumerate(UNITS)}

        def conv_units(i):
            return [2 + 2 * (i - 3), 3 + 2 * (i - 3)] if 3 <= i <= 11 else []

        def halves(ap, lev):
            v = ap.rearrange("p (n b) -> p n b", b=lev)
            return v[:, :, 0:lev // 2], v[:, :, lev // 2:lev]

        def middles(ap, lev):
            v, h = ap.rearrange("p (n b) -> p n b", b=lev), lev // 2
            return v[:, :, h - 1:h].to_broadcast([P, T // lev, h])

        def by_head(ap):
            return ap[:, 0:T].rearrange("p (h n) -> p h n", h=2)

        def head_rows(h):
            return slice(HD * (h % 2), HD * (h % 2) + HD)

        def tok(i, n=1):
            return slice(i * P, (i + n) * P)

        def rope_tile(i):
            if i < 5:
                return (a_q[:, i, :] if i < 4 else a_k[:, 0, :]), i, 0
            return (d_q if i < 9 else d_k)[:, (i - 5) % 4, :], i + 1, 2

        def dense_tile(j):
            if j < 4:
                return a_q[:, j, :], a_q_lo[:, j, :], [st[:, j, :] for st in a_q_st]
            return a_k[:, 0, :], a_k_lo[:, 0, :], [st[:, 0, :] for st in a_k_st]

        def dilated_part(j):
            h, pair = j % 2, slice(j // 2 % 2 * 2, j // 2 % 2 * 2 + 2)
            of, lo, st = (d_q, d_q_lo, d_q_st) if j < 4 else (d_k, d_k_lo, d_k_st)
            rows = head_rows(h)
            return of[rows, pair, :], lo[rows, pair, :], st[h][rows, pair, :]

        def attention_unit(u):
            dense, t, h, it = u < 32, u % 32 // 8, u // 4 % 2, u % 4
            return dense, t, h, it, HD * (t + 4 * h if dense else 8 + 2 * t + h)

        block = ctx.enter_context(nc.Block())

        @block.sync
        def _(sp):
            sp.dma_start(pos_i[:, :], dram["positions"].to_broadcast([P, T])).then_inc(positions_in, 16)
            sp.dma_start(inv_freq[:, :], dram["inv_freq"]).then_inc(positions_in, 16)
            sp.dma_start(par2[:, :], dram["par2"]).then_inc(gains_in, 16)
            for i in range(X_PARTS):
                part = slice(i * KD // X_PARTS, (i + 1) * KD // X_PARTS)
                sp.dma_start(x[:, part, :], dram["x"][:, part, :]).then_inc(x_in[i], 16)

            def load(bl, p, col, size):
                if isinstance(col, int):
                    src = dram["weights"][:, col:col + size]
                else:
                    src = dram["weights"][:, bass.ds(sp.snap(col), size)]
                sp.wait_ge(lo_split, bl.n(p) + 1)
                sp.dma_start(raw[:, bl.raw(p), 0:size], src).then_inc(raw_in[bl.raw(p)], 16)

            def ffn(bl, col):
                with sp.Fori(0, UP_TURNS) as j:
                    for i in range(N_UP):
                        load(Blocks(bl.quads + j, bl.s), i, j * (N_UP * BLK) + (col + i * BLK), BLK)
                b, c = bl.on(N_UP * UP_TURNS), col + UP_TURNS * N_UP * BLK
                with sp.Fori(0, DOWN_TURNS) as j:
                    at = 0
                    for m in range(4):
                        for q, kn in enumerate(DOWN_K):
                            load(Blocks(b.quads + j * (N_DOWN // 4), b.s), 3 * m + q, j * COLS_DOWN + (c + at), kn * P)
                            at += kn * P

            with sp.Fori(0, LAYERS) as li:
                bl, col = Blocks(li * (N_LAYER // 4)), li * COLS_LAYER
                for i in range(N_HEAD):
                    load(bl, i, col + i * BLK, BLK)
                    if i == RV + 3:
                        src = side("out3", li)
                        sp.wait_ge(src.drained, src.n + 2)
                        sp.dma_start(ret_mask[:, :, :], dram["ret_mask"]).then_inc(masks_in, 16)
                with sp.Fori(0, GATE_TURNS) as j:
                    at = N_HEAD * BLK
                    for i in range(N_GATE):
                        size = BLK if i % 2 == 0 else BLK // 2
                        load(Blocks(bl.quads + j * (N_GATE // 4), N_HEAD), i, li * COLS_LAYER + j * COLS_GATE + at, size)
                        at += size
                b = bl.on(N_HEAD + N_GATE * GATE_TURNS)
                c = N_HEAD * BLK + GATE_TURNS * COLS_GATE
                for i in range(KD):
                    load(b, i, col + (c + i * BLK), BLK)
                ffn(b.on(KD), col + (c + KD * BLK))
            bl, col = Blocks(LAYERS * (N_LAYER // 4)), LAYERS * COLS_LAYER
            ffn(bl, col)
            bl, col = bl.on(N_FFN), col + COLS_FFN
            for i in range(N_QKV + KD):
                load(bl, i, col + i * BLK, BLK)
                if i == RING:
                    sp.wait_ge(r_done.sem, r_done.upto(4, 2))
                    sp.dma_start(rope_tab[:, :, :], dram["rope_tab"]).then_inc(tables_in, 16)
                if 12 <= i < 17:
                    j = i - 12
                    _, lo, st = dense_tile(j)
                    sp.wait_ge(dense_lo.sem, 2 * j + 2)
                    for h in range(2):
                        rows, other = head_rows(h), head_rows(1 - h)
                        sp.dma_start(st[h][other].bitcast(F32), (lo[rows] if j < 4 else st[h][rows]).bitcast(F32)).then_inc(dense_stacked, 16)
                if i == N_QKV + AHEAD + RAW - 1:
                    sp.wait_ge(rope_y.sem, 13)
                    sp.dma_start(bias[:, :, :], dram["bias"]).then_inc(bias_in, 16)
                    sp.wait_ge(dilated_lo.sem, 8)
                    for h in range(2):
                        rows, other = head_rows(h), head_rows(1 - h)
                        sp.dma_start(d_q_st[h][other].bitcast(F32), d_q_lo[rows, :, :].bitcast(F32)).then_inc(dilated_stacked, 16)
                        sp.dma_start(d_k_st[h][other].bitcast(F32), d_k_st[h][rows].bitcast(F32)).then_inc(dilated_stacked, 16)
            ffn(bl.on(N_QKV + KD), col + (N_QKV + KD) * BLK)
            for k in range(KD):
                if k in LAST_DVE:
                    sp.wait_ge(x_last, LAST_DVE.index(k) + 1)
                else:
                    sp.wait_ge(x_ready.sem, x_ready.upto(7, k + 1 - sum(v < k for v in LAST_DVE)))
                sp.dma_start(dram["out"][:, k, :], x[:, k, :]).then_inc(stored, 16)
            sp.wait_ge(stored, 16 * KD)

        @block.gpsimd
        def _(pool):
            credits = [(lo_split, RAW), (block_done, RING)] + [(d, 1) for d in drained]
            for i, (free, n) in enumerate(credits):
                nc.gpsimd.memset(wait_cell[:, i:i + 1], 0.0).then_inc(free, n)
            for i in range(X_PARTS):
                pool.wait_ge(x_in[i], 16)
                c = len(credits) + i
                nc.gpsimd.memset(wait_cell[:, c:c + 1], 0.0).then_inc(x_ready.sem, KD // X_PARTS)
            with pool.Fori(0, LAYERS) as li:
                nc.gpsimd.memset(ga_w[:, :, :].bitcast(F32), 0.0).then_inc(zeroed.sem, 1)
                nc.gpsimd.memset(lev_q[:, :, :], 0.0).then_inc(zeroed.sem, 1)
                nc.gpsimd.memset(lev_k[:, :, :], 0.0).then_inc(zeroed.sem, 1)
                nc.gpsimd.memset(c_z[:, 0:2], 0.0).then_inc(zeroed.sem, 1)
                ou = layer_outs(li)
                for i in range(8):
                    to = (r_q if i < 4 else r_k)[:, i % 4, :]
                    if i == 0:
                        old = side(f"gla{len(UNITS) - 1}1", li)
                        pool.wait_ge(old.filled, old.n + 1)
                    pool.wait_ge(drained[ou.bank(RQ + i)], ou.uses(RQ + i) + 2)
                    nc.gpsimd.tensor_tensor(to, rot_in[:, i % 2, :], ret_cos[:, :], ALU.mult).then_inc(rot_c.sem, 1)
                    pool.wait_ge(rot_z.sem, rot_z.upto(li, i + 1))
                    pool.wait_ge(rot_c.sem, rot_c.upto(li, i + 1))
                    nc.gpsimd.tensor_tensor(to, to, rot_s[:, i % 2, :], ALU.add).then_inc(rot_y.sem, 1)
                pool_post(pool, li * 2, mix_out)
                pool_post(pool, li * 2 + 1, ffn_out)
            pool_post(pool, 4, ffn_out)
            ou = Outs(LAYERS * (OUT_LAYER // 4), OUT_FFN)
            pool.wait_ge(tables_in, 16)
            for i in range(13):
                to, e, tab = rope_tile(i)
                if i < 5:
                    pool.wait_ge(q_n.sem, q_n.upto(0, i + 1))
                else:
                    pool.wait_ge(drained[ou.bank(e)], ou.uses(e) + 2)
                nc.gpsimd.tensor_tensor(to, q_in[:, i % Q_IN, :], rope_tab[:, tab, :], ALU.mult).then_inc(rope_c.sem, 1)
                pool.wait_ge(rope_z.sem, rope_z.upto(0, i + 1))
                pool.wait_ge(rope_c.sem, rope_c.upto(0, i + 1))
                nc.gpsimd.tensor_tensor(to, to, q_s[:, i % Q_S, :], ALU.add).then_inc(rope_y.sem, 1)
            for j in range(8):
                of, lo, st = dilated_part(j)
                pool.wait_ge(qk_hi.sem, 10 + j + 1)
                nc.gpsimd.tensor_tensor(lo, of, st.bitcast(F32), ALU.subtract).then_inc(dilated_lo.sem, 1)
            pool_post(pool, 5, mix_out)
            pool_post(pool, 6, ffn_out, [k for k in range(KD) if k not in LAST_DVE])

        @block.tensor
        def _(pe):
            def unit(u, li):
                lev, t = UNITS[u]
                if lev == 1:
                    for e in range(4):
                        pe.wait_ge(drained[layer_outs(li).bank(GQ + e)], layer_outs(li).uses(GQ + e) + 2)
                    q, k = g_q[:, t, :], g_k[:, t, :]
                else:
                    pe.wait_ge(lev_qk.sem, lev_qk.upto(li, u - 1))
                    q, k = lev_q[:, u % 2, :], lev_k[:, u % 2, :]
                for i, key in enumerate(level_keys(u)):
                    use = side(key, li)
                    pe.wait_ge(use.drained, use.n + 1)
                    if lev == 1:
                        for kt in range(TT):
                            mm = nc.tensor.matmul(use.mem[:, tok(kt)], k[head_rows(i), tok(kt)], q[head_rows(i), tok(kt)],
                                                  start=True, stop=True)
                    else:
                        tiles = [i] if lev == 512 else [0, 2] if lev == 256 else range(TT)
                        n = T // 2 // len(tiles)
                        for c, kt in enumerate(tiles):
                            cols = slice(c * n, (c + 1) * n)
                            mm = nc.tensor.matmul(by_head(use.mem)[:, :, cols], k[:, tok(kt)], by_head(q)[:, :, cols],
                                                  start=True, stop=True)
                    mm.then_inc(use.filled, 1)

            def gla_out(h, li):
                if h % 2 == 0:
                    for t in range(TT):
                        pe.wait_ge(drained[layer_outs(li).bank(GV + t)], layer_outs(li).uses(GV + t) + 2)
                    for hh in range(2):
                        src = side(f"gla{unit_no[(512, h // 2)]}{hh}", li)
                        pe.wait_ge(src.drained, src.n + 2)
                use = side(f"out{h}", li)
                pe.wait_ge(use.drained, use.n + 1)

                def add(kt, qt, n, s, first=False, last=False):
                    return nc.tensor.matmul(use.mem[:, tok(qt, n)], g_v[:, kt, tok(h)], s, start=first, stop=last)
                for i in range(TT):
                    add(i, i, 1, s_diag[:, h, tok(i)], i == 0)
                add(0, 1, 1, s_off[:, h, 0:128])
                add(2, 3, 1, s_off[:, h, 128:256])
                add(0, 2, 2, s_off[:, h, 256:512])
                add(1, 2, 2, s_off[:, h, 512:768], last=True).then_inc(use.filled, 1)

            def ret_scores(h, li):
                pe.wait_ge(rot_y.sem, rot_y.upto(li, 4 + h + 1))
                use = side(f"s{h}0", li)
                pe.wait_ge(use.drained, use.n + 1)
                nc.tensor.matmul(use.mem[:, :], r_k[:, h, tok(0)], r_q[:, h, :], start=True, stop=True).then_inc(use.filled, 1)
                use = side(f"s{h}1", li)
                pe.wait_ge(use.drained, use.n + 1)
                nc.tensor.matmul(use.mem[:, 0:384], r_k[:, h, tok(1)], r_q[:, h, tok(1, 3)], start=True, stop=True)
                nc.tensor.matmul(use.mem[:, 384:512], r_k[:, h, tok(3)], r_q[:, h, tok(3)], start=True, stop=True).then_inc(use.filled, 1)
                use = side(f"s{h}2", li)
                pe.wait_ge(use.drained, use.n + 1)
                nc.tensor.matmul(use.mem[:, 0:256], r_k[:, h, tok(2)], r_q[:, h, tok(2, 2)], start=True, stop=True).then_inc(use.filled, 1)

            def ret_out(h, li):
                for i in range(3):
                    src = side(f"s{h}{i}", li)
                    pe.wait_ge(src.drained, src.n + 2)
                if h == 0:
                    pe.wait_ge(rv_cent.sem, rv_cent.upto(li, 4))
                use = side(f"out{4 + h}", li)
                pe.wait_ge(use.drained, use.n + 1)
                s = s_ret[:, h % 2, :]
                for kt, a, b in ((0, 0, 512), (1, 512, 896), (2, 896, 1152), (3, 1152, 1280)):
                    mm = nc.tensor.matmul(use.mem[:, tok(kt, TT - kt)], r_v[:, kt, tok(h)], s[:, a:b], start=kt == 0, stop=kt == 3)
                mm.then_inc(use.filled, 1)

            def head_var(n, li):
                pe.wait_ge(hn_sq.sem, hn_sq.upto(li, n + 1))
                use = side(f"var{n}", li)
                pe.wait_ge(use.drained, use.n + 1)
                nc.tensor.matmul(use.mem[:, :], ones_c, sq_h[n % 2][:, :], start=True, stop=True).then_inc(use.filled, 1)

            def layer(li):
                bl, ou, s = Blocks(li * (N_LAYER // 4)), layer_outs(li), li * 2

                def project(i):
                    pe_block(pe, bl, i, ou, i, u_hi, u_lo)

                pe_pair(pe, bl, 0, ou, 0, u_hi, u_lo, u_lo_ev, s)
                project(2)
                pe.wait_ge(consts_in, CONSTS)
                pe_sums_pre(pe, "pre0", s, li)
                pe_sums_tm(pe, "tm0", li)
                project(3)
                pe.wait_ge(ga_split.sem, ga_split.upto(li, 2))
                use = side("ga", li)
                pe.wait_ge(use.drained, use.n + 1)
                for k in range(KD):
                    nc.tensor.matmul(use.mem[:, :], ga_w[:, k, :], u_hi[:, k, :], start=k == 0, stop=False)
                    mm = nc.tensor.matmul(use.mem[:, :], ga_w[:, k, :], u_lo[:, k, :], start=False, stop=k == KD - 1)
                mm.then_inc(use.filled, 1)
                pe_values(pe, bl, GV, ou, GV)
                src = side("ga", li)
                pe.wait_ge(src.drained, src.n + 2)
                pe.wait_ge(par_done.sem, par_done.upto(li, 2))
                for t in range(2):
                    use = side(f"z{t}", li)
                    pe.wait_ge(use.drained, use.n + 1)
                    nc.tensor.matmul(use.mem[:, :], wa2[:, tok(t)], ga_t[:, :], start=True, stop=True).then_inc(use.filled, 1)
                unit(0, li)
                unit(1, li)
                for i in range(12):
                    project(CV + i)
                    for u in conv_units(i - 1):
                        unit(u, li)
                project(RQ)
                for u in conv_units(11):
                    unit(u, li)
                for i in range(1, 8):
                    project(RQ + i)
                    if i <= 4:
                        gla_out(i - 1, li)
                    if 2 <= i <= 5:
                        head_var(i - 2, li)
                pe_values(pe, bl, RV, ou, RV)
                for h in range(HEADS):
                    project(GR + h)
                    ret_scores(h, li)
                    if h >= 1:
                        ret_out(h - 1, li)
                    if h >= 2:
                        head_var(2 + h, li)
                project(RG)
                ret_out(3, li)
                head_var(6, li)
                project(RG + 1)
                head_var(7, li)
                project(RG + 2)
                project(RG + 3)
                with pe.Fori(0, GATE_TURNS) as j:
                    b, o = turn(bl.on(N_HEAD), ou.on(N_HEAD), j, N_GATE, N_GATE)
                    for i in range(N_GATE // 2):
                        pe_block(pe, b, 2 * i, o, 2 * i, u_hi, u_lo)
                        pe.wait_ge(y_lo.sem, y_lo.upto(li, 12 if i % 3 == 2 else 8))
                        y = ((ya_hi, ya_lo), (yc_hi, yc_lo), (yb_hi, yb_lo))[i % 3]
                        pe_block(pe, b, 2 * i + 1, o, 2 * i + 1, y[0], y[1], kn=4)
                b, o = bl.on(N_HEAD + N_GATE * GATE_TURNS), ou.on(N_HEAD + N_GATE * GATE_TURNS)

                def merged_k(k):
                    pe.wait_ge(mg_lo_ev.sem, mg_lo_ev.upto(li, k + 1))
                for i in range(KD):
                    pe_block(pe, b, i, o, i, mg_hi, mg_lo, each_k=merged_k if i == 0 else None)
                pe_sums_post(pe, "post0", s, li)
                pe_ffn(pe, s + 1, li, b.on(KD), o.on(KD), "pre1", "post1", li)

            pe.wait_ge(x_in[0], 16)
            pe.wait_ge(drained[7], 1)
            for _ in range(5):
                nc.tensor.matmul(ps[7][:, :], x[:, 0, 0:P], x[:, 0, :], start=True, stop=True)
            with pe.Fori(0, LAYERS) as li:
                layer(li)

            bl, ou = Blocks(LAYERS * (N_LAYER // 4)), Outs(LAYERS * (OUT_LAYER // 4))
            pe_ffn(pe, 4, 2, bl, ou, "pre2", "post2")
            bl, ou = bl.on(N_FFN), ou.on(OUT_FFN)

            def q_var(i):
                pe.wait_ge(q_sq.sem, q_sq.upto(0, i + 1))
                use = side(f"qvar{i}")
                pe.wait_ge(use.drained, use.n + 1)
                nc.tensor.matmul(use.mem[:, :], sq_consts[:, C_BD64, :], sq_h[i % 2][:, :], start=True, stop=True).then_inc(use.filled, 1)

            pe_pair(pe, bl, 0, ou, 0, u_hi, u_lo, u_lo_ev, 5)
            for i in range(2, 14):
                if i == 5:
                    b, s = ou.bank(5), bl.slot(5)
                    pe.wait_ge(lo_split, bl.n(5) + (RAW + 1))
                    pe.wait_ge(drained[b], ou.uses(5) + 1)
                    for t in range(TT):
                        for k in range(KD):
                            mm = three(ps[b][:, tok(t)], u_hi[:, k, tok(t)], u_lo[:, k, tok(t)],
                                       w_hi[:, s, tok(k)], w_lo[:, s, tok(k)], k == 0, k == KD - 1)
                    mm.then_inc(block_done, 1)
                else:
                    pe_block(pe, bl, i, ou, i, u_hi, u_lo)
                if i == 2:
                    pe_sums_pre(pe, "pre3", 5)
                    pe_sums_tm(pe, "tm3")
                if 3 <= i <= 7:
                    q_var(i - 3)
            pe_values(pe, bl, 14, ou, 14)

            def score(u):
                dense, t, h, it, _ = attention_unit(u)
                if u == 0:
                    pe.wait_ge(dense_lo.sem, 10)
                    pe.wait_ge(dense_stacked, 160)
                if u == 32:
                    pe.wait_ge(dilated_lo.sem, 8)
                    pe.wait_ge(dilated_stacked, 64)
                e = N_QKV + u
                pe.wait_ge(drained[ou.bank(e)], ou.uses(e) + 1)
                to, rows = ps[ou.bank(e)][:, :], head_rows(h)
                if dense:
                    q, k, k_lo = a_q_st[h], a_k_st[h][:, 0, :], a_k_lo[rows, 0, :]
                else:
                    q, k, k_lo = d_q_st[h], d_k_st[h][:, t, :], d_k_lo[rows, t, :]
                nc.tensor.matmul(to, q[:, t, tok(it)], k, start=True, stop=False)
                nc.tensor.matmul(to, q[rows, t, tok(it)], k_lo, start=False, stop=True).then_inc(scored.sem, 1)

            def turn_probs(u):
                pe.wait_ge(drained[ou.bank(N_QKV + u)], ou.uses(N_QKV + u) + 2)
                use = side(f"pt{u}")
                pe.wait_ge(use.drained, use.n + 1)
                for j in range(TT):
                    mm = nc.tensor.transpose(use.mem[:, tok(j)], prob[:, u % 3, tok(j)], ident_c)
                mm.then_inc(use.filled, 1)

            def weigh(u):
                dense, t, h, it, _ = attention_unit(u)
                if u == 0:
                    pe.wait_ge(drained[ou.bank(5)], ou.uses(5) + 2)
                if u == 32:
                    for i in range(TT):
                        pe.wait_ge(drained[ou.bank(14 + i)], ou.uses(14 + i) + 2)
                src = side(f"pt{u}")
                pe.wait_ge(src.drained, src.n + 2)
                use = side(f"o{u}")
                pe.wait_ge(use.drained, use.n + 1)
                v, c = (a_v, HD * h) if dense else (d_v, HD * (2 * t + h))
                for j in range(TT):
                    mm = nc.tensor.matmul(use.mem[:, 0:HD], prob_t[:, u % 2, tok(j)], v[:, j, c:c + HD], start=j == 0, stop=j == TT - 1)
                mm.then_inc(use.filled, 1)

            for u in range(-3, 64):
                if u + 3 < 64:
                    score(u + 3)
                if u >= 0:
                    turn_probs(u)
                if u >= 1:
                    weigh(u - 1)
            weigh(63)
            for k in range(KD):
                e = N_QKV + 64 + k
                if k == 0:
                    src = side("o62")
                    pe.wait_ge(src.drained, src.n + 2)
                    src = side("o63")
                    pe.wait_ge(src.drained, src.n + 2)
                pe.wait_ge(drained[ou.bank(e)], ou.uses(e) + 1)
                for t in range(TT):
                    mm = nc.tensor.transpose(ps[ou.bank(e)][:, tok(t)], heads[:, t, tok(k)], ident_c)
                mm.then_inc(turned.sem, 1)

            def heads_k(k):
                pe.wait_ge(drained[ou.bank(N_QKV + 64 + k)], ou.uses(N_QKV + 64 + k) + 2)
            for i in range(KD):
                pe_block(pe, bl, N_QKV + i, ou, N_QKV + 64 + KD + i, u_hi, u_lo, each_k=heads_k if i == 0 else None)
            pe_sums_post(pe, "post3", 5)
            pe_ffn(pe, 6, 3, bl.on(N_QKV + KD), ou.on(N_QKV + 64 + 2 * KD), "pre4", "post4")

        @block.scalar
        def _(act):
            def head_copy(n, li):
                y = (y_c if n < 4 else y_b)[:, n % 4, :]
                if n == 4:
                    act.wait_ge(rot_y.sem, rot_y.upto(li, 8))
                use = side(f"out{n}", li)
                act.wait_ge(use.filled, use.n + 1)
                nc.scalar.activation(y, use.mem[:, :], ACT.Copy).then_inc(use.drained, 1)
                src = side(f"out{n}", li)
                act.wait_ge(src.drained, src.n + 2)
                nc.scalar.activation(sq_h[n % 2][:, :], y, ACT.Square).then_inc(hn_sq.sem, 1)

            def head_rsqrt(n, li):
                use = side(f"var{n}", li)
                act.wait_ge(use.filled, use.n + 1)
                if n >= 2:
                    act.wait_ge(hn_y.sem, hn_y.upto(li, n - 1))
                nc.scalar.activation(hn_r[:, n % 2, :], use.mem[:, :], ACT.Ln, scale=1.0 / P, bias=EPS).then_inc(use.drained, 1)
                src = side(f"var{n}", li)
                act.wait_ge(src.drained, src.n + 2)
                nc.scalar.activation(hn_r[:, n % 2, :], hn_r[:, n % 2, :], ACT.Exp, scale=-0.5).then_inc(hn_rr.sem, 1)

            def level_exp(u, li):
                act.wait_ge(lev_d.sem, lev_d.upto(li, u - 1))
                nc.scalar.activation(lev_e[:, u % 2, :], lev_e[:, u % 2, :], ACT.Exp, scale=1.0 / 16).then_inc(lev_x.sem, 1)

            def take_off(u, li):
                lev, t = UNITS[u]
                for i, key in enumerate(level_keys(u)):
                    use = side(key, li)
                    act.wait_ge(use.filled, use.n + 1)
                    a = 0 if lev == 256 else 256 * (i + 1)
                    nc.scalar.activation(s_off[:, 2 * t:2 * t + 2, a:a + T // 2], by_head(use.mem), ACT.Copy).then_inc(use.drained, 1)

            def values(bl, p, ou, e, to):
                for t in range(TT):
                    use = result(ou, e + t)
                    act.wait_ge(block_done, bl.n(p + 3) + (RING + 1))
                    nc.scalar.activation(to[:, t, :], use.mem[:, :], ACT.Copy, scale=r_tm[:, t:t + 1]).then_inc(use.drained, 1)

            def gate_silu(g, ou, li):
                act.wait_ge(drained[ou.bank(GR + g)], ou.uses(GR + g) + 2)
                nc.scalar.activation(tgate[g % 2][:, :], tgate[g % 2][:, :], ACT.Silu).then_inc(silu_g.sem, 1)

            def y_high(n, li):
                if n < 4:
                    act.wait_ge(conv_y.sem, conv_y.upto(li, n + 1))
                    to, of = ya_hi, c_a[:, :]
                else:
                    act.wait_ge(y_gated.sem, y_gated.upto(li, n - 3))
                    to, of = (yc_hi, y_c[:, n % 4, :]) if n < 8 else (yb_hi, y_b[:, n % 4, :])
                nc.scalar.activation(to[:, n % 4, :], of, ACT.Copy).then_inc(y_hi.sem, 1)

            def rotate(i, ou, li):
                act.wait_ge(drained[ou.bank(RQ + i)], ou.uses(RQ + i) + 2)
                if i >= 2:
                    act.wait_ge(rot_y.sem, rot_y.upto(li, i - 1))
                for to, of in ((0, HALF), (HALF, 0)):
                    act.dma_start(rot_s[to:to + HALF, i % 2, :], rot_in[of:of + HALF, i % 2, :]).then_inc(rot_moved[i % 2], 16)

            def layer(li):
                bl, ou, s = Blocks(li * (N_LAYER // 4)), layer_outs(li), li * 2

                def split(i):
                    act_split(act, bl, i + AHEAD)
                nc.scalar.preload_act_table_set(EXP_LN)
                act.wait_ge(par_done.sem, par_done.upto(li, 2))
                act.wait_ge(zeroed.sem, zeroed.upto(li, 4))
                nc.scalar.activation(ga_w[:, :, 0:RANK], par[:, P_WGA:].rearrange("p (k n) -> p k n", k=KD),
                                     ACT.Copy).then_inc(ga_split.sem, 1)
                split(0)
                split(1)
                act_rsqrt(act, "pre0", li)
                act_rsqrt_tm(act, "tm0", li)
                for i in range(2, 8):
                    split(i)
                act.wait_ge(r_tm_done.sem, r_tm_done.upto(li, 1))
                values(bl, GV, ou, GV, g_v)
                for t in range(2):
                    act.wait_ge(z_abs.sem, z_abs.upto(li, t + 1))
                    nc.scalar.activation(z_a[t][:, :], z_a[t][:, :], ACT.Exp).then_inc(z_exp.sem, 1)
                for t in range(2):
                    act.wait_ge(z_exp.sem, z_exp.upto(li, t + 1))
                    nc.scalar.activation(z_a[t][:, :], z_a[t][:, :], ACT.Ln, bias=1.0).then_inc(z_ln.sem, 1)
                for i in range(12):
                    split(CV + i)
                    for u in conv_units(i):
                        level_exp(u, li)
                    if i == 11:
                        take_off(16, li)
                        take_off(17, li)
                    if i % 3 == 2:
                        y_high(i // 3, li)
                split(RQ)
                take_off(18, li)
                take_off(19, li)
                for i in range(1, 8):
                    split(RQ + i)
                    rotate(i - 1, ou, li)
                    if i <= 4:
                        head_copy(i - 1, li)
                    if 2 <= i <= 5:
                        head_rsqrt(i - 2, li)
                for i in range(4):
                    split(RV + i)
                    if i == 0:
                        rotate(7, ou, li)
                values(bl, RV, ou, RV, r_v)
                for h in range(HEADS):
                    split(GR + h)
                    gate_silu(h, ou, li)
                    if h >= 1:
                        head_copy(3 + h, li)
                    if h >= 2:
                        head_rsqrt(2 + h, li)
                split(RG)
                gate_silu(4, ou, li)
                head_copy(7, li)
                head_rsqrt(6, li)
                split(RG + 1)
                gate_silu(5, ou, li)
                head_rsqrt(7, li)
                for n in range(4, 9):
                    y_high(n, li)
                split(RG + 2)
                gate_silu(6, ou, li)
                y_high(9, li)
                split(RG + 3)
                gate_silu(7, ou, li)
                y_high(10, li)
                y_high(11, li)
                with act.Fori(0, GATE_TURNS) as j:
                    b, o = turn(bl.on(N_HEAD), ou.on(N_HEAD), j, N_GATE, N_GATE)
                    for i in range(N_GATE // 2):
                        act_split(act, b, 2 * i + AHEAD)
                        act.wait_ge(drained[o.bank(2 * i)], o.uses(2 * i) + 2)
                        nc.scalar.activation(gt[i % 2][:, :], gt[i % 2][:, :], ACT.Sigmoid).then_inc(sig.sem, 1)
                        act_split(act, b, 2 * i + 1 + AHEAD)
                        if i % 3 == 2:
                            m = i // 3
                            act.wait_ge(mac_add.sem, mac_add.upto(li, j * 4 + (2 * m + 2)))
                            act.wait_ge(consts_in, CONSTS)
                            nc.scalar.activation(mg_hi[:, one(j * 2 + m), :], flat(mac[m]), ACT.Copy).then_inc(mg_hi_ev.sem, 1)
                b, o = bl.on(N_HEAD + N_GATE * GATE_TURNS), ou.on(N_HEAD + N_GATE * GATE_TURNS)
                nc.scalar.preload_act_table_set(EXP_LN)
                for m in range(KD):
                    act_split(act, b, m + AHEAD)
                    act_out(act, s, m, b, m, o, m)
                act_rsqrt(act, "post0", li)
                act_pre(act, s + 1, par[:, G_FFN_PRE:G_FFN_PRE + KD])
                act_ffn(act, s + 1, li, b.on(KD), o.on(KD), "pre1", "post1", li, next_gains=par[:, G_NEXT:G_NEXT + KD])

            nc.scalar.preload_act_table_set(EXP_LN)
            first = par2[:, H_FIRST:H_FIRST + KD]
            act.wait_ge(gains_in, 16)
            act_pre(act, 0, first, range(KD // 2))
            for to, name in ((par_all[:, :, :], "par_all"),
                             (sq_consts[:, :, :], "sq_consts"), (wa2_all[:, :, :], "wa2"), (gla_masks[:, :, :], "gla_masks")):
                act.dma_start(to, dram[name]).then_inc(consts_in, 16)
            act_split(act, Blocks(0), 0)
            act_split(act, Blocks(0), 1)
            act_pre(act, 0, first, range(KD // 2, KD))
            act_split(act, Blocks(0), 2)
            for i, to in ((0, ret_sin), (1, ret_cos)):
                act.wait_ge(trig_done, i + 1)
                nc.scalar.activation(to[:, :], ang[2 + i][:, :], ACT.Sin).then_inc(trig_tab, 1)
            with act.Fori(0, LAYERS) as li:
                layer(li)

            bl, ou = Blocks(LAYERS * (N_LAYER // 4)), Outs(LAYERS * (OUT_LAYER // 4))
            act_ffn(act, 4, 2, bl, ou, "pre2", "post2", half=True, next_gains=par2[:, H_MPRE:H_MPRE + KD])
            bl, ou = bl.on(N_FFN), ou.on(OUT_FFN)

            def q_square(i):
                act.wait_ge(drained[ou.bank(i)], ou.uses(i) + 2)
                nc.scalar.activation(sq_h[i % 2][:, :], q_in[:, i % Q_IN, :], ACT.Square).then_inc(q_sq.sem, 1)

            def q_rsqrt(i):
                use = side(f"qvar{i}")
                act.wait_ge(use.filled, use.n + 1)
                if i >= 1:
                    act.wait_ge(q_n.sem, q_n.upto(0, i))
                n = HD if i < 4 else 1
                nc.scalar.activation(q_r[:, :], use.mem[:, :], ACT.Ln, scale=n / HD, bias=n * EPS).then_inc(use.drained, 1)
                src = side(f"qvar{i}")
                act.wait_ge(src.drained, src.n + 2)
                nc.scalar.activation(q_r[:, :], q_r[:, :], ACT.Exp, scale=-0.5).then_inc(q_rr.sem, 1)

            for i in range(18):
                if i != 1:
                    act_split(act, bl, i + AHEAD)
                if i == 0:
                    act_split(act, bl, 1 + AHEAD)
                    act_rsqrt(act, "pre3")
                    act_rsqrt_tm(act, "tm3")
                if i <= 4:
                    q_square(i)
                if i == 5:
                    act.wait_ge(r_tm_done.sem, r_tm_done.upto(LAYERS, 1))
                    use = result(ou, 5)
                    act.wait_ge(block_done, bl.n(5) + (RING + 1))
                    for t in range(TT):
                        last = nc.scalar.activation(a_v[:, t, :], use.mem[:, tok(t)], ACT.Copy, scale=r_tm[:, t:t + 1])
                    last.then_inc(use.drained, 1)
                if 1 <= i <= 5:
                    q_rsqrt(i - 1)
                if 2 <= i < 15:
                    j = i - 2
                    _, e, _ = rope_tile(j)
                    if j < 5:
                        act.wait_ge(q_n.sem, j + 1)
                    else:
                        act.wait_ge(drained[ou.bank(e)], ou.uses(e) + 2)
                    if j >= Q_S:
                        act.wait_ge(rope_y.sem, j - Q_S + 1)
                    for q in range(4):
                        to, of = 32 * q, 32 * (q ^ 1)
                        act.dma_start(q_s[to:to + 32, j % Q_S, :], q_in[of:of + 32, j % Q_IN, :]).then_inc(rope_moved[j % Q_S], 16)
                if 6 <= i < 11:
                    of, _, st = dense_tile(i - 6)
                    act.wait_ge(rope_y.sem, i - 5)
                    for h in range(2):
                        rows = head_rows(h)
                        nc.scalar.activation(st[h][rows], of[rows], ACT.Copy).then_inc(qk_hi.sem, 1)
            values(bl, 14, ou, 14, d_v)
            for u in range(65):
                if 2 <= u < 18 and u % 2 == 0:
                    of, _, st = dilated_part(u // 2 - 1)
                    act.wait_ge(rope_y.sem, 13)
                    nc.scalar.activation(st, of, ACT.Copy).then_inc(qk_hi.sem, 1)
                if u == 0:
                    act.wait_ge(rope_y.sem, 13)
                if u < 64:
                    e = N_QKV + u
                    act.wait_ge(maxed.sem, maxed.upto(0, u + 1))
                    if u >= 3:
                        old = side(f"pt{u - 3}")
                        act.wait_ge(old.filled, old.n + 1)
                    if u >= 4:
                        act.wait_ge(inv_done.sem, inv_done.upto(0, u - 3))
                    b = ou.bank(e)
                    nc.scalar.activation(prob[:, u % 3, :], ps[b][:, :], ACT.Exp, bias=row_max[:, u % 4:u % 4 + 1],
                                         accum_out=row_sum[:, u % 4:u % 4 + 1]).then_inc(drained[b], 1)
                if u >= 33:
                    v = u - 1
                    use = side(f"pt{v}")
                    act.wait_ge(use.filled, use.n + 1)
                    old = side(f"o{v - 2}")
                    act.wait_ge(old.filled, old.n + 1)
                    nc.scalar.activation(prob_t[:, v % 2, :], use.mem[:, :], ACT.Copy).then_inc(use.drained, 1)
            for k in range(KD):
                act.wait_ge(turned.sem, turned.upto(0, k + 1))
                nc.scalar.activation(u_hi[:, k, :], ps[ou.bank(N_QKV + 64 + k)][:, :], ACT.Copy).then_inc(hd_hi.sem, 1)
            for m in range(KD):
                act_split(act, bl, N_QKV + m + AHEAD)
                act_out(act, 5, m, bl, N_QKV + m, ou, N_QKV + 64 + KD + m)
            act_rsqrt(act, "post3")
            act_pre(act, 6, par2[:, H_F2PRE:H_F2PRE + KD])
            act_ffn(act, 6, 3, bl.on(N_QKV + KD), ou.on(N_QKV + 64 + 2 * KD), "pre4", "post4", half=True)

        @block.vector
        def _(dve):
            def exponents(u, li):
                lev, t = UNITS[u]
                cl, cr = halves(g_cum[:, t, :], lev)
                mid = middles(g_cum[:, t, :], lev)
                el, er = halves(lev_e[:, u % 2, :], lev)
                if t == 0:
                    dve.wait_ge(cum_done.sem, cum_done.upto(li, 2))
                if u >= 4:
                    dve.wait_ge(lev_qk.sem, lev_qk.upto(li, u - 3))
                nc.vector.tensor_tensor(er, cr, mid, ALU.subtract)
                nc.vector.tensor_tensor(el, mid, cl, ALU.subtract).then_inc(lev_d.sem, 1)

            def decayed(u, li):
                lev, t = UNITS[u]
                el, er = halves(lev_e[:, u % 2, :], lev)
                dve.wait_ge(lev_x.sem, lev_x.upto(li, u - 1))
                if u >= 4:
                    for key in level_keys(u - 2):
                        old = side(key, li)
                        dve.wait_ge(old.filled, old.n + 1)
                for h in range(2):
                    to = by_head(lev_q[:, u % 2, :])[head_rows(h), h, :].rearrange("p (n b) -> p n b", b=lev // 2)
                    nc.vector.tensor_tensor(to, halves(g_q[:, t, :], lev)[1][head_rows(h)], er[head_rows(h)], ALU.mult)
                nc.vector.tensor_tensor(halves(lev_k[:, u % 2, :], lev)[0], halves(g_k[:, t, :], lev)[0], el, ALU.mult).then_inc(lev_qk.sem, 1)

            def select(u, li):
                lev, t = UNITS[u]
                if lev == 1:
                    for h, key in enumerate(level_keys(u)):
                        use = side(key, li)
                        dve.wait_ge(use.filled, use.n + 1)
                        tiles = [ap.rearrange("p (a n) -> p a n", a=TT) for ap in (s_diag[:, 2 * t + h, :], use.mem[:, :])]
                        diagonal = ident_c.rearrange("p (o n) -> p o n", o=1).to_broadcast([P, TT, P])
                        nc.vector.tensor_tensor(tiles[0], tiles[1], diagonal, ALU.mult).then_inc(use.drained, 1)
                elif lev in MASKED:
                    use = side(f"gla{u}0", li)
                    dve.wait_ge(use.filled, use.n + 1)
                    n, b = P // lev, lev // 2
                    mask = gla_masks[:, MASKED.index(lev), :].rearrange("p (o n b) -> p o n b", o=1, b=b).to_broadcast([P, TT, n, b])
                    nc.vector.memset(wait_cell[:, u:u + 1], 0.0)
                    for h in range(2):
                        to = s_diag[:, 2 * t + h, :].rearrange("p (a n b) -> p a n b", a=TT, b=lev)[:, :, :, b:]
                        of = by_head(use.mem)[:, h, :].rearrange("p (a n b) -> p a n b", a=TT, b=b)
                        copy = nc.vector.copy_predicated(to, mask.bitcast(U32), of)
                    copy.then_inc(use.drained, 1)

            def y_low(n, li):
                dve.wait_ge(y_hi.sem, y_hi.upto(li, n + 1))
                hi, lo, of = ((ya_hi, ya_lo, c_a[:, :]), (yc_hi, yc_lo, y_c[:, n % 4, :]), (yb_hi, yb_lo, y_b[:, n % 4, :]))[n // 4]
                nc.vector.tensor_tensor(lo[:, n % 4, :], of, hi[:, n % 4, :].bitcast(F32), ALU.subtract).then_inc(y_lo.sem, 1)

            def conv(i, bl, ou, li):
                c, part = i // 3, i % 3
                use = result(ou, CV + i)
                dve.wait_ge(block_done, bl.n(CV + i) + (RING + 1))
                if part == 0:
                    nc.vector.tensor_tensor(c_t[:, :], use.mem[:, :], r[:, :], ALU.mult).then_inc(use.drained, 1)
                    dve.wait_ge(drained[ou.bank(CV + i)], ou.uses(CV + i) + 2)
                    nc.vector.tensor_tensor(c_t[:, :], c_t[:, :], r[:, :], ALU.mult).then_inc(conv_t.sem, 1)
                elif part == 1:
                    dve.wait_ge(conv_t.sem, conv_t.upto(li, c + 1))
                    nc.vector.tensor_tensor(c_z[:, 2:], use.mem[:, :], c_t[:, :], ALU.mult).then_inc(use.drained, 1)
                    dve.wait_ge(drained[ou.bank(CV + i)], ou.uses(CV + i) + 2)
                    if c == 0:
                        dve.wait_ge(zeroed.sem, zeroed.upto(li, 4))
                    for w in range(3):
                        gain = par[:, P_CONV + 4 * w + c:P_CONV + 4 * w + c + 1]
                        if w == 0:
                            nc.vector.tensor_scalar(c_a[:, :], c_z[:, 0:T], gain, None, ALU.mult).then_inc(conv_a.sem, 1)
                        else:
                            dve.wait_ge(conv_a.sem, conv_a.upto(li, 3 * c + w))
                            nc.vector.scalar_tensor_tensor(c_a[:, :], c_z[:, w:w + T], gain, c_a[:, :], ALU.mult, ALU.add).then_inc(conv_a.sem, 1)
                else:
                    nc.vector.tensor_tensor(c_b[:, :], use.mem[:, :], r[:, :], ALU.mult).then_inc(use.drained, 1)
                    dve.wait_ge(drained[ou.bank(CV + i)], ou.uses(CV + i) + 2)
                    dve.wait_ge(conv_a.sem, conv_a.upto(li, 3 * c + 3))
                    nc.vector.tensor_tensor(c_a[:, :], c_a[:, :], c_b[:, :], ALU.mult).then_inc(conv_y.sem, 1)

            def rotated(i, li):
                dve.wait_ge(rot_moved[i % 2], li * 128 + (i // 2 * 32 + 32))
                nc.vector.tensor_tensor(rot_s[:, i % 2, :], rot_s[:, i % 2, :], ret_sin[:, :], ALU.mult).then_inc(rot_z.sem, 1)

            def head_norm(n, li):
                y = (y_c if n < 4 else y_b)[:, n % 4, :]
                gain = (P_GLAGN if n < 4 else P_RETGN) + n % 4
                dve.wait_ge(hn_rr.sem, hn_rr.upto(li, n + 1))
                nc.vector.scalar_tensor_tensor(y, y, par[:, gain:gain + 1], hn_r[:, n % 2, :], ALU.mult, ALU.mult).then_inc(hn_y.sem, 1)

            def gate_in(g, bl, ou, li):
                use = result(ou, GR + g)
                dve.wait_ge(block_done, bl.n(GR + g) + (RING + 1))
                if g >= 2:
                    dve.wait_ge(y_gated.sem, y_gated.upto(li, g - 1))
                nc.vector.tensor_tensor(tgate[g % 2][:, :], use.mem[:, :], r[:, :], ALU.mult).then_inc(use.drained, 1)

            def gated(g, li):
                y = (y_c if g < 4 else y_b)[:, g % 4, :]
                dve.wait_ge(hn_y.sem, hn_y.upto(li, g + 1))
                dve.wait_ge(silu_g.sem, silu_g.upto(li, g + 1))
                nc.vector.tensor_tensor(y, y, tgate[g % 2][:, :], ALU.mult).then_inc(y_gated.sem, 1)

            def ret_decay(h, li):
                s, mask = s_ret[:, h % 2, :], ret_mask[:, h, :]
                if h == 0:
                    dve.wait_ge(masks_in, li * 16 + 16)
                if h >= 2:
                    old = side(f"out{2 + h}", li)
                    dve.wait_ge(old.filled, old.n + 1)
                use = side(f"s{h}0", li)
                dve.wait_ge(use.filled, use.n + 1)
                nc.vector.tensor_tensor(s[:, 0:512], use.mem[:, :], mask, ALU.mult).then_inc(use.drained, 1)
                use = side(f"s{h}1", li)
                dve.wait_ge(use.filled, use.n + 1)
                nc.vector.tensor_tensor(s[:, 512:896], use.mem[:, 0:384], mask[:, 0:384], ALU.mult)
                nc.vector.tensor_tensor(s[:, 1152:1280], use.mem[:, 384:512], mask[:, 0:128], ALU.mult).then_inc(use.drained, 1)
                use = side(f"s{h}2", li)
                dve.wait_ge(use.filled, use.n + 1)
                nc.vector.tensor_tensor(s[:, 896:1152], use.mem[:, 0:256], mask[:, 0:256], ALU.mult).then_inc(use.drained, 1)

            def layer(li):
                bl, ou, s = Blocks(li * (N_LAYER // 4)), layer_outs(li), li * 2

                def split(i):
                    dve_split(dve, bl, i + AHEAD)
                nc.vector.tensor_copy(flat(par), par_all[:, one(li), :]).then_inc(par_done.sem, 1)
                nc.vector.tensor_copy(flat(wa2), wa2_all[:, one(li), :]).then_inc(par_done.sem, 1)
                dve.wait_ge(par_done.sem, par_done.upto(li, 2))
                dve.wait_ge(ga_split.sem, ga_split.upto(li, 1))
                nc.vector.tensor_tensor(ga_w[:, :, RANK:2 * RANK], par[:, P_WGA:].rearrange("p (k n) -> p k n", k=KD),
                                        ga_w[:, :, 0:RANK].bitcast(F32), ALU.subtract).then_inc(ga_split.sem, 1)
                for i in range(4):
                    if i != 1:
                        split(i)
                    if i == 0:
                        split(1)
                        dve.wait_ge(r_done.sem, r_done.upto(s, 1))
                    use = result(ou, i)
                    dve.wait_ge(block_done, bl.n(i) + (RING + 1))
                    if i < 2:
                        nc.vector.scalar_tensor_tensor(g_q[:, i, :], use.mem[:, :], HD ** -0.5, r[:, :], ALU.mult, ALU.mult).then_inc(use.drained, 1)
                    else:
                        nc.vector.tensor_tensor(g_k[:, i - 2, :], use.mem[:, :], r[:, :], ALU.mult).then_inc(use.drained, 1)
                split(4)
                use = side("ga", li)
                dve.wait_ge(use.filled, use.n + 1)
                nc.vector.tensor_tensor(ga_t[:, :], use.mem[0:2 * RANK, :], r[0:2 * RANK, :], ALU.mult).then_inc(use.drained, 1)
                for i in range(5, 8):
                    split(i)
                for t in range(2):
                    use = side(f"z{t}", li)
                    dve.wait_ge(use.filled, use.n + 1)
                    nc.vector.tensor_scalar(z_b[:, t, :], use.mem[:, :], par[:, P_BA + t:P_BA + t + 1], None, ALU.add).then_inc(use.drained, 1)
                for t in range(2):
                    src = side(f"z{t}", li)
                    dve.wait_ge(src.drained, src.n + 2)
                    nc.vector.scalar_tensor_tensor(z_a[t][:, :], z_b[:, t, :], -1.0, z_b[:, t, :], ALU.mult, ALU.min).then_inc(z_abs.sem, 1)
                select(0, li)
                select(1, li)
                for t in range(2):
                    dve.wait_ge(z_ln.sem, z_ln.upto(li, t + 1))
                    nc.vector.scalar_tensor_tensor(z_b[:, t, :], z_b[:, t, :], 0.0, z_a[t][:, :], ALU.min, ALU.subtract).then_inc(z_log.sem, 1)
                for t in range(2):
                    dve.wait_ge(z_log.sem, z_log.upto(li, t + 1))
                    nc.vector.tensor_tensor_scan(g_cum[:, t, :], ones_c[:, 0:1].to_broadcast([P, T]), z_b[:, t, :], 0.0,
                                                 ALU.mult, ALU.add).then_inc(cum_done.sem, 1)
                dve.wait_ge(zeroed.sem, zeroed.upto(li, 4))
                for i in range(12):
                    for u in conv_units(i):
                        exponents(u, li)
                    split(CV + i)
                    if i % 3 == 0 and i > 0:
                        y_low(i // 3 - 1, li)
                    conv(i, bl, ou, li)
                    for u in conv_units(i):
                        decayed(u, li)
                    for u in conv_units(i - 1):
                        select(u, li)
                for i in range(8):
                    split(RQ + i)
                    if i == 0:
                        y_low(3, li)
                    if i >= 2:
                        dve.wait_ge(rot_c.sem, rot_c.upto(li, i - 1))
                    use = result(ou, RQ + i)
                    dve.wait_ge(block_done, bl.n(RQ + i) + (RING + 1))
                    if i < 4:
                        nc.vector.scalar_tensor_tensor(rot_in[:, i % 2, :], use.mem[:, :], P ** -0.5, r[:, :], ALU.mult, ALU.mult).then_inc(use.drained, 1)
                    else:
                        nc.vector.tensor_tensor(rot_in[:, i % 2, :], use.mem[:, :], r[:, :], ALU.mult).then_inc(use.drained, 1)
                    if i >= 1:
                        rotated(i - 1, li)
                    if 3 <= i <= 6:
                        head_norm(i - 3, li)
                for i in range(4):
                    split(RV + i)
                    if i == 0:
                        pass
                rotated(7, li)
                for t in range(TT):
                    dve.wait_ge(drained[ou.bank(RV + t)], ou.uses(RV + t) + 2)
                    nc.vector.tensor_reduce(v_sum[:, t, :], r_v[:, t, :].rearrange("p (h n) -> p h n", h=HEADS),
                                            AX.X, ALU.add).then_inc(rv_sum.sem, 1)
                for t in range(TT):
                    dve.wait_ge(rv_sum.sem, rv_sum.upto(li, t + 1))
                    v = r_v[:, t, :].rearrange("p (h n) -> p h n", h=HEADS)
                    mean = v_sum[:, t, :].rearrange("p (h o) -> p h o", o=1).to_broadcast([P, HEADS, P])
                    nc.vector.scalar_tensor_tensor(v, mean, -1.0 / P, v, ALU.mult, ALU.add).then_inc(rv_cent.sem, 1)
                for h in range(HEADS):
                    split(GR + h)
                    gate_in(h, bl, ou, li)
                    ret_decay(h, li)
                    gated(h, li)
                    if h == 3:
                        head_norm(4, li)
                split(RG)
                gate_in(4, bl, ou, li)
                head_norm(5, li)
                gated(4, li)
                split(RG + 1)
                gate_in(5, bl, ou, li)
                head_norm(6, li)
                gated(5, li)
                for n in range(4, 9):
                    y_low(n, li)
                split(RG + 2)
                gate_in(6, bl, ou, li)
                head_norm(7, li)
                gated(6, li)
                y_low(9, li)
                split(RG + 3)
                gate_in(7, bl, ou, li)
                gated(7, li)
                y_low(10, li)
                y_low(11, li)
                with dve.Fori(0, GATE_TURNS) as j:
                    b, o = turn(bl.on(N_HEAD), ou.on(N_HEAD), j, N_GATE, N_GATE)
                    for i in range(N_GATE // 2):
                        m, branch = i // 3, i % 3
                        dve_split(dve, b, 2 * i + AHEAD)
                        use = result(o, 2 * i)
                        dve.wait_ge(block_done, b.n(2 * i) + (RING + 1))
                        nc.vector.tensor_tensor(gt[i % 2][:, :], use.mem[:, :], r[:, :], ALU.mult).then_inc(use.drained, 1)
                        dve_split(dve, b, 2 * i + 1 + AHEAD)
                        use = result(o, 2 * i + 1)
                        dve.wait_ge(block_done, b.n(2 * i + 1) + (RING + 1))
                        dve.wait_ge(sig.sem, sig.upto(li, j * 6 + (i + 1)))
                        to = mac[m] if branch == 0 else br
                        nc.vector.tensor_tensor(to[:, :], use.mem[:, :], gt[i % 2][:, :], ALU.mult).then_inc(use.drained, 1)
                        if branch > 0:
                            dve.wait_ge(drained[o.bank(2 * i + 1)], o.uses(2 * i + 1) + 2)
                            if branch == 2:
                                dve.wait_ge(mac_add.sem, mac_add.upto(li, j * 4 + (2 * m + 1)))
                            nc.vector.tensor_tensor(mac[m][:, :], mac[m][:, :], br[:, :], ALU.add).then_inc(mac_add.sem, 1)
                        if branch == 2:
                            dve.wait_ge(mg_hi_ev.sem, mg_hi_ev.upto(li, j * 2 + (m + 1)))
                            nc.vector.tensor_tensor(mg_lo[:, one(j * 2 + m), :], flat(mac[m]),
                                                    mg_hi[:, one(j * 2 + m), :].bitcast(F32), ALU.subtract).then_inc(mg_lo_ev.sem, 1)
                b, o = bl.on(N_HEAD + N_GATE * GATE_TURNS), ou.on(N_HEAD + N_GATE * GATE_TURNS)
                for m in range(KD):
                    dve_split(dve, b, m + AHEAD)
                    dve_out(dve, s, m, o, m, par[:, G_MIX_POST:G_MIX_POST + KD], mix_out)
                dve_between(dve, s, o, KD - 1, mix_out, par[:, G_FFN_PRE:G_FFN_PRE + KD])
                dve_ffn(dve, s + 1, li, b.on(KD), o.on(KD), par[:, G_FFN_POST:G_FFN_POST + KD], par[:, G_NEXT:G_NEXT + KD])
                dve.wait_ge(u_lo_ev.sem, u_lo_ev.upto(s + 2, KD))
                nc.vector.memset(wait_cell[:, 0:1], 0.0)

            dve.wait_ge(positions_in, 32)
            steps = [0]

            def step(ins):
                ins.then_inc(ang_step, 1)
                steps[0] += 1
                dve.wait_ge(ang_step, steps[0])
            magic = 1.5 * 2 ** 23
            two_pi = [201 / 32]
            two_pi.append(float(np.float32(round((2 * math.pi - two_pi[0]) * 2 ** 20) / 2 ** 20)))
            two_pi.append(2 * math.pi - two_pi[0] - two_pi[1])
            step(nc.vector.tensor_copy(ang[0][:, :], pos_i[:, :]))
            step(nc.vector.tensor_scalar(ang[0][:, :], ang[0][:, :], inv_freq[:, 0:1], None, ALU.mult))
            def within_turn(i, shift):
                to = ang[2 + i]
                step(nc.vector.tensor_scalar(ang[1][:, :], ang[0][:, :], 1 / (2 * math.pi), shift, ALU.mult, ALU.add))
                step(nc.vector.tensor_scalar(ang[1][:, :], ang[1][:, :], magic, magic, ALU.add, ALU.subtract))
                for n, part in enumerate(two_pi):
                    of = ang[0] if n == 0 else to
                    step(nc.vector.scalar_tensor_tensor(to[:, :], ang[1][:, :], -part, of[:, :], ALU.mult, ALU.add))
                step(nc.vector.tensor_scalar(to[:, :], to[:, :], shift * 2 * math.pi, 3.1415925, ALU.add, ALU.min))
                nc.vector.tensor_scalar(to[:, :], to[:, :], -3.1415925, None, ALU.max).then_inc(trig_done, 1)
            within_turn(0, 0.0)
            first = par2[:, H_FIRST:H_FIRST + KD]
            dve.wait_ge(gains_in, 16)
            for k in range(KD // 2):
                dve_low(dve, 0, first, k)
            dve_split(dve, Blocks(0), 0)
            dve_split(dve, Blocks(0), 1)
            for k in range(KD // 2, KD):
                dve_low(dve, 0, first, k)
            dve_split(dve, Blocks(0), 2)
            within_turn(1, 0.25)
            dve_squares(dve, 0)
            dve.wait_ge(consts_in, CONSTS)
            dve.wait_ge(trig_tab, 2)
            with dve.Fori(0, LAYERS) as li:
                layer(li)

            bl, ou = Blocks(LAYERS * (N_LAYER // 4)), Outs(LAYERS * (OUT_LAYER // 4))
            dve_ffn(dve, 4, 2, bl, ou, par2[:, H_F1POST:H_F1POST + KD], par2[:, H_MPRE:H_MPRE + KD])
            bl, ou = bl.on(N_FFN), ou.on(OUT_FFN)

            def q_norm(i):
                gain = H_QN if i < 4 else H_KN
                dve.wait_ge(q_rr.sem, q_rr.upto(0, i + 1))
                nc.vector.scalar_tensor_tensor(q_in[:, i % Q_IN, :], q_in[:, i % Q_IN, :], par2[:, gain:gain + 1], q_r[:, :],
                                               ALU.mult, ALU.mult).then_inc(q_n.sem, 1)

            def roped(i):
                _, _, tab = rope_tile(i)
                dve.wait_ge(rope_moved[i % Q_S], i // Q_S * 64 + 64)
                if i == 0:
                    dve.wait_ge(tables_in, 16)
                nc.vector.tensor_tensor(q_s[:, i % Q_S, :], q_s[:, i % Q_S, :], rope_tab[:, tab + 1, :], ALU.mult).then_inc(rope_z.sem, 1)

            for i in range(18):
                if i != 1:
                    dve_split(dve, bl, i + AHEAD)
                if i == 0:
                    dve_split(dve, bl, 1 + AHEAD)
                    dve.wait_ge(r_done.sem, r_done.upto(5, 1))
                tile = i if i < 5 else i - 1
                if i != 5 and i < 14:
                    use = result(ou, i)
                    dve.wait_ge(block_done, bl.n(i) + (RING + 1))
                    if tile >= Q_IN:
                        dve.wait_ge(rope_c.sem, rope_c.upto(0, tile - Q_IN + 1))
                    to = q_in[:, tile % Q_IN, :]
                    if 6 <= i < 10:
                        nc.vector.scalar_tensor_tensor(to, use.mem[:, :], HD ** -0.5, r[:, :], ALU.mult, ALU.mult).then_inc(use.drained, 1)
                    else:
                        nc.vector.tensor_tensor(to, use.mem[:, :], r[:, :], ALU.mult).then_inc(use.drained, 1)
                if 1 <= i <= 5:
                    q_norm(i - 1)
                if 4 <= i < 17:
                    roped(i - 4)
                if 7 <= i < 12:
                    j = i - 7
                    of, lo, st = dense_tile(j)
                    dve.wait_ge(qk_hi.sem, 2 * j + 2)
                    for h in range(2):
                        rows = head_rows(h)
                        nc.vector.tensor_tensor(lo[rows], of[rows], st[h][rows].bitcast(F32), ALU.subtract).then_inc(dense_lo.sem, 1)

            def row_maximum(u):
                dense, t, h, it, _ = attention_unit(u)
                scores = ps[ou.bank(N_QKV + u)]
                dve.wait_ge(scored.sem, scored.upto(0, u + 1))
                if not dense:
                    nc.vector.tensor_tensor(scores[:, :], scores[:, :], bias[:, it, :], ALU.add).then_inc(biased.sem, 1)
                    dve.wait_ge(biased.sem, biased.upto(0, u - 31))
                nc.vector.tensor_reduce(row_max[:, u % 4:u % 4 + 1], scores[:, :], AX.X, ALU.max, negate=True).then_inc(maxed.sem, 1)

            for u in range(67):
                if u == 32:
                    dve.wait_ge(bias_in, 16)
                if u < 64:
                    row_maximum(u)
                v = u - 2
                if 0 <= v < 64:
                    dve.wait_ge(drained[ou.bank(N_QKV + v)], ou.uses(N_QKV + v) + 2)
                    nc.vector.reciprocal(row_inv[:, v % 4:v % 4 + 1], row_sum[:, v % 4:v % 4 + 1]).then_inc(inv_done.sem, 1)
                if 0 <= v < 32:
                    use = side(f"pt{v}")
                    dve.wait_ge(use.filled, use.n + 1)
                    if v >= 2:
                        old = side(f"o{v - 2}")
                        dve.wait_ge(old.filled, old.n + 1)
                    nc.vector.tensor_copy(prob_t[:, v % 2, :], use.mem[:, :]).then_inc(use.drained, 1)
                v = u - 3
                if v >= 0:
                    _, _, _, it, col = attention_unit(v)
                    use = side(f"o{v}")
                    dve.wait_ge(use.filled, use.n + 1)
                    dve.wait_ge(inv_done.sem, inv_done.upto(0, v + 1))
                    nc.vector.tensor_scalar(heads[:, it, col:col + HD], use.mem[:, 0:HD], row_inv[:, v % 4:v % 4 + 1], None,
                                            ALU.mult).then_inc(use.drained, 1)
            for k in range(KD):
                b = ou.bank(N_QKV + 64 + k)
                dve.wait_ge(hd_hi.sem, hd_hi.upto(0, k + 1))
                nc.vector.tensor_tensor(u_lo[:, k, :], ps[b][:, :], u_hi[:, k, :].bitcast(F32), ALU.subtract).then_inc(drained[b], 1)
            for m in range(KD):
                e = N_QKV + 64 + KD + m
                dve_split(dve, bl, N_QKV + m + AHEAD)
                dve_out(dve, 5, m, ou, e, par2[:, H_MPOST:H_MPOST + KD], mix_out)
            dve_between(dve, 5, ou, N_QKV + 64 + 2 * KD - 1, mix_out, par2[:, H_F2PRE:H_F2PRE + KD])
            dve_ffn(dve, 6, 3, bl.on(N_QKV + KD), ou.on(N_QKV + 64 + 2 * KD), par2[:, H_F2POST:H_F2POST + KD])


def tile_columns(w, c):
    k = w.shape[0] // P
    return w[:, c:c + P].reshape(k, P, P).transpose(1, 0, 2).reshape(P, k * P)


def value_columns(w, c):
    return w[:, c:c + T].reshape(KD, P, T).transpose(1, 0, 2).reshape(P, KD * T)


def ffn_blocks(gate, up, down):
    out = []
    for f in range(FT):
        out += [tile_columns(gate, f * P), tile_columns(up, f * P)]
    return out + [tile_columns(down, m * P) for m in range(KD)]


AXIAL = np.arange(HD).reshape(2, 2, HD // 4).transpose(1, 0, 2).reshape(HD)


def weight_stream(a):
    out = []
    for li in range(LAYERS):
        w = a["w_in"][li]
        out += [tile_columns(w, 3584 + i * P) for i in range(4)]
        out += [value_columns(w, 4096)]
        for c in range(4):
            out += [tile_columns(w, at + c * P) for at in (0, 1024, 512)]
        out += [tile_columns(w, 1536 + i * P) for i in range(8)]
        out += [value_columns(w, 2560)]
        out += [tile_columns(w, 4608 + i * P) for i in range(4)]
        out += [tile_columns(w, 3072 + i * P) for i in range(4)]
        for m in range(KD):
            for at, name in ((5136, "w_branch_a"), (7184, "w_branch_c"), (6160, "w_branch_b")):
                out += [tile_columns(w, at + m * P), tile_columns(a[name][li], m * P)]
        out += [tile_columns(a["w_out"][li], m * P) for m in range(KD)]
        out += ffn_blocks(a["w_ffn_gate"][li], a["w_ffn_up"][li], a["w_ffn_down"][li])
    out += ffn_blocks(a["ffn1_w_gate_2"][0], a["ffn1_w_up_2"][0], a["ffn1_w_down_2"][0])
    w = a["w_qkv_2"][0]
    for t in range(4):
        out += [tile_columns(np.concatenate([w[:, h * HD + AXIAL] for h in (t, t + 4)], axis=1), 0)]
    out += [tile_columns(w[:, 512 + np.concatenate([AXIAL, HD + AXIAL])], 0)]
    out += [tile_columns(w, 640 + i * P) for i in range(9)]
    out += [value_columns(w, 1792)]
    out += [tile_columns(a["w_out_2"][0], m * P) for m in range(KD)]
    out += ffn_blocks(a["ffn2_w_gate_2"][0], a["ffn2_w_up_2"][0], a["ffn2_w_down_2"][0])
    return np.concatenate(out, axis=1)


def per_partition(v):
    return v.reshape(-1, P).T


def layer_parameters(a):
    out = []
    for li in range(LAYERS):
        cols = [per_partition(a["norm_mix_pre"][li + 1] if li + 1 < LAYERS else a["ffn1_pre_g_2"][0])]
        cols += [per_partition(a[n][li]) for n in ("norm_mix_post", "norm_ffn_pre", "norm_ffn_post")]
        cols += [per_partition(a["conv_w"][li][w]) for w in range(3)]
        cols += [per_partition(a[n][li]) for n in ("ret_gn_w", "gla_gn_w", "gla_b_a")]
        cols += [a["w_in"][li][:, 5120:5120 + RANK].reshape(KD, P, RANK).transpose(1, 0, 2).reshape(P, KD * RANK)]
        out.append(np.concatenate(cols, axis=1))
    return np.stack(out, axis=1)


def second_gains(a):
    cols = [per_partition(a["norm_mix_pre"][0])]
    cols += [per_partition(a[n + "_2"][0]) for n in ("ffn1_post_g", "mix_pre_g", "mix_post_g", "ffn2_pre_g", "ffn2_post_g")]
    cols += [np.concatenate([a[n + "_2"][0][AXIAL]] * 2).reshape(P, 1) for n in ("q_norm_g", "k_norm_g")]
    return np.concatenate(cols, axis=1)


def constants():
    f = np.float32
    i, j = np.arange(P)[None, :], np.arange(P)[:, None]
    squares = [np.ones((P, P), f), np.eye(P, dtype=f), (i // HD == j // HD).astype(f)]
    masks = []
    for lev in MASKED:
        mask = (i // lev == j // lev) & (j % lev < lev // 2)
        masks.append(mask[:, np.arange(P) % lev >= lev // 2].astype(f))
    c = np.arange(T)[None, :] - np.arange(P)[:, None]
    log_g = np.log(1.0 - 2.0 ** (-5.0 - np.arange(HEADS)))
    decay = [np.where(c >= 0, np.exp(lg * np.maximum(c, 0)), 0.0).astype(f) for lg in log_g]
    inv = np.power(f(10000.0), -np.arange(HD, dtype=f) / f(HD)).astype(f)
    t = np.arange(T)

    def angles(pos, dim):
        freqs = np.power(f(10000.0), -np.arange(0, dim, 2, dtype=f) / f(dim)).astype(f)
        return pos.astype(f)[:, None] * freqs[None, :]
    row, col, seq = angles(t // 64, HD // 2), angles(t % 64, HD // 2), angles(t, HD)
    axial = np.concatenate([row, col] * 4, axis=1).T
    along = np.concatenate([seq, seq] * 2, axis=1).T
    sign = np.where(np.arange(P) % HD < HD // 2, -1, 1).astype(f)[:, None]
    tables = [g.astype(f) for x in (axial, along) for g in (np.cos(x), sign * np.sin(x))]
    d = t[None, :] - t[:, None]
    times = sum(((d % dil == 0) & (np.abs(d // dil) <= win // 2 // dil)).astype(int) for win, dil in ((128, 1), (512, 4), (2048, 16)))
    bias = np.where(times > 0, np.log(np.maximum(times, 1)), NEG).astype(f)
    return {
        "sq_consts": np.stack(squares, axis=1), "gla_masks": np.stack(masks, axis=1), "ret_mask": np.stack(decay, axis=1),
        "inv_freq": np.concatenate([-inv, inv]).reshape(P, 1), "rope_tab": np.stack(tables, axis=1),
        "bias": bias.reshape(TT, P, T).transpose(1, 0, 2),
    }


def kernel(**inputs):
    import concourse.bacc as bacc
    from concourse.bass_utils import run_bass_kernel_spmd

    a = {k: np.asarray(v) for k, v in inputs.items()}
    arrays = {
        "x": a["x"][0].T.reshape(KD, P, T).transpose(1, 0, 2),
        "positions": a["positions"].reshape(1, T),
        "weights": weight_stream(a),
        "par_all": layer_parameters(a),
        "par2": second_gains(a),
        "wa2": np.concatenate([a["gla_w_a2"].transpose(1, 0, 2)] * 2),
    }
    arrays.update(constants())
    arrays = {k: np.ascontiguousarray(v) for k, v in arrays.items()}
    nc = bacc.Bacc("TRN2", target_bir_lowering=False, num_devices=1)
    dram = {k: nc.dram_tensor(f"in_{k}", v.shape, mybir.dt.from_np(v.dtype), kind="ExternalInput").ap() for k, v in arrays.items()}
    dram["out"] = nc.dram_tensor("out", (P, KD, T), F32, kind="ExternalOutput").ap()
    build(nc, dram)
    result = run_bass_kernel_spmd(nc, [{f"in_{k}": v for k, v in arrays.items()}], core_ids=[0])
    y = result.results[0]["out"]
    return y.transpose(2, 1, 0).reshape(1, T, D)
```
